# Optimizing a Trainium2 kernel written in Bass

```python
import jax, jax.numpy as jnp
from jax import lax
import numpy as np

D_MODEL = 1024
BATCH = 1
SEQ = 256
DEPTH = 1

HEAD_DIM = 64
ATTN_HEADS = 8
ATTN_WIDTH = ATTN_HEADS * HEAD_DIM
RWKV_HEADS = 8
RWKV_WIDTH = RWKV_HEADS * HEAD_DIM
MIX_WIDTH = ATTN_WIDTH + RWKV_WIDTH
DECAY_RANK = 64
ICLR_RANK = 64
MOBA_BLOCK = 256
MOBA_TOPK = 3
Q_CHUNK = 32
ROPE_THETA = 10000.0
RMS_EPS = 1e-6
GN_EPS = 64e-5
NORMALIZE_EPS_SQ = 1e-24

SHIFT_WIDTH = 3 * RWKV_WIDTH + DECAY_RANK + ICLR_RANK
IN_WIDTH = 4 * ATTN_WIDTH + SHIFT_WIDTH + RWKV_WIDTH
B_SHIFT_START = 4 * ATTN_WIDTH
B_GATE_START = B_SHIFT_START + SHIFT_WIDTH

kernel_name = 'hybrid_moba_rwkv7_parallel_heads'

def rms_norm(x, gain):
    xf = x.astype(jnp.float32)
    return xf * lax.rsqrt(jnp.mean(xf * xf, axis=-1, keepdims=True) + RMS_EPS) * gain.astype(jnp.float32)

def rotary(x):
    t, d = x.shape[2], x.shape[3]
    inv_freq = 1.0 / (ROPE_THETA ** (jnp.arange(0, d, 2, dtype=jnp.float32) / d))
    ang = jnp.arange(t, dtype=jnp.float32)[:, None] * inv_freq[None, :]
    cos, sin = jnp.cos(ang), jnp.sin(ang)
    x1, x2 = x[..., : d // 2], x[..., d // 2:]
    return jnp.concatenate([x1 * cos - x2 * sin, x2 * cos + x1 * sin], axis=-1)

def moba_attention(q, k, v):
    b, h, t, d = q.shape
    nb = -(-t // MOBA_BLOCK)
    t_pad = nb * MOBA_BLOCK
    pad = ((0, 0), (0, 0), (0, t_pad - t), (0, 0))
    q, k, v = jnp.pad(q, pad), jnp.pad(k, pad), jnp.pad(v, pad)
    kb = k.reshape(b, h, nb, MOBA_BLOCK, d)
    vb = v.reshape(b, h, nb, MOBA_BLOCK, d)
    k_mean = kb.mean(axis=3)
    n_sel = min(MOBA_TOPK, nb)
    scale = d ** -0.5
    b_idx = jnp.arange(b)[:, None, None, None]
    h_idx = jnp.arange(h)[None, :, None, None]
    block_ids = jnp.arange(nb)

    def query_chunk(i):
        start = i * Q_CHUNK
        cur = start // MOBA_BLOCK
        qc = lax.dynamic_slice_in_dim(q, start, Q_CHUNK, axis=2)
        gate = jnp.einsum('bhqd,bhnd->bhqn', qc, k_mean)
        gate = jnp.where(block_ids < cur, gate, -jnp.inf)
        _, sel = lax.top_k(gate, n_sel)
        sel_ok = jnp.arange(n_sel) < cur
        k_sel = kb[b_idx, h_idx, sel]
        v_sel = vb[b_idx, h_idx, sel]
        s_sel = jnp.einsum('bhqd,bhqjsd->bhqjs', qc, k_sel) * scale
        s_sel = jnp.where(sel_ok[:, None], s_sel, -jnp.inf)
        k_own = lax.dynamic_index_in_dim(kb, cur, axis=2, keepdims=False)
        v_own = lax.dynamic_index_in_dim(vb, cur, axis=2, keepdims=False)
        s_own = jnp.einsum('bhqd,bhsd->bhqs', qc, k_own) * scale
        q_pos = start + jnp.arange(Q_CHUNK)
        k_pos = cur * MOBA_BLOCK + jnp.arange(MOBA_BLOCK)
        s_own = jnp.where(k_pos[None, :] <= q_pos[:, None], s_own, -jnp.inf)
        scores = jnp.concatenate([s_sel.reshape(b, h, Q_CHUNK, n_sel * MOBA_BLOCK), s_own], axis=-1)
        probs = jax.nn.softmax(scores, axis=-1)
        p_sel = probs[..., : n_sel * MOBA_BLOCK].reshape(b, h, Q_CHUNK, n_sel, MOBA_BLOCK)
        p_own = probs[..., n_sel * MOBA_BLOCK:]
        return (jnp.einsum('bhqjs,bhqjsd->bhqd', p_sel, v_sel)
                + jnp.einsum('bhqs,bhsd->bhqd', p_own, v_own))

    out = lax.map(query_chunk, jnp.arange(t_pad // Q_CHUNK))
    out = jnp.moveaxis(out, 0, 2).reshape(b, h, t_pad, d)
    return out[:, :, :t]

def rwkv7_time_mix(p, shift_mu, decay_bias, decay_up, iclr_bias, iclr_up, k_k, k_a, r_k, gn_gain, gn_bias):
    f32 = jnp.float32
    p = p.astype(f32)
    b, t, _ = p.shape
    c = RWKV_WIDTH
    prev = jnp.pad(p[:, :-1], ((0, 0), (1, 0), (0, 0)))
    p = p + (prev - p) * shift_mu.astype(f32)
    r, k, v = p[..., :c], p[..., c:2 * c], p[..., 2 * c:3 * c]
    w_down = p[..., 3 * c:3 * c + DECAY_RANK]
    a_down = p[..., 3 * c + DECAY_RANK:]
    w_log = -jax.nn.softplus(-(decay_bias.astype(f32) + jnp.tanh(w_down) @ decay_up.astype(f32))) - 0.5
    decay = jnp.exp(-jnp.exp(w_log))
    a = jax.nn.sigmoid(iclr_bias.astype(f32) + a_down @ iclr_up.astype(f32))
    kk = k * k_k.astype(f32)
    k = k * (1.0 + (a - 1.0) * k_a.astype(f32))
    heads = lambda z: z.reshape(b, t, RWKV_HEADS, HEAD_DIM)
    r, k, v, decay, a, kk = (heads(z) for z in (r, k, v, decay, a, kk))
    kk = kk * lax.rsqrt(jnp.maximum(jnp.sum(kk * kk, axis=-1, keepdims=True), NORMALIZE_EPS_SQ))

    def step(state, inp):
        r_t, w_t, k_t, v_t, kk_t, a_t = inp
        sa = jnp.einsum('bhvk,bhk->bhv', state, -kk_t)
        state = (state * w_t[:, :, None, :]
                 + sa[..., None] * (kk_t * a_t)[:, :, None, :]
                 + v_t[..., None] * k_t[:, :, None, :])
        return state, jnp.einsum('bhvk,bhk->bhv', state, r_t)

    seq_first = lambda z: jnp.moveaxis(z, 1, 0)
    state0 = jnp.zeros((b, RWKV_HEADS, HEAD_DIM, HEAD_DIM), f32)
    _, y = lax.scan(step, state0, tuple(seq_first(z) for z in (r, decay, k, v, kk, a)))
    y = jnp.moveaxis(y, 0, 1)
    mu = jnp.mean(y, axis=-1, keepdims=True)
    var = jnp.mean(jnp.square(y - mu), axis=-1, keepdims=True)
    y = ((y - mu) * lax.rsqrt(var + GN_EPS)).reshape(b, t, c) * gn_gain.astype(f32) + gn_bias.astype(f32)
    bonus = jnp.sum(r * k * r_k.astype(f32), axis=-1, keepdims=True) * v
    return y + bonus.reshape(b, t, c)

def setup_inputs(seed: int = 0) -> dict:
    key = jax.random.key(seed)
    ks = jax.random.split(key, 16)
    f32 = jnp.float32
    nrm = lambda kk, shape, s: s * jax.random.normal(kk, shape, f32)
    L = DEPTH
    return {
        'x': jax.random.normal(ks[0], (BATCH, SEQ, D_MODEL), f32),
        'norm_gain': 1.0 + nrm(ks[1], (L, D_MODEL), 0.02),
        'w_in': nrm(ks[2], (L, D_MODEL, IN_WIDTH), D_MODEL ** -0.5),
        'shift_mu': jax.random.uniform(ks[3], (L, SHIFT_WIDTH), f32),
        'decay_bias': nrm(ks[4], (L, RWKV_WIDTH), 0.5) - 2.0,
        'decay_up': nrm(ks[5], (L, DECAY_RANK, RWKV_WIDTH), 0.5 * DECAY_RANK ** -0.5),
        'iclr_bias': nrm(ks[6], (L, RWKV_WIDTH), 0.5),
        'iclr_up': nrm(ks[7], (L, ICLR_RANK, RWKV_WIDTH), ICLR_RANK ** -0.5),
        'k_k': 0.85 + nrm(ks[8], (L, RWKV_WIDTH), 0.1),
        'k_a': 1.0 + nrm(ks[9], (L, RWKV_WIDTH), 0.1),
        'r_k': nrm(ks[10], (L, RWKV_HEADS, HEAD_DIM), 0.1),
        'gn_gain': 1.0 + nrm(ks[11], (L, RWKV_WIDTH), 0.02),
        'gn_bias': nrm(ks[12], (L, RWKV_WIDTH), 0.02),
        'w_out': nrm(ks[13], (L, MIX_WIDTH, D_MODEL), MIX_WIDTH ** -0.5),
        'final_gain': 1.0 + nrm(ks[14], (D_MODEL,), 0.02),
    }

def reference(x, norm_gain, w_in, shift_mu, decay_bias, decay_up, iclr_bias, iclr_up,
              k_k, k_a, r_k, gn_gain, gn_bias, w_out, final_gain):
    f32 = jnp.float32
    b, t, _ = x.shape
    h = x.astype(f32)
    to_heads = lambda z: z.reshape(b, t, ATTN_HEADS, HEAD_DIM).transpose(0, 2, 1, 3)
    for layer in range(DEPTH):
        u = rms_norm(h, norm_gain[layer])
        p = jnp.einsum('btd,dc->btc', u, w_in[layer].astype(f32))
        q = rotary(to_heads(p[..., 0:ATTN_WIDTH]))
        k = rotary(to_heads(p[..., ATTN_WIDTH:2 * ATTN_WIDTH]))
        v = to_heads(p[..., 2 * ATTN_WIDTH:3 * ATTN_WIDTH])
        y_a = moba_attention(q, k, v).transpose(0, 2, 1, 3).reshape(b, t, ATTN_WIDTH)
        y_a = y_a * jax.nn.silu(p[..., 3 * ATTN_WIDTH:4 * ATTN_WIDTH])
        y_b = rwkv7_time_mix(p[..., B_SHIFT_START:B_GATE_START], shift_mu[layer], decay_bias[layer],
                             decay_up[layer], iclr_bias[layer], iclr_up[layer], k_k[layer], k_a[layer],
                             r_k[layer], gn_gain[layer], gn_bias[layer])
        y_b = y_b * jax.nn.silu(p[..., B_GATE_START:])
        h = h + jnp.einsum('btc,cd->btd', jnp.concatenate([y_a, y_b], axis=-1), w_out[layer].astype(f32))
    return rms_norm(h, final_gain).astype(x.dtype)


_drawn_inputs = setup_inputs


def setup_inputs(seed=0):
    import zlib

    import numpy as np

    out = dict(_drawn_inputs(seed))
    spreads = {}
    factors = {'norm_gain': 3.088,
     'decay_up': 2.807,
     'k_k': 3.951,
     'gn_gain': 7.168,
     'gn_bias': 7.442,
     'final_gain': 2.882}
    for name, (base, spread) in spreads.items():
        noise = np.random.default_rng([zlib.crc32(name.encode()), seed]).standard_normal(out[name].shape)
        drawn = base * np.exp(spread * noise) if base else spread * noise
        out[name] = __import__('jax').numpy.asarray(drawn.astype(out[name].dtype))
    for name, factor in factors.items():
        out[name] = (out[name] * factor).astype(out[name].dtype)
    return out
```

```python
import concourse.bass as bass
from concourse import mybir
from contextlib import ExitStack
import numpy as np

D_MODEL, SEQ, HEAD, HEADS = 1024, 256, 64, 8
WIDTH = HEAD * HEADS
P = 128
PAIRS = WIDTH // P
KC = D_MODEL // P
TT = SEQ // P
C = 64
CHUNKS = SEQ // C
UNITS = CHUNKS * PAIRS
BASE = 16
DECAY = 0.5 * float(np.exp(-0.5))

CONST = {}
_at = 0
for _name, _n in (("ident", P), ("head_mean", P), ("head_sum", P), ("gram_mask", P), ("a_mask", C),
                  ("low16", C), ("low32", C), ("scan", SEQ), ("causal", 3 * P), ("cos", TT * HEAD),
                  ("sin", TT * HEAD), ("block_eye", BASE * BASE)):
    CONST[_name] = (_at, _at + _n)
    _at += _n
N_CONST = _at
PARAM = {}
_at = 0
for _name, _n in (("mu_r", PAIRS), ("mu_k", PAIRS), ("mu_v", PAIRS), ("mu_w", 1), ("decay_bias", PAIRS),
                  ("iclr_bias", PAIRS), ("k_k", PAIRS), ("k_a", PAIRS), ("r_k", PAIRS),
                  ("gn_gain", PAIRS), ("gn_bias", PAIRS), ("norm_gain", KC)):
    PARAM[_name] = (_at, _at + _n)
    _at += _n
N_PARAM = _at

BLOCKS = ["k", "r", "v", "aq", "ak", "av", "ga", "gb", "wo0", "wo1"]
SLOTS = 3

PROJ_BANKS, AUX_BANKS = (0, 1, 2), (3, 4, 5, 6, 7)


def job_order():
    pj, ax = "proj", "aux"
    jobs = [(("xT", j), ax) for j in range(4)]
    jobs += [(("k", 0), pj), (("k", 1), pj), (("wd", 0), pj), (("r", 0), pj)]
    jobs += [(("upw", 0), ax), (("upa", 0), ax), (("upw", 1), ax), (("upa", 1), ax)]
    jobs += [(("r", 1), pj), (("kn", 0), ax), (("kn", 1), ax), (("v", 0), pj), (("v", 1), pj)]
    jobs += [(("aq", 0), pj), (("aq", 1), pj), (("bonus", 0), ax), (("bonus", 1), ax)]
    jobs += [(("ak", 0), pj), (("A", 0), ax), (("A", 1), ax), (("ak", 1), pj)]
    jobs += [(("qT", 0), ax), (("qT", 1), ax), (("kT", 0), ax), (("kT", 1), ax)]
    jobs += [(("av", 0), pj), (("vT", 0), ax), (("bT", 0), ax), (("gram", 0, 0), ax), (("gram", 0, 1), ax)]
    jobs += [(("S", 0), ax), (("S", 1), ax), (("av", 1), pj)]
    jobs += [(("Y1", 0), ax), (("Y1", 1), ax), (("PT", 0), ax), (("S", 2), ax)]
    jobs += [(("T1", 0), ax), (("U1", 0), ax), (("T1", 1), ax), (("U1", 1), ax), (("PT", 1), ax), (("S", 3), ax)]
    jobs += [(("Y2", 0), ax), (("Y2", 1), ax), (("ga", 0), pj), (("U2", 0), ax), (("U2", 1), ax), (("ga", 1), pj), (("PV", 0), ax)]
    for c in range(CHUNKS):
        fill = [[(("PT", 2 * c + 2), ax), (("S", 2 * c + 4), ax)],
                [(("PT", 2 * c + 3), ax), (("PV", c + 1), ax), (("S", 2 * c + 5), ax)]] if c < 3 else [[], []]
        fill = [[j for j in f if not (j[0][0] == "S" and j[0][1] >= HEADS)] for f in fill]
        jobs += [(("R", c), ax)] + fill[0]
        if c < 2:
            jobs += [(("gb", c), pj)]
        jobs += [(("SA", c, 0), ax), (("SA", c, 1), ax)] + fill[1]
        if c + 1 < CHUNKS:
            jobs += [(("vT", c + 1), ax), (("bT", c + 1), ax), (("gram", c + 1, 0), ax), (("gram", c + 1, 1), ax)]
            jobs += [(("St", c), ax)]
        jobs += [(("Yc", c), ax), (("mean", c), ax), (("var", c), ax)]
    jobs += [(("out", t, n), pj if t == 0 else ax) for t in range(TT) for n in range(2)]
    return jobs


def place_jobs():
    turn, used, place = {"proj": 0, "aux": 0}, [0] * 8, {}
    for name, kind in job_order():
        banks = PROJ_BANKS if kind == "proj" else AUX_BANKS
        b = banks[turn[kind] % len(banks)]
        turn[kind] += 1
        place[name] = (b, used[b])
        used[b] += 1
    return place


def hybrid_layer(nc, x, w_blocks, w_wd, up, const, param, final_gain, a_scratch, t_scratch, out):
    f32 = mybir.dt.float32
    ALU = mybir.AluOpType
    ACT = mybir.ActivationFunctionType
    AX = mybir.AxisListType
    PLACE = place_jobs()
    ctx = ExitStack()
    with ctx:
        def sb(name, shape):
            return ctx.enter_context(nc.sbuf_tensor(name, shape, f32))

        def sem(name):
            return ctx.enter_context(nc.semaphore(name))

        banks = [ctx.enter_context(nc.psum_tensor(f"bank{b}", [P, 512], f32)) for b in range(8)]

        cst = sb("cst", [P, N_CONST])
        prm = sb("prm", [P, N_PARAM])
        drv = sb("drv", [P, 6, PAIRS])
        slots = [sb(f"w_slot{s}", [P, KC, 512]) for s in range(SLOTS)]
        w_wd_sb = sb("w_wd_sb", [P, KC, P])
        up_sb = sb("up_sb", [P, WIDTH])
        fgain = sb("fgain", [P, D_MODEL])
        xt = sb("xt", [P, TT, D_MODEL])
        uT = sb("uT", [P, KC, SEQ])
        stat = sb("stat", [P, 4 * TT])
        pad_a = sb("pad_a", [P, PAIRS, SEQ + 1])
        pad_b = sb("pad_b", [P, PAIRS, SEQ + 1])
        pad_w = sb("pad_w", [P, SEQ + 1])
        wd = sb("wd", [P, SEQ])
        dif = sb("dif", [P, PAIRS, SEQ])
        k1 = sb("k1", [P, PAIRS, SEQ])
        r1 = sb("r1", [P, PAIRS, SEQ])
        v1 = sb("v1", [P, PAIRS, C + SEQ])
        kk = sb("kk", [P, PAIRS, SEQ])
        rn = sb("rn", [P, PAIRS, SEQ])
        thw = sb("thw", [P, PAIRS, SEQ])
        cs = sb("cs", [P, PAIRS, SEQ])
        tha = sb("tha", [P, PAIRS, SEQ])
        kp = sb("kp", [P, PAIRS, SEQ])
        pinc = sb("pinc", [P, UNITS, C + 1])
        bk = sb("bk", [P, UNITS, 2, C])
        kr = sb("kr", [P, UNITS, 2, C])
        head_rk = sb("head_rk", [P, PAIRS, P])
        y_sb = sb("y_sb", [P, UNITS, C])
        blk = sb("blk", [P, 4, BASE * BASE])
        lr = sb("lr", [P, 2, HEADS, P])
        bkt = sb("bkt", [P, 2, HEADS, C])
        sav = sb("sav", [P, 2, HEADS, C])
        state = sb("state", [P, 2, PAIRS, C])
        r_neg = sb("r_neg", [P, PAIRS, C])
        yc = sb("yc", [P, 2, PAIRS, C])
        gn_r = sb("gn_r", [P, 2, PAIRS, C])
        ycat = sb("ycat", [P, 2 * PAIRS, SEQ])
        g_b = sb("g_b", [P, PAIRS, SEQ])
        qT = sb("qT", [P, PAIRS, SEQ])
        kT = sb("kT", [P, PAIRS, SEQ])
        amax = sb("amax", [P, HEADS, 3, TT])
        xn = y_sb[:, :, :].rearrange("p u c -> p (u c)")
        xn_tiles = [xn, bk[:, 0:8, :, :].rearrange("p u s c -> p (u s c)")]
        a_neg = kk[:, :, :].rearrange("p a (b c) -> p (a b) c", c=C)
        b16 = rn[:, :, :].rearrange("p a (b c) -> p (a b) c", c=C)
        b32 = thw[:, :, :].rearrange("p a (b c) -> p (a b) c", c=C)
        t_inv = cs[:, :, :].rearrange("p a (b c) -> p (a b) c", c=C)
        u_inv = tha[:, :, :].rearrange("p a (b c) -> p (a b) c", c=C)
        rot = r1[:, :, :].rearrange("p a b -> p (a b)").rearrange("p (t n) -> p t n", t=TT)
        v_att = kp[:, :, :].rearrange("p a b -> p (a b)").rearrange("p (t n) -> p t n", t=TT)
        rot_k = pad_b[:, :, :].rearrange("p a b -> p (a b)")[:, 0:TT * WIDTH].rearrange("p (t n) -> p t n", t=TT)
        g_a = ycat[:, 0:PAIRS, :]
        pad_a_flat = pad_a[:, :, :].rearrange("p a b -> p (a b)")
        rtmp = dif[:, :, :].rearrange("p a b -> p (a b)")
        bonus = k1
        pr = rtmp[:, 0:6 * P].rearrange("p (b n) -> p b n", b=2)
        prT = pad_a_flat[:, 0:6 * P].rearrange("p (b n) -> p b n", b=2)

        def cn(name):
            a, b = CONST[name]
            return cst[:, a:b]

        def pm(name, i=0):
            a, _ = PARAM[name]
            return prm[:, a + i:a + i + 1]

        def pm_all(name):
            a, b = PARAM[name]
            return prm[:, a:b]

        HALF_DB, HALF_IB, HALF_KA, ONE_KA, HALF_GAIN = range(5)

        s_const = sem("s_const")
        s_x = sem("s_x")
        s_w = [sem(f"s_w{n}") for n in range(len(BLOCKS))]
        s_wk = sem("s_wk")
        s_wwd = sem("s_wwd")
        s_up = sem("s_up")
        s_fg = sem("s_fg")
        s_out = sem("s_out")
        s_gather = sem("s_gather")
        s_scatter = sem("s_scatter")
        s_a_out = sem("s_a_out")
        s_t_out = sem("s_t_out")
        filled = [sem(f"filled{b}") for b in range(8)]
        emptied = [sem(f"emptied{b}") for b in range(8)]
        zeroed = sem("zeroed")
        drv_done = sem("drv_done")
        ss_done = sem("ss_done")
        ms_done = sem("ms_done")
        sq_done = sem("sq_done")
        rstd_done = sem("rstd_done")
        xn_done = sem("xn_done")
        dif_done = sem("dif_done")
        k1_done = sem("k1_done")
        wd_done = sem("wd_done")
        wd_tanh = sem("wd_tanh")
        r1_done = sem("r1_done")
        v1_done = sem("v1_done")
        kk_raw = sem("kk_raw")
        kk_sq = sem("kk_sq")
        kk_root = sem("kk_root")
        kk_inv = sem("kk_inv")
        kk_done = sem("kk_done")
        thw1_done = sem("thw1_done")
        cs_done = sem("cs_done")
        pinc_done = sem("pinc_done")
        pinv_done = sem("pinv_done")
        kgain_done = sem("kgain_done")
        kp_done = sem("kp_done")
        a_done = sem("a_done")
        b_done = sem("b_done")
        bk_done = sem("bk_done")
        kr_done = sem("kr_done")
        rk_prod = sem("rk_prod")
        head_rk_done = sem("head_rk_done")
        bonus_done = sem("bonus_done")
        low_done = sem("low_done")
        inv_step = sem("inv_step")
        inv_done = sem("inv_done")
        tu_zero = sem("tu_zero")
        st_done = sem("st_done")
        csq_done = sem("csq_done")
        groot = sem("groot")
        ginv = sem("ginv")
        gn_step = sem("gn_step")
        yb_done = sem("yb_done")
        gth = sem("gth")
        gb_done = sem("gb_done")
        rot_done = sem("rot_done")
        nmax = sem("nmax")
        exp_done = sem("exp_done")
        rsum_done = sem("rsum_done")
        pr_done = sem("pr_done")
        fs_done = sem("fs_done")
        fm_done = sem("fm_done")
        fr_done = sem("fr_done")
        fi_done = sem("fi_done")
        o_done = sem("o_done")

        def free_bank(eng, job):
            b, turn = PLACE[job]
            if turn:
                eng.wait_ge(emptied[b], turn)
            return banks[b]

        def fill(ins, job):
            ins.then_inc(filled[PLACE[job][0]], 1)

        def full_bank(eng, job):
            b, turn = PLACE[job]
            eng.wait_ge(filled[b], turn + 1)
            return banks[b]

        def taken(eng, *job):
            b, turn = PLACE[job]
            eng.wait_ge(emptied[b], turn + 1)

        def empty(ins, job):
            ins.then_inc(emptied[PLACE[job][0]], 1)

        def state_ready(eng, c):
            if c == 0:
                taken(eng, "St", 0)
            else:
                eng.wait_ge(st_done, c)

        block = ctx.enter_context(nc.Block())

        @block.sync
        def _(sp):
            sp.dma_start(xt[:, 0, :], x[0:P, :]).then_inc(s_x, 16)
            sp.dma_start(xt[:, 1, :], x[P:SEQ, :]).then_inc(s_x, 16)
            sp.dma_start(cst[:, :], const).then_inc(s_const, 16)
            sp.dma_start(prm[:, :], param).then_inc(s_const, 16)
            for q in range(4):
                sp.dma_start(slots[0][:, 2 * q:2 * q + 2, :], w_blocks["k"][:, 2 * q:2 * q + 2, :]).then_inc(s_wk, 16)
            sp.dma_start(w_wd_sb[:, :, :], w_wd).then_inc(s_wwd, 16)
            sp.dma_start(up_sb[:, :], up).then_inc(s_up, 16)
            for n in range(1, len(BLOCKS)):
                if n >= SLOTS:
                    b, turn = PLACE[(BLOCKS[n - SLOTS], 1)]
                    sp.wait_ge(filled[b], turn + 1)
                if BLOCKS[n] == "av":
                    taken(sp, "A", 0)
                    taken(sp, "A", 1)
                    sp.dma_start(a_scratch, a_neg).then_inc(s_a_out, 16)
                    sp.wait_ge(s_a_out, 16)
                    for par in range(2):
                        for b in range(C // BASE):
                            u0, row, col = (par * 4 + b) * UNITS, 64 * par + BASE * b, BASE * b
                            sp.dma_start(blk[u0:u0 + UNITS, 0, :].rearrange("u (i j) -> u i j", i=BASE),
                                         a_scratch[row:row + BASE, :, col:col + BASE].rearrange("i u j -> u i j")
                                         ).then_inc(s_gather, 16)
                sp.dma_start(slots[n % SLOTS][:, :, :], w_blocks[BLOCKS[n]]).then_inc(s_w[n], 16)
                if BLOCKS[n] == "av":
                    sp.dma_start(fgain[:, :], final_gain.partition_broadcast(P)).then_inc(s_fg, 16)
                    sp.wait_ge(inv_done, 1)
                    sp.dma_start(t_scratch, blk[:, 1:3, :]).then_inc(s_t_out, 16)
                    sp.wait_ge(tu_zero, 2)
                    sp.wait_ge(s_t_out, 16)
                    for dst, src in ((t_inv, 0), (u_inv, 1)):
                        for par in range(2):
                            for b in range(C // BASE):
                                u0, row, col = (par * 4 + b) * UNITS, 64 * par + BASE * b, BASE * b
                                sp.dma_start(dst[row:row + BASE, :, col:col + BASE],
                                             t_scratch[u0:u0 + UNITS, src, :].rearrange("u (i j) -> i u j", i=BASE)
                                             ).then_inc(s_scatter, 16)
            for t in range(TT):
                sp.wait_ge(o_done, t + 1)
                sp.dma_start(out[t * P:(t + 1) * P, :], xt[:, t, :]).then_inc(s_out, 16)
            sp.wait_ge(s_out, 16 * TT)

        @block.gpsimd
        def _(pool):
            nc.gpsimd.memset(pad_a[:, :, 0:1], 0.0).then_inc(zeroed, 1)
            nc.gpsimd.memset(pad_b[:, :, 0:1], 0.0).then_inc(zeroed, 1)
            nc.gpsimd.memset(pad_w[:, 0:1], 0.0).then_inc(zeroed, 1)
            nc.gpsimd.memset(v1[:, :, 0:C], 0.0).then_inc(zeroed, 1)
            nc.gpsimd.memset(pinc[:, :, 0:1], 1.0).then_inc(zeroed, 1)
            nc.gpsimd.memset(sav[0:C, :, :, :], 0.0).then_inc(zeroed, 1)
            pool.wait_ge(kr_done, 2)
            pool.wait_ge(bk_done, 2)
            nc.gpsimd.memset(t_inv, 0.0).then_inc(tu_zero, 1)
            nc.gpsimd.memset(u_inv, 0.0).then_inc(tu_zero, 1)
            taken(pool, "A", 0)
            taken(pool, "A", 1)
            for m, dst in (("low16", b16), ("low32", b32)):
                nc.gpsimd.tensor_tensor(dst, a_neg, cn(m).unsqueeze(1).to_broadcast([P, UNITS, C]),
                                        ALU.mult).then_inc(low_done, 1)

        @block.scalar
        def _(act):
            for t in range(TT):
                act.wait_ge(s_x, 32)
                unused = (fgain[:, :], r1[:, :, :].rearrange("p a b -> p (a b)"))[t]
                nc.scalar.activation(unused, xt[:, t, :], ACT.Square,
                                     accum_out=stat[:, t:t + 1]).then_inc(ss_done, 1)
            act.wait_ge(ms_done, 1)
            nc.scalar.activation(stat[:, 4:6], stat[:, 2:4], ACT.Sqrt).then_inc(sq_done, 1)
            act.wait_ge(s_const, 32)
            for j in range(4):
                bank = full_bank(act, ("xT", j))
                for i in range(2):
                    ins = nc.scalar.activation(uT[:, 2 * j + i, :], bank[:, i * SEQ:(i + 1) * SEQ], ACT.Copy,
                                               scale=pm("norm_gain", 2 * j + i))
                    if i == 1:
                        empty(ins, ("xT", j))

            def to_pad(dst, job, j, n=2):
                bank = full_bank(act, job)
                ins = nc.scalar.activation(dst[:, n * j:n * j + n, 1:SEQ + 1],
                                           bank[:, 0:n * SEQ].rearrange("p (a b) -> p a b", a=n),
                                           ACT.Copy)
                empty(ins, job)

            act.wait_ge(zeroed, 6)
            for j in range(2):
                to_pad(pad_a, ("k", j), j)
            bank = full_bank(act, ("wd", 0))
            empty(nc.scalar.activation(pad_w[:, 1:SEQ + 1], bank[:, 0:SEQ], ACT.Copy), ("wd", 0))
            act.wait_ge(wd_done, 1)
            nc.scalar.activation(wd[0:64, :], wd[0:64, :], ACT.Tanh).then_inc(wd_tanh, 1)
            to_pad(pad_b, ("r", 0), 0)
            act.wait_ge(drv_done, 5)
            for j in range(2):
                bank = full_bank(act, ("upw", j))
                for i in range(2):
                    ins = nc.scalar.activation(thw[:, 2 * j + i, :], bank[:, i * SEQ:(i + 1) * SEQ], ACT.Tanh,
                                               scale=0.5, bias=drv[:, HALF_DB, 2 * j + i:2 * j + i + 1])
                    if i == 1:
                        empty(ins, ("upw", j))
                bank = full_bank(act, ("upa", j))
                for i in range(2):
                    ins = nc.scalar.activation(tha[:, 2 * j + i, :], bank[:, i * SEQ:(i + 1) * SEQ], ACT.Tanh,
                                               scale=0.5, bias=drv[:, HALF_IB, 2 * j + i:2 * j + i + 1])
                    if i == 1:
                        empty(ins, ("upa", j))
            for p in range(PAIRS):
                act.wait_ge(k1_done, p + 1)
                act.wait_ge(dif_done, 1)
                nc.scalar.activation(rn[:, p, :], k1[:, p, :], ACT.Square, scale=pm("k_k", p)).then_inc(kk_sq, 1)
            to_pad(pad_b, ("r", 1), 1)
            act.wait_ge(cs_done, PAIRS)
            cs_u = cs[:, :, :].rearrange("p a (b c) -> p (a b) c", c=C)
            nc.scalar.activation(pinc[:, :, 1:C + 1], cs_u, ACT.Exp, scale=-DECAY).then_inc(pinc_done, 1)
            nc.scalar.activation(cs_u, cs_u, ACT.Exp, scale=DECAY).then_inc(pinv_done, 1)
            taken(act, "kn", 0)
            taken(act, "kn", 1)
            nc.scalar.activation(rn[:, :, :], rn[:, :, :], ACT.Sqrt).then_inc(kk_root, 1)
            act.wait_ge(k1_done, PAIRS)
            for j in range(2):
                to_pad(pad_a, ("v", j), j)
            for j in range(2):
                bank = full_bank(act, ("qT", j))
                empty(nc.scalar.activation(qT[:, 2 * j:2 * j + 2, :], bank[:, :].rearrange("p (a b) -> p a b", a=2),
                                           ACT.Copy), ("qT", j))
            for j in range(2):
                bank = full_bank(act, ("kT", j))
                empty(nc.scalar.activation(kT[:, 2 * j:2 * j + 2, :], bank[:, :].rearrange("p (a b) -> p a b", a=2),
                                           ACT.Copy), ("kT", j))

            def value_tile(t):
                bank = full_bank(act, ("av", t))
                empty(nc.scalar.activation(v_att[:, t, :], bank[:, :], ACT.Copy), ("av", t))

            def tokens(c):
                if c >= 2:
                    taken(act, "Yc", c - 2)
                    taken(act, "St", c - 2)
                bank = full_bank(act, ("vT", c))
                empty(nc.scalar.activation(sav[C:P, c % 2, :, :], bank[C:P, :].rearrange("p (h v) -> p h v", h=HEADS),
                                           ACT.Copy), ("vT", c))
                bank = full_bank(act, ("bT", c))
                empty(nc.scalar.activation(bkt[:, c % 2, :, :], bank[:, :].rearrange("p (h v) -> p h v", h=HEADS),
                                           ACT.Copy), ("bT", c))

            def exps(h):
                act.wait_ge(nmax, h + 1)
                for t in range(TT):
                    a, b = (0, P) if t == 0 else (P, 3 * P)
                    nc.scalar.activation(pr[:, h % 2, a:b], pr[:, h % 2, a:b], ACT.Exp, scale=HEAD ** -0.5,
                                         bias=amax[:, h, 1, t:t + 1], accum_out=amax[:, h, 2, t:t + 1]).then_inc(exp_done, 1)

            def probs_T(h):
                bank = full_bank(act, ("PT", h))
                act.wait_ge(v1_done, PAIRS)
                if h >= 2:
                    taken(act, "PV", (h - 2) // 2)
                empty(nc.scalar.activation(prT[:, h % 2, :], bank[:, 0:3 * P], ACT.Copy), ("PT", h))

            def doubled(kind, half, dst):
                bank = full_bank(act, (kind, half))
                empty(nc.scalar.activation(dst[:, 8 * half:8 * half + 8, :], bank[:, :].rearrange("p (u c) -> p u c", c=C),
                                           ACT.Copy), (kind, half))

            def gate_tanh(kind, j, dst):
                bank = full_bank(act, (kind, j))
                nc.scalar.activation(dst[:, 2 * j:2 * j + 2, :], bank[:, :].rearrange("p (a b) -> p a b", a=2),
                                     ACT.Tanh, scale=0.5).then_inc(gth, 1)

            act.wait_ge(rk_prod, 1)
            value_tile(0)
            tokens(0)
            exps(0)
            exps(1)
            value_tile(1)
            doubled("Y1", 0, y_sb)
            doubled("Y1", 1, y_sb)
            probs_T(0)
            exps(2)
            probs_T(1)
            exps(3)
            taken(act, "U1", 1)
            doubled("Y2", 0, y_sb)
            doubled("Y2", 1, y_sb)
            gate_tanh("ga", 0, g_a)
            gate_tanh("ga", 1, g_a)
            for c in range(CHUNKS):
                bank = full_bank(act, ("R", c))
                if c >= 1:
                    taken(act, "SA", c - 1, 1)
                empty(nc.scalar.activation(r_neg[:, :, :], bank[:, 0:PAIRS * C].rearrange("p (a v) -> p a v", a=PAIRS),
                                           ACT.Copy, scale=-1.0), ("R", c))
                if c < 3:
                    probs_T(2 * c + 2)
                    if 2 * c + 4 < HEADS:
                        exps(2 * c + 4)
                if c < 2:
                    gate_tanh("gb", c, g_b)
                if c < 3:
                    probs_T(2 * c + 3)
                    if 2 * c + 5 < HEADS:
                        exps(2 * c + 5)
                if c + 1 < CHUNKS:
                    tokens(c + 1)
                bank = full_bank(act, ("Yc", c))
                if c >= 2:
                    act.wait_ge(yb_done, c - 1)
                empty(nc.scalar.activation(yc[:, c % 2, :, :], bank[:, 0:PAIRS * C].rearrange("p (a v) -> p a v", a=PAIRS),
                                           ACT.Copy), ("Yc", c))
                taken(act, "mean", c)
                nc.scalar.activation(gn_r[:, c % 2, :, :], yc[:, c % 2, :, :], ACT.Square).then_inc(csq_done, 1)
                taken(act, "var", c)
                nc.scalar.activation(gn_r[:, c % 2, :, :], gn_r[:, c % 2, :, :], ACT.Sqrt).then_inc(groot, 1)
            for t in range(TT):
                taken(act, "out", t, 0)
                taken(act, "out", t, 1)
                nc.scalar.activation(slots[1][:, 2 * t:2 * t + 2, :].rearrange("p a b -> p (a b)"), xt[:, t, :], ACT.Square,
                                     accum_out=stat[:, t:t + 1]).then_inc(fs_done, 1)
                act.wait_ge(fm_done, t + 1)
                nc.scalar.activation(stat[:, 4 + t:5 + t], stat[:, 2 + t:3 + t], ACT.Sqrt).then_inc(fr_done, 1)

        @block.vector
        def _(dve):
            V = nc.vector
            dve.wait_ge(ss_done, TT)
            V.tensor_scalar(stat[:, 2:4], stat[:, 0:2], 1.0 / D_MODEL, 1e-6, ALU.mult, ALU.add).then_inc(ms_done, 1)
            dve.wait_ge(sq_done, 1)
            V.reciprocal(stat[:, 6:8], stat[:, 4:6]).then_inc(rstd_done, 1)
            dve.wait_ge(rstd_done, 1)
            for t in range(TT):
                V.tensor_scalar(xn_tiles[t], xt[:, t, :], stat[:, 6 + t:7 + t], None, ALU.mult).then_inc(xn_done, 1)
            dve.wait_ge(s_const, 32)
            for i, (name, s, o) in enumerate((("decay_bias", 0.5, 0.0), ("iclr_bias", 0.5, 0.0), ("k_a", 0.5, 0.0),
                                              ("k_a", -0.5, 1.0), ("gn_gain", 0.5, 0.0))):
                V.tensor_scalar(drv[:, i, :], pm_all(name), s, o, ALU.mult, ALU.add).then_inc(drv_done, 1)
            for p in range(PAIRS):
                V.tensor_scalar(head_rk[:, p, :], cn("head_sum"), pm("r_k", p), None, ALU.mult).then_inc(head_rk_done, 1)

            def shift(pad, mu, dst, off, kind, n_dif, done, after=None):
                taken(dve, kind, 0)
                taken(dve, kind, 1)
                if after is not None:
                    dve.wait_ge(*after)
                V.tensor_tensor(dif[:, :, :], pad[:, :, 0:SEQ], pad[:, :, 1:SEQ + 1], ALU.subtract).then_inc(dif_done, 1)
                dve.wait_ge(dif_done, n_dif)
                for p in range(PAIRS):
                    V.scalar_tensor_tensor(dst[:, p, off:off + SEQ], dif[:, p, :], pm(mu, p), pad[:, p, 1:SEQ + 1],
                                           ALU.mult, ALU.add).then_inc(done, 1)

            shift(pad_a, "mu_k", k1, 0, "k", 1, k1_done)
            taken(dve, "wd", 0)
            dve.wait_ge(k1_done, PAIRS)
            V.tensor_tensor(dif[:, 0, :], pad_w[:, 0:SEQ], pad_w[:, 1:SEQ + 1], ALU.subtract).then_inc(dif_done, 1)
            dve.wait_ge(dif_done, 2)
            V.scalar_tensor_tensor(wd[:, :], dif[:, 0, :], pm("mu_w"), pad_w[:, 1:SEQ + 1], ALU.mult, ALU.add).then_inc(wd_done, 1)
            dve.wait_ge(k1_done, PAIRS)
            for p in range(PAIRS):
                V.tensor_scalar(kk[:, p, :], k1[:, p, :], pm("k_k", p), None, ALU.mult).then_inc(kk_raw, 1)
            for p in range(PAIRS):
                taken(dve, "upw", p // 2)
                V.tensor_scalar(thw[:, p, :], thw[:, p, :], 1.0, None, ALU.add).then_inc(thw1_done, 1)
                dve.wait_ge(thw1_done, p + 1)
                V.tensor_tensor_scan(cs[:, p, :], cn("scan"), thw[:, p, :], 0.0, ALU.mult, ALU.add).then_inc(cs_done, 1)
            for p in range(PAIRS):
                taken(dve, "upa", p // 2)
                dve.wait_ge(drv_done, 5)
                V.tensor_scalar(kp[:, p, :], tha[:, p, :], drv[:, HALF_KA, p:p + 1], drv[:, ONE_KA, p:p + 1],
                                ALU.mult, ALU.add).then_inc(kgain_done, 1)
            dve.wait_ge(kgain_done, PAIRS)
            V.tensor_scalar(tha[:, :, :], tha[:, :, :], 0.5, 0.5, ALU.mult, ALU.add).then_inc(a_done, 1)
            V.tensor_tensor(kp[:, :, :], kp[:, :, :], k1[:, :, :], ALU.mult).then_inc(kp_done, 1)
            shift(pad_b, "mu_r", r1, 0, "r", 3, r1_done, (wd_done, 1))
            for j in range(2):
                bank = full_bank(dve, ("kn", j))
                empty(V.tensor_scalar(rn[:, 2 * j:2 * j + 2, :], bank[:, :].rearrange("p (a b) -> p a b", a=2),
                                      1e-24, None, ALU.max), ("kn", j))
            dve.wait_ge(kk_root, 1)
            V.reciprocal(rn[:, :, :], rn[:, :, :]).then_inc(kk_inv, 1)
            dve.wait_ge(kp_done, 1)
            dve.wait_ge(kk_inv, 1)
            dve.wait_ge(kk_raw, PAIRS)
            V.tensor_tensor(kk[:, :, :], kk[:, :, :], rn[:, :, :], ALU.mult).then_inc(kk_done, 1)
            dve.wait_ge(kk_done, 1)
            dve.wait_ge(a_done, 1)
            V.tensor_tensor(tha[:, :, :], tha[:, :, :], kk[:, :, :], ALU.mult).then_inc(b_done, 1)

            def units(t):
                return t[:, :, :].rearrange("p a (b c) -> p (a b) c", c=C)

            dve.wait_ge(pinc_done, 1)
            V.tensor_tensor(kr[:, :, 0, :], units(kk), pinc[:, :, 0:C], ALU.mult).then_inc(kr_done, 1)
            dve.wait_ge(pinv_done, 1)
            dve.wait_ge(b_done, 1)
            taken(dve, "xT", 3)
            V.tensor_tensor(bk[:, :, 0, :], units(tha), units(cs), ALU.mult).then_inc(bk_done, 1)
            dve.wait_ge(kp_done, 1)
            V.tensor_tensor(bk[:, :, 1, :], units(kp), units(cs), ALU.mult).then_inc(bk_done, 1)
            dve.wait_ge(r1_done, PAIRS)
            V.tensor_tensor(kr[:, :, 1, :], units(r1), pinc[:, :, 1:C + 1], ALU.mult).then_inc(kr_done, 1)
            V.tensor_tensor(k1[:, :, :], r1[:, :, :], kp[:, :, :], ALU.mult).then_inc(rk_prod, 1)
            shift(pad_a, "mu_v", v1, C, "v", 4, v1_done, (r1_done, PAIRS))

            def rotate(kind, t, dst, n):
                bank = full_bank(dve, (kind, t))
                v = bank[:, :].rearrange("p (h d) -> p h d", d=HEAD)
                cos = cn("cos")[:, t * HEAD:(t + 1) * HEAD].unsqueeze(1).to_broadcast([P, HEADS, HEAD])
                sin = cn("sin")[:, t * HEAD:(t + 1) * HEAD].unsqueeze(1).to_broadcast([P, HEADS, HEAD])
                o = dst[:, t, :].rearrange("p (h d) -> p h d", d=HEAD)
                tmp = rtmp[:, (n % 2) * WIDTH:(n % 2 + 1) * WIDTH].rearrange("p (h d) -> p h d", d=HEAD)
                H2 = HEAD // 2
                if n >= 2:
                    dve.wait_ge(rot_done, n - 1)
                V.tensor_tensor(o, v, cos, ALU.mult)
                V.tensor_tensor(tmp[:, :, 0:H2], v[:, :, H2:HEAD], sin[:, :, 0:H2], ALU.mult)
                empty(V.tensor_tensor(tmp[:, :, H2:HEAD], v[:, :, 0:H2], sin[:, :, H2:HEAD], ALU.mult), (kind, t))
                taken(dve, kind, t)
                V.tensor_tensor(o, o, tmp, ALU.add).then_inc(rot_done, 1)

            dve.wait_ge(v1_done, PAIRS)
            for t in range(TT):
                rotate("aq", t, rot, t)
            for j in range(2):
                bank = full_bank(dve, ("bonus", j))
                ins = V.tensor_tensor(bonus[:, 2 * j:2 * j + 2, :], bank[:, :].rearrange("p (a b) -> p a b", a=2),
                                      v1[:, 2 * j:2 * j + 2, C:C + SEQ], ALU.mult)
                empty(ins, ("bonus", j))
            taken(dve, "bonus", 0)
            taken(dve, "bonus", 1)
            for p in range(PAIRS):
                V.tensor_scalar(bonus[:, p, :], bonus[:, p, :], pm("gn_bias", p), None, ALU.add).then_inc(bonus_done, 1)
            rotate("ak", 0, rot_k, 2)
            for j in range(2):
                bank = full_bank(dve, ("A", j))
                ins = V.tensor_tensor(a_neg[:, 8 * j:8 * j + 8, :], bank[:, :].rearrange("p (u c) -> p u c", c=C),
                                      cn("a_mask").unsqueeze(1).to_broadcast([P, 8, C]), ALU.mult)
                empty(ins, ("A", j))
            rotate("ak", 1, rot_k, 3)

            dve.wait_ge(s_gather, 16 * 8)
            V.tensor_copy(blk[:, 1, :], cn("block_eye")).then_inc(inv_step, 1)
            A = blk[:, 0, :].rearrange("p (i j) -> p i j", i=BASE)
            T = blk[:, 1, :].rearrange("p (i j) -> p i j", i=BASE)
            TTr = blk[:, 1, :].rearrange("p (i j) -> p j i", i=BASE)
            prod = blk[:, 3, :].rearrange("p (i j) -> p i j", i=BASE)
            steps = 1
            for i in range(1, BASE):
                dve.wait_ge(inv_step, steps)
                V.tensor_tensor(prod[:, 0:i, 0:i], TTr[:, 0:i, 0:i], A[:, i:i + 1, 0:i].to_broadcast([P, i, i]),
                                ALU.mult).then_inc(inv_step, 1)
                dve.wait_ge(inv_step, steps + 1)
                V.tensor_reduce(T[:, i, 0:i], prod[:, 0:i, 0:i], AX.X, ALU.add).then_inc(inv_step, 1)
                steps += 2
            dve.wait_ge(inv_step, steps)
            V.tensor_copy(blk[:, 2, :].rearrange("p (i j) -> p i j", i=BASE), TTr).then_inc(inv_done, 1)

            def gram(c, par):
                if c >= 2:
                    taken(dve, "Yc", c - 2)
                bank = full_bank(dve, ("gram", c, par))
                heads = lr[:, c % 2, :, :].rearrange("p (a b) n -> p a b n", b=2)[:, :, par, :]
                ins = V.tensor_tensor(heads, bank[:, :].rearrange("p (a n) -> p a n", a=PAIRS),
                                      cn("gram_mask").unsqueeze(1).to_broadcast([P, PAIRS, P]), ALU.mult)
                empty(ins, ("gram", c, par))

            def scores(h):
                bank = full_bank(dve, ("S", h))
                if h >= 2:
                    taken(dve, "PT", h - 2)
                for t in range(TT):
                    a, b = (0, P) if t == 0 else (P, 3 * P)
                    ins = V.tensor_tensor_reduce(out=pr[:, h % 2, a:b], in0=bank[:, a:b], in1=cn("causal")[:, a:b],
                                                 scale=1.0, scalar=-3.0e38, op0=ALU.add, op1=ALU.max,
                                                 accum_out=amax[:, h, 0, t:t + 1])
                empty(ins, ("S", h))
                taken(dve, "S", h)
                V.tensor_scalar(amax[:, h, 1, :], amax[:, h, 0, :], -HEAD ** -0.5, None, ALU.mult).then_inc(nmax, 1)

            def normalise(h):
                dve.wait_ge(exp_done, TT * (h + 1))
                V.reciprocal(amax[:, h, 0, :], amax[:, h, 2, :]).then_inc(rsum_done, 1)
                dve.wait_ge(rsum_done, h + 1)
                for t in range(TT):
                    a, b = (0, P) if t == 0 else (P, 3 * P)
                    V.tensor_scalar(pr[:, h % 2, a:b], pr[:, h % 2, a:b], amax[:, h, 0, t:t + 1], None,
                                    ALU.mult).then_inc(pr_done, 1)

            def head_out(p):
                bank = full_bank(dve, ("PV", p))
                taken(dve, "ga", 1)
                empty(V.scalar_tensor_tensor(ycat[:, p, :], bank[:, 0:SEQ], 0.5, g_a[:, p, :], ALU.mult,
                                             ALU.mult), ("PV", p))

            def doubled(kind, half, dst):
                bank = full_bank(dve, (kind, half))
                d = dst[:, 8 * half:8 * half + 8, :]
                empty(V.tensor_tensor(d, bank[:, :].rearrange("p (u c) -> p u c", c=C), d, ALU.add),
                      (kind, half))

            def gate(kind, j, dst, n):
                dve.wait_ge(gth, n)
                bank = full_bank(dve, (kind, j))
                d = dst[:, 2 * j:2 * j + 2, :]
                empty(V.scalar_tensor_tensor(d, d, 1.0, bank[:, :].rearrange("p (a b) -> p a b", a=2), ALU.add,
                                             ALU.mult), (kind, j))

            gram(0, 0)
            gram(0, 1)
            scores(0)
            scores(1)
            normalise(0)
            normalise(1)
            scores(2)
            dve.wait_ge(s_scatter, 16 * 16)
            for half in range(2):
                doubled("U1", half, u_inv)
                doubled("T1", half, t_inv)
            scores(3)
            doubled("U2", 0, u_inv)
            doubled("U2", 1, u_inv)
            gate("ga", 0, g_a, 1)
            gate("ga", 1, g_a, 2)
            head_out(0)
            for c in range(CHUNKS):
                if c < 3:
                    normalise(2 * c + 2)
                    if 2 * c + 4 < HEADS:
                        scores(2 * c + 4)
                if c < 2:
                    gate("gb", c, g_b, 3 + c)
                for par in range(2):
                    bank = full_bank(dve, ("SA", c, par))
                    heads = sav[0:C, c % 2, :, :].rearrange("p (a b) v -> p a b v", b=2)[:, :, par, :]
                    dve.wait_ge(zeroed, 6)
                    empty(V.tensor_copy(heads, bank[0:C, 0:PAIRS * C].rearrange("p (a v) -> p a v", a=PAIRS)),
                          ("SA", c, par))
                if c < 3:
                    normalise(2 * c + 3)
                    if 2 * c + 5 < HEADS:
                        scores(2 * c + 5)
                    head_out(c + 1)
                if c + 1 < CHUNKS:
                    gram(c + 1, 0)
                    gram(c + 1, 1)
                    bank = full_bank(dve, ("St", c))
                    new, old = state[:, (c + 1) % 2, :, :], state[:, c % 2, :, :]
                    p_end = pinc[:, :, C:C + 1].rearrange("p (a b) o -> p a b o", b=CHUNKS)[:, :, c, :].to_broadcast([P, PAIRS, C])
                    st = bank[:, 0:PAIRS * C].rearrange("p (a v) -> p a v", a=PAIRS)
                    if c == 0:
                        empty(V.tensor_tensor(new, st, p_end, ALU.mult), ("St", c))
                    else:
                        state_ready(dve, c - 1)
                        empty(V.tensor_tensor(new, st, old, ALU.add), ("St", c))
                        taken(dve, "St", c)
                        V.tensor_tensor(new, new, p_end, ALU.mult).then_inc(st_done, 1)
                y = yc[:, c % 2, :, :]
                taken(dve, "Yc", c)
                bank = full_bank(dve, ("mean", c))
                empty(V.tensor_tensor(y, y, bank[:, 0:PAIRS * C].rearrange("p (a v) -> p a v", a=PAIRS),
                                      ALU.subtract), ("mean", c))
                bank = full_bank(dve, ("var", c))
                g = gn_r[:, c % 2, :, :]
                empty(V.tensor_scalar(g, bank[:, 0:PAIRS * C].rearrange("p (a v) -> p a v", a=PAIRS), 64e-5, None,
                                      ALU.add), ("var", c))
                if c == 1:
                    taken(dve, "gb", 1)
                    dve.wait_ge(bonus_done, PAIRS)
                    V.scalar_tensor_tensor(bonus[:, :, :], bonus[:, :, :], 0.5, g_b[:, :, :], ALU.mult, ALU.mult).then_inc(bonus_done, 1)
                    dve.wait_ge(bonus_done, 1 + PAIRS)
                    for p in range(PAIRS):
                        V.tensor_scalar(g_b[:, p, :], g_b[:, p, :], drv[:, HALF_GAIN, p:p + 1], None, ALU.mult).then_inc(gb_done, 1)
                for cc in ([c] if c >= 2 else [0, 1] if c == 1 else []):
                    y = yc[:, cc % 2, :, :]
                    g = gn_r[:, cc % 2, :, :]
                    tok = slice(cc * C, (cc + 1) * C)
                    dve.wait_ge(groot, cc + 1)
                    V.reciprocal(g, g).then_inc(ginv, 1)
                    dve.wait_ge(ginv, cc + 1)
                    V.tensor_tensor(y, y, g, ALU.mult).then_inc(gn_step, 1)
                    dve.wait_ge(gn_step, 2 * cc + 1)
                    dve.wait_ge(gb_done, PAIRS)
                    V.tensor_tensor(y, y, g_b[:, :, tok], ALU.mult).then_inc(gn_step, 1)
                    dve.wait_ge(gn_step, 2 * cc + 2)
                    dve.wait_ge(bonus_done, 1 + PAIRS)
                    V.tensor_tensor(ycat[:, PAIRS:2 * PAIRS, tok], y, bonus[:, :, tok], ALU.add).then_inc(yb_done, 1)
            for t in range(TT):
                for n in range(2):
                    bank = full_bank(dve, ("out", t, n))
                    h = xt[:, t, n * 512:(n + 1) * 512]
                    empty(V.tensor_tensor(h, bank[:, :], h, ALU.add), ("out", t, n))
            for t in range(TT):
                dve.wait_ge(fs_done, t + 1)
                V.tensor_scalar(stat[:, 2 + t:3 + t], stat[:, t:t + 1], 1.0 / D_MODEL, 1e-6, ALU.mult, ALU.add).then_inc(fm_done, 1)
                dve.wait_ge(fr_done, t + 1)
                V.reciprocal(stat[:, 6 + t:7 + t], stat[:, 4 + t:5 + t]).then_inc(fi_done, 1)
                dve.wait_ge(fi_done, t + 1)
                dve.wait_ge(s_fg, 16)
                V.scalar_tensor_tensor(xt[:, t, :], xt[:, t, :], stat[:, 6 + t:7 + t], fgain[:, :], ALU.mult,
                                       ALU.mult).then_inc(o_done, 1)

        @block.tensor
        def _(pe):
            mm = nc.tensor.matmul

            def rows(par):
                return slice(64 * par, 64 * par + 64)

            def block_ready(name):
                n = BLOCKS.index(name)
                if n == 0:
                    pe.wait_ge(s_wk, 64)
                else:
                    pe.wait_ge(s_w[n], 16)
                return slots[n % SLOTS]

            def project_T(name, j):
                bank = free_bank(pe, (name, j))
                w = block_ready(name)
                taken(pe, "xT", 3)
                for i in range(2):
                    for k in range(KC):
                        if name == "k":
                            pe.wait_ge(s_wk, 64)
                        ch = (2 * j + i) * P
                        ins = mm(bank[:, i * SEQ:(i + 1) * SEQ], w[:, k, ch:ch + P], uT[:, k, :],
                                 start=(k == 0), stop=(k == KC - 1))
                fill(ins, (name, j))

            def project(name, t):
                bank = free_bank(pe, (name, t))
                w = block_ready(name)
                for k in range(KC):
                    ins = mm(bank[:, :], uT[:, k, t * P:(t + 1) * P], w[:, k, :], start=(k == 0), stop=(k == KC - 1))
                fill(ins, (name, t))

            def project_wd():
                bank = free_bank(pe, ("wd", 0))
                pe.wait_ge(s_wwd, 16)
                for k in range(KC):
                    ins = mm(bank[:, 0:SEQ], w_wd_sb[:, k, :], uT[:, k, :], start=(k == 0), stop=(k == KC - 1))
                fill(ins, ("wd", 0))

            def up_project(kind, j):
                bank = free_bank(pe, (kind, j))
                pe.wait_ge(s_up, 16)
                pe.wait_ge(wd_done, 1)
                pe.wait_ge(wd_tanh, 1)
                r = rows(0 if kind == "upw" else 1)
                for i in range(2):
                    ch = (2 * j + i) * P
                    ins = mm(bank[:, i * SEQ:(i + 1) * SEQ], up_sb[r, ch:ch + P], wd[r, :], start=True, stop=True)
                fill(ins, (kind, j))

            def head_sums(kind, j):
                bank = free_bank(pe, (kind, j))
                if kind == "kn":
                    pe.wait_ge(kk_sq, 2 * j + 2)
                    ins = mm(bank[:, :], cn("head_sum"), rn[:, 2 * j:2 * j + 2, :].rearrange("p a b -> p (a b)"),
                             start=True, stop=True)
                else:
                    pe.wait_ge(rk_prod, 1)
                    pe.wait_ge(head_rk_done, PAIRS)
                    for i in range(2):
                        ins = mm(bank[:, i * SEQ:(i + 1) * SEQ], head_rk[:, 2 * j + i, :], k1[:, 2 * j + i, :],
                                 start=True, stop=True)
                fill(ins, (kind, j))

            def a_matrix(half):
                bank = free_bank(pe, ("A", half))
                pe.wait_ge(kr_done, 1)
                pe.wait_ge(bk_done, 1)
                for n in range(8):
                    c, p = 2 * half + n // PAIRS, n % PAIRS
                    u = p * CHUNKS + c
                    for par in range(2):
                        ins = mm(bank[rows(par), n * C:(n + 1) * C], kr[rows(par), u, 0, :], bk[rows(par), u, 0, :],
                                 start=True, stop=True)
                fill(ins, ("A", half))

            def transposed(kind, j, src):
                bank = free_bank(pe, (kind, j))
                for i in range(2):
                    for t in range(TT):
                        at = i * SEQ + t * P
                        ins = nc.tensor.transpose(bank[:, at:at + P], src[:, t, (2 * j + i) * P:(2 * j + i + 1) * P], cn("ident"))
                fill(ins, (kind, j))

            def tokens(c):
                bank = free_bank(pe, ("vT", c))
                pe.wait_ge(v1_done, PAIRS)
                pe.wait_ge(zeroed, 6)
                for p in range(PAIRS):
                    ins = nc.tensor.transpose(bank[:, p * P:(p + 1) * P], v1[:, p, c * C:c * C + P], cn("ident"))
                fill(ins, ("vT", c))
                bank = free_bank(pe, ("bT", c))
                pe.wait_ge(bk_done, 2)
                for p in range(PAIRS):
                    src = bk[:, p * CHUNKS + c, :, :].rearrange("p s c -> p (s c)")
                    ins = nc.tensor.transpose(bank[:, p * P:(p + 1) * P], src, cn("ident"))
                fill(ins, ("bT", c))

            def gram(c, par):
                bank = free_bank(pe, ("gram", c, par))
                pe.wait_ge(kr_done, 2)
                for p in range(PAIRS):
                    u = p * CHUNKS + c
                    ins = mm(bank[:, p * P:(p + 1) * P], bk[rows(par), u, :, :].rearrange("p s c -> p (s c)"),
                             kr[rows(par), u, :, :].rearrange("p s c -> p (s c)"), start=True, stop=True)
                fill(ins, ("gram", c, par))

            def scores(h):
                p, par = h // 2, h % 2
                bank = free_bank(pe, ("S", h))
                taken(pe, "qT", p // 2)
                taken(pe, "kT", p // 2)
                mm(bank[:, 0:P], qT[rows(par), p, 0:P], kT[rows(par), p, 0:P], start=True, stop=True)
                ins = mm(bank[:, P:3 * P], qT[rows(par), p, P:SEQ], kT[rows(par), p, :], start=True, stop=True)
                fill(ins, ("S", h))

            def probs_T(h):
                bank = free_bank(pe, ("PT", h))
                pe.wait_ge(pr_done, TT * (h + 1))
                for i in range(3):
                    ins = nc.tensor.transpose(bank[:, i * P:(i + 1) * P], pr[:, h % 2, i * P:(i + 1) * P], cn("ident"))
                fill(ins, ("PT", h))

            def head_out(p):
                bank = free_bank(pe, ("PV", p))
                taken(pe, "PT", 2 * p)
                taken(pe, "PT", 2 * p + 1)
                taken(pe, "av", 0)
                taken(pe, "av", 1)
                for par in range(2):
                    h = 2 * p + par
                    mm(bank[rows(par), 0:SEQ], v_att[:, 0, h * HEAD:(h + 1) * HEAD], prT[:, par, 0:SEQ], start=True, stop=False)
                    ins = mm(bank[rows(par), P:SEQ], v_att[:, 1, h * HEAD:(h + 1) * HEAD], prT[:, par, SEQ:3 * P],
                             start=False, stop=True)
                fill(ins, ("PV", p))

            def double(kind, half, lhs, rhs):
                bank = free_bank(pe, (kind, half))
                for n in range(8):
                    u = 8 * half + n
                    for par in range(2):
                        ins = mm(bank[rows(par), n * C:(n + 1) * C], lhs[rows(par), u, :], rhs[rows(par), u, :],
                                 start=True, stop=True)
                fill(ins, (kind, half))

            def right_side(c):
                bank = free_bank(pe, ("R", c))
                taken(pe, "gram", c, 0)
                taken(pe, "gram", c, 1)
                taken(pe, "vT", c)
                for h in range(HEADS):
                    p, par = h // 2, h % 2
                    ins = mm(bank[rows(par), p * C:(p + 1) * C], lr[:, c % 2, h, 0:C], sav[:, c % 2, h, :],
                             start=(p == 0), stop=(c == 0), skip_group_check=True)
                if c:
                    state_ready(pe, c - 1)
                    for h in range(HEADS):
                        p, par = h // 2, h % 2
                        ins = mm(bank[rows(par), p * C:(p + 1) * C], kr[rows(par), p * CHUNKS + c, 0, :],
                                 state[rows(par), c % 2, p, :], start=False, stop=True, skip_group_check=True)
                fill(ins, ("R", c))

            def solve(c, par):
                bank = free_bank(pe, ("SA", c, par))
                taken(pe, "R", c)
                taken(pe, "U2", c // 2)
                for p in range(PAIRS):
                    ins = mm(bank[0:C, p * C:(p + 1) * C], u_inv[rows(par), c * PAIRS + p, :], r_neg[rows(par), p, :],
                             start=True, stop=True)
                fill(ins, ("SA", c, par))

            def new_state(c):
                bank = free_bank(pe, ("St", c))
                taken(pe, "SA", c, 0)
                taken(pe, "SA", c, 1)
                taken(pe, "bT", c)
                for h in range(HEADS):
                    p, par = h // 2, h % 2
                    ins = mm(bank[rows(par), p * C:(p + 1) * C], bkt[:, c % 2, h, :], sav[:, c % 2, h, :], start=True, stop=True)
                fill(ins, ("St", c))

            def chunk_out(c):
                bank = free_bank(pe, ("Yc", c))
                taken(pe, "SA", c, 0)
                taken(pe, "SA", c, 1)
                for h in range(HEADS):
                    p, par = h // 2, h % 2
                    ins = mm(bank[rows(par), p * C:(p + 1) * C], sav[:, c % 2, h, :], lr[:, c % 2, h, C:P],
                             start=(p == 0), stop=(c == 0), skip_group_check=True)
                if c:
                    for h in range(HEADS):
                        p, par = h // 2, h % 2
                        ins = mm(bank[rows(par), p * C:(p + 1) * C], state[rows(par), c % 2, p, :],
                                 kr[rows(par), p * CHUNKS + c, 1, :], start=False, stop=True, skip_group_check=True)
                fill(ins, ("Yc", c))

            def mean(c):
                bank = free_bank(pe, ("mean", c))
                taken(pe, "Yc", c)
                fill(mm(bank[:, 0:PAIRS * C], cn("head_mean"), yc[:, c % 2, :, :].rearrange("p a v -> p (a v)"),
                        start=True, stop=True), ("mean", c))

            def var(c):
                bank = free_bank(pe, ("var", c))
                pe.wait_ge(csq_done, c + 1)
                fill(mm(bank[:, 0:PAIRS * C], cn("head_mean"), gn_r[:, c % 2, :, :].rearrange("p a v -> p (a v)"),
                        start=True, stop=True), ("var", c))

            def out_project(t, n):
                bank = free_bank(pe, ("out", t, n))
                w = block_ready(f"wo{n}")
                taken(pe, "PV", PAIRS - 1)
                for k in range(2 * PAIRS):
                    if k == PAIRS:
                        pe.wait_ge(yb_done, 2 * t + 2)
                    ins = mm(bank[:, :], ycat[:, k, t * P:(t + 1) * P], w[:, k, :], start=(k == 0), stop=(k == KC - 1))
                fill(ins, ("out", t, n))

            def x_transposed(j):
                bank = free_bank(pe, ("xT", j))
                pe.wait_ge(s_const, 32)
                pe.wait_ge(xn_done, TT)
                for i in range(2):
                    for t in range(TT):
                        at = i * SEQ + t * P
                        ins = nc.tensor.transpose(bank[:, at:at + P], xn_tiles[t][:, (2 * j + i) * P:(2 * j + i + 1) * P],
                                                  cn("ident"))
                fill(ins, ("xT", j))

            for name, _ in job_order():
                kind, args = name[0], name[1:]
                if kind == "xT":
                    x_transposed(*args)
                elif kind in ("k", "r", "v", "ga", "gb"):
                    project_T(kind, *args)
                elif kind == "wd":
                    project_wd()
                elif kind in ("aq", "ak", "av"):
                    project(kind, *args)
                elif kind in ("upw", "upa"):
                    up_project(kind, *args)
                elif kind in ("kn", "bonus"):
                    head_sums(kind, *args)
                elif kind == "A":
                    a_matrix(*args)
                elif kind in ("qT", "kT"):
                    pe.wait_ge(rot_done, 2 if kind == "qT" else 4)
                    transposed(kind, *args, rot if kind == "qT" else rot_k)
                elif kind == "vT":
                    tokens(*args)
                elif kind == "gram":
                    gram(*args)
                elif kind == "S":
                    scores(*args)
                elif kind == "PT":
                    probs_T(*args)
                elif kind == "PV":
                    head_out(*args)
                elif kind == "Y1":
                    pe.wait_ge(s_scatter, 16 * 16)
                    pe.wait_ge(low_done, 1)
                    double(kind, *args, b16, u_inv)
                elif kind == "T1":
                    taken(pe, "Y1", args[0])
                    double(kind, *args, y_sb, t_inv)
                elif kind == "U1":
                    double(kind, *args, t_inv, y_sb)
                elif kind == "Y2":
                    taken(pe, "U1", args[0])
                    pe.wait_ge(low_done, 2)
                    double(kind, *args, b32, u_inv)
                elif kind == "U2":
                    taken(pe, "T1", args[0])
                    taken(pe, "Y2", args[0])
                    double(kind, *args, t_inv, y_sb)
                elif kind == "R":
                    right_side(*args)
                elif kind == "SA":
                    solve(*args)
                elif kind == "St":
                    new_state(*args)
                elif kind == "Yc":
                    chunk_out(*args)
                elif kind == "mean":
                    mean(*args)
                elif kind == "var":
                    var(*args)
                elif kind == "out":
                    out_project(*args)


def constants():
    a = np.zeros((P, N_CONST), np.float32)
    i = np.arange(P)

    def put(name, v):
        s, e = CONST[name]
        a[:, s:e] = v

    put("ident", np.eye(P))
    same = (i[:, None] // HEAD == i[None, :] // HEAD).astype(np.float32)
    put("head_sum", same)
    put("head_mean", same / HEAD)
    j, t, col = i[:, None] % C, i[None, :] % C, i[None, :] // C
    g = np.where(col == 0, j < t, j <= t).astype(np.float32)
    g[0:C, 0:C] = 0
    put("gram_mask", g)
    r, q = i[:, None] % C, np.arange(C)[None, :]
    put("a_mask", np.where(q < r, -1.0, 0.0))
    put("low16", (r // 32 == q // 32) & (r % 32 >= 16) & (q % 32 < 16))
    put("low32", (r >= 32) & (q < 32))
    put("scan", (np.arange(SEQ) % C != 0)[None, :])
    causal = np.where(i[None, :] <= i[:, None], 0.0, -1e30)
    put("causal", np.concatenate([causal, np.zeros((P, P)), causal], 1))
    inv = 1.0 / (np.float32(10000.0) ** (np.arange(0, HEAD, 2, dtype=np.float32) / np.float32(HEAD)))
    ang = np.arange(SEQ, dtype=np.float32)[:, None] * inv[None, :].astype(np.float32)
    cos, sin = np.cos(ang), np.sin(ang)
    cos2, sin2 = np.concatenate([cos, cos], 1), np.concatenate([-sin, sin], 1)
    put("cos", cos2.reshape(TT, P, HEAD).transpose(1, 0, 2).reshape(P, -1))
    put("sin", sin2.reshape(TT, P, HEAD).transpose(1, 0, 2).reshape(P, -1))
    put("block_eye", np.eye(BASE).reshape(1, -1))
    return a


def kernel(x, norm_gain, w_in, shift_mu, decay_bias, decay_up, iclr_bias, iclr_up,
           k_k, k_a, r_k, gn_gain, gn_bias, w_out, final_gain):
    import concourse.bacc as bacc
    from concourse.bass_utils import run_bass_kernel_spmd as run

    w = np.asarray(w_in)[0].reshape(KC, P, -1).transpose(1, 0, 2)
    wo = np.asarray(w_out)[0].reshape(KC, P, -1).transpose(1, 0, 2)
    W = WIDTH
    start = {"aq": 0, "ak": W, "av": 2 * W, "ga": 3 * W, "r": 4 * W, "k": 5 * W, "v": 6 * W, "gb": 7 * W + P}
    arrays = {"in_" + n: np.ascontiguousarray(w[:, :, s:s + W]) for n, s in start.items()}
    arrays["in_wo0"] = np.ascontiguousarray(wo[:, :, 0:512])
    arrays["in_wo1"] = np.ascontiguousarray(wo[:, :, 512:1024])
    arrays["in_wd"] = np.ascontiguousarray(w[:, :, 7 * W:7 * W + P])
    arrays["in_up"] = np.concatenate([np.asarray(decay_up)[0], np.asarray(iclr_up)[0]], 0)
    arrays["in_x"] = np.ascontiguousarray(np.asarray(x)[0])
    arrays["in_const"] = constants()
    by_channel = lambda a: np.asarray(a).reshape(-1, P).T
    mu = np.asarray(shift_mu)[0]
    cols = {"mu_r": mu[0:W], "mu_k": mu[W:2 * W], "mu_v": mu[2 * W:3 * W], "mu_w": mu[3 * W:],
            "decay_bias": decay_bias, "iclr_bias": iclr_bias, "k_k": k_k, "k_a": k_a, "r_k": r_k,
            "gn_gain": gn_gain, "gn_bias": gn_bias, "norm_gain": norm_gain}
    arrays["in_param"] = np.ascontiguousarray(np.concatenate([by_channel(cols[n]) for n in PARAM], 1))
    arrays["in_fg"] = np.ascontiguousarray(np.asarray(final_gain))

    nc = bacc.Bacc("TRN2", target_bir_lowering=False, num_devices=1)
    f32 = mybir.dt.float32
    ap = {n: nc.dram_tensor(n, a.shape, f32, kind="ExternalInput").ap() for n, a in arrays.items()}
    a_scratch = nc.dram_tensor("a_scratch", (P, UNITS, C), f32, kind="Internal").ap()
    t_scratch = nc.dram_tensor("t_scratch", (P, 2, BASE * BASE), f32, kind="Internal").ap()
    out = nc.dram_tensor("out", (SEQ, D_MODEL), f32, kind="ExternalOutput").ap()
    hybrid_layer(nc, ap["in_x"], {n: ap["in_" + n] for n in BLOCKS}, ap["in_wd"], ap["in_up"], ap["in_const"],
                 ap["in_param"], ap["in_fg"], a_scratch, t_scratch, out)
    r = run(nc, [arrays], core_ids=[0])
    return r.results[0]["out"].reshape(1, SEQ, D_MODEL)
```

```python
import concourse.bass as bass
from concourse import mybir
from contextlib import ExitStack
import numpy as np

D_MODEL, SEQ, HEAD, HEADS = 1024, 256, 64, 8
WIDTH = HEAD * HEADS
P = 128
PAIRS = WIDTH // P
KC = D_MODEL // P
TT = SEQ // P
C = 64
CHUNKS = SEQ // C
UNITS = CHUNKS * PAIRS
BASE = 16
DECAY = 0.5 * float(np.exp(-0.5))

CONST = {}
_at = 0
for _name, _n in (("ident", P), ("head_mean", P), ("head_sum", P), ("gram_mask", P), ("a_mask", C),
                  ("low16", C), ("low32", C), ("scan", SEQ), ("causal", 3 * P), ("cos", TT * HEAD),
                  ("sin", TT * HEAD), ("block_eye", BASE * BASE)):
    CONST[_name] = (_at, _at + _n)
    _at += _n
N_CONST = _at
PARAM = {}
_at = 0
for _name, _n in (("mu_r", PAIRS), ("mu_k", PAIRS), ("mu_v", PAIRS), ("mu_w", 1), ("decay_bias", PAIRS),
                  ("iclr_bias", PAIRS), ("k_k", PAIRS), ("k_a", PAIRS), ("r_k", PAIRS),
                  ("gn_gain", PAIRS), ("gn_bias", PAIRS), ("norm_gain", KC)):
    PARAM[_name] = (_at, _at + _n)
    _at += _n
N_PARAM = _at

BLOCKS = ["wd", "k", "r", "v", "aq", "ak", "av", "ga", "gb", "wo"]
PIECES = [("wd", 0)] + [(b, q) for b in BLOCKS[1:-1] for q in range(4)] + \
         [("wo", 2 * q + n) for q in range(4) for n in range(2)]
RAW_SLOTS, SLOTS, LEAD = 4, 5, 4
WARM_UP = 8

PROJ_BANKS, AUX_BANKS = (0, 1, 2, 3), (4, 5, 6, 7)
PROJ = ("wd", "k", "r", "v", "aq", "ak", "av", "ga", "gb", "out")


def order():
    w = lambda b, *qs: [("w", b, q) for q in qs]
    o = [("xT", j) for j in range(4)]
    o += w("wd", 0) + [("take", "wd")] + w("k", 0, 1)
    o += [("upw", 0), ("upa", 0), ("upw", 1), ("upa", 1), ("decay",)] + w("k", 2, 3) + [("take", "k")]
    o += w("r", 0) + [("sq",)] + w("r", 1) + [("kn", 0), ("kn", 1), ("kk",)] + w("r", 2, 3) + [("take", "r")]
    o += w("v", 0, 1, 2, 3) + [("A", 0), ("A", 1), ("gather",), ("clear",), ("masks",), ("rk",), ("take", "v")]
    o += w("aq", 0) + [("bonus", 0), ("bonus", 1)] + w("aq", 1) + [("vT", 0), ("bT", 0), ("inv", 1, 8)]
    o += w("aq", 2) + [("inv", 8, 12), ("gram", 0, 0), ("gram", 0, 1)] + w("aq", 3) + [("inv", 12, 16), ("take", "aq")]
    o += w("ak", 0, 1) + [("qT", 0), ("qT", 1)] + w("ak", 2, 3) + [("take", "ak")]
    o += [("Y1", 0), ("Y1", 1)] + w("av", 0) + [("kT", 0), ("kT", 1), ("T1", 0), ("U1", 0), ("T1", 1), ("U1", 1)]
    o += w("av", 1) + [("S", 0), ("S", 1), ("Y2", 0), ("Y2", 1)] + w("av", 2) + [("U2", 0), ("U2", 1)]
    o += w("av", 3) + [("take", "av"), ("norm", 0), ("norm", 1)]
    chain = [[("R", 0)], [("SA", 0, 0), ("SA", 0, 1)]]
    for c in range(CHUNKS):
        if c < CHUNKS - 1:
            chain += [[("St", c), ("vT", c + 1), ("bT", c + 1)], [("gram", c + 1, 0), ("gram", c + 1, 1), ("Yc", c)],
                      [("R", c + 1)], [("SA", c + 1, 0), ("SA", c + 1, 1)]]
    att = []
    for p in range(PAIRS):
        att += [[("PT", 2 * p), ("PT", 2 * p + 1)]]
        if p < PAIRS - 1:
            att += [[("S", 2 * p + 2), ("S", 2 * p + 3)]]
        att += [[("PV", p)]]
        if p < PAIRS - 1:
            att += [[("norm", 2 * p + 2), ("norm", 2 * p + 3)]]
    gates = w("ga", 0, 1, 2, 3) + [("take", "ga")] + w("gb", 0, 1, 2, 3) + [("take", "gb")]
    while chain or att or gates:
        for l, n in ((chain, 1), (gates, 1)):
            for _ in range(n):
                if l:
                    x = l.pop(0)
                    o += x if isinstance(x, list) else [x]
        if ("take", "ga") in o and att:
            o += att.pop(0)
    o += [("Yc", CHUNKS - 1), ("mean", 0), ("var", 0), ("gn", 0), ("mean", 1), ("var", 1), ("gn", 1)]
    for q in range(4):
        o += w("wo", 2 * q, 2 * q + 1)
    return o + [("take", "out")]


ORDER = order()
LAST_PIECE = {b: max(q for b2, q in PIECES if b2 == b) for b in BLOCKS}


def piece_number(item):
    return PIECES.index(item[1:])


def place_jobs():
    turn, used, place = {"proj": 0, "aux": 0}, [0] * 8, {}

    def put(name, kind):
        banks = PROJ_BANKS if kind == "proj" else AUX_BANKS
        b = banks[turn[kind] % len(banks)]
        turn[kind] += 1
        place[name] = (b, used[b])
        used[b] += 1

    for item in ORDER:
        if item[0] == "w":
            if item[2] == 0:
                for j in range(1 if item[1] == "wd" else 4 if item[1] == "wo" else 2):
                    put(("out", j // 2, j % 2) if item[1] == "wo" else (item[1], j), "proj")
        elif item[0] not in ("take", "decay", "kk", "rk", "inv", "norm", "gn", "gather", "sq", "clear", "masks"):
            put(item, "aux")
    return place


def hybrid_layer(nc, x, w_blocks, up, const, param, final_gain, a_scratch, t_scratch, out):
    f32, f32r = mybir.dt.float32, mybir.dt.float32r
    ALU = mybir.AluOpType
    ACT = mybir.ActivationFunctionType
    AX = mybir.AxisListType
    PLACE = place_jobs()
    ctx = ExitStack()
    with ctx:
        def sb(name, shape, dt=f32, scope=ctx):
            return scope.enter_context(nc.sbuf_tensor(name, shape, dt))

        def sem(name):
            return ctx.enter_context(nc.semaphore(name))

        banks = [ctx.enter_context(nc.psum_tensor(f"bank{b}", [P, 512], f32)) for b in range(8)]

        cst = sb("cst", [P, N_CONST])
        prm = sb("prm", [P, N_PARAM])
        drv = sb("drv", [P, 6, PAIRS])
        w_raw = [sb(f"w_raw{s}", [P, 2, 512]) for s in range(RAW_SLOTS)]
        w_hi = [sb(f"w_hi{s}", [P, 2, 512], f32r) for s in range(SLOTS)]
        w_lo = [sb(f"w_lo{s}", [P, 2, 512], f32r) for s in range(SLOTS)]
        up_sb = sb("up_sb", [P, WIDTH])
        u_hi = sb("u_hi", [P, KC, SEQ], f32r)
        u_lo = sb("u_lo", [P, KC, SEQ], f32r)
        stat = sb("stat", [P, 4 * TT])
        pad_a = sb("pad_a", [P, PAIRS, SEQ + 1])
        pad_b = sb("pad_b", [P, PAIRS, SEQ + 1])
        pad_w = sb("pad_w", [P, SEQ + 1])
        wd = sb("wd", [P, SEQ])
        dif = sb("dif", [P, PAIRS, SEQ])
        k1 = sb("k1", [P, PAIRS, SEQ])
        r1 = sb("r1", [P, PAIRS, SEQ])
        v1 = sb("v1", [P, PAIRS, C + SEQ])
        with ExitStack() as early:
            kk = sb("kk", [P, PAIRS, SEQ], scope=early)
            rn = sb("rn", [P, PAIRS, SEQ], scope=early)
            thw = sb("thw", [P, PAIRS, SEQ], scope=early)
            cs = sb("cs", [P, PAIRS, SEQ], scope=early)
        y_hi = sb("y_hi", [P, 2 * PAIRS, SEQ], f32r)
        y_lo = sb("y_lo", [P, 2 * PAIRS, SEQ], f32r)
        with ExitStack() as early:
            xt = sb("xt", [P, TT, D_MODEL], scope=early)
        lr = sb("lr", [P, 2, HEADS, P])
        tha = sb("tha", [P, PAIRS, SEQ])
        kp = sb("kp", [P, PAIRS, SEQ])
        pinc = sb("pinc", [P, UNITS, C + 1])
        bk = sb("bk", [P, UNITS, 2, C])
        kr = sb("kr", [P, UNITS, 2, C])
        head_rk = sb("head_rk", [P, PAIRS, P])
        y_sb = sb("y_sb", [P, UNITS, C])
        blk = sb("blk", [P, 4, BASE * BASE])
        bkt = sb("bkt", [P, 2, HEADS, C])
        sav = sb("sav", [P, 2, HEADS, C])
        state = sb("state", [P, 2, PAIRS, C])
        r_neg = sb("r_neg", [P, PAIRS, C])
        yc = sb("yc", [P, PAIRS, SEQ])
        gn_r = sb("gn_r", [P, 2, PAIRS, P])
        ya = sb("ya", [P, 2, SEQ])
        g_b = sb("g_b", [P, PAIRS, SEQ])
        qT = sb("qT", [P, PAIRS, SEQ])
        kT = sb("kT", [P, PAIRS, SEQ])
        amax = sb("amax", [P, HEADS, 3, TT])
        diag = y_sb[:, :, :].rearrange("p u c -> p (u c)")[:, 0:TT * P].rearrange("p (t n) -> p t n", t=TT)
        a_neg = kk[:, :, :].rearrange("p a (b c) -> p (a b) c", c=C)
        b16 = rn[:, :, :].rearrange("p a (b c) -> p (a b) c", c=C)
        b32 = thw[:, :, :].rearrange("p a (b c) -> p (a b) c", c=C)
        t_inv = cs[:, :, :].rearrange("p a (b c) -> p (a b) c", c=C)
        u_inv = tha[:, :, :].rearrange("p a (b c) -> p (a b) c", c=C)
        rot = r1[:, :, :].rearrange("p a b -> p (a b)").rearrange("p (t n) -> p t n", t=TT)
        v_att = kp[:, :, :].rearrange("p a b -> p (a b)").rearrange("p (t n) -> p t n", t=TT)
        rot_k = pad_b[:, :, :].rearrange("p a b -> p (a b)")[:, 0:TT * WIDTH].rearrange("p (t n) -> p t n", t=TT)
        g_a = r1
        x_res = kr[:, :, :, :].rearrange("p u s c -> p (u s c)").rearrange("p (t n) -> p t n", t=TT)
        fgain = bk[:, 0:8, :, :].rearrange("p u s c -> p (u s c)")
        pad_a_flat = pad_a[:, :, :].rearrange("p a b -> p (a b)")
        rtmp = dif[:, :, :].rearrange("p a b -> p (a b)")
        bonus = k1
        pr = rtmp[:, 0:6 * P].rearrange("p (b n) -> p b n", b=2)
        prT = pad_a_flat[:, 0:6 * P].rearrange("p (b n) -> p b n", b=2)

        def cn(name):
            a, b = CONST[name]
            return cst[:, a:b]

        def pm(name, i=0):
            a, _ = PARAM[name]
            return prm[:, a + i:a + i + 1]

        def pm_all(name):
            a, b = PARAM[name]
            return prm[:, a:b]

        HALF_DB, HALF_IB, HALF_KA, ONE_KA, HALF_GAIN = range(5)

        s_const = sem("s_const")
        s_x = [sem(f"s_x{t}") for t in range(TT)]
        s_ident = sem("s_ident")
        s_raw = [sem(f"s_raw{s}") for s in range(RAW_SLOTS)]
        s_res = sem("s_res")
        hi_done = sem("hi_done")
        lo_done = sem("lo_done")
        w_used = sem("w_used")
        ya_hi = sem("ya_hi")
        ya_lo = sem("ya_lo")
        y_done = sem("y_done")
        yb_hi = sem("yb_hi")
        s_up = sem("s_up")
        s_fg = sem("s_fg")
        s_out = sem("s_out")
        s_gather = sem("s_gather")
        s_scatter = sem("s_scatter")
        s_a_out = sem("s_a_out")
        s_t_out = sem("s_t_out")
        filled = [sem(f"filled{b}") for b in range(8)]
        emptied = [sem(f"emptied{b}") for b in range(8)]
        warm_zero = sem("warm_zero")
        zeroed = sem("zeroed")
        drv_done = sem("drv_done")
        ss_done = sem("ss_done")
        ss1_done = sem("ss1_done")
        u_hi_done = sem("u_hi_done")
        ms_done = sem("ms_done")
        sq_done = sem("sq_done")
        rstd_done = sem("rstd_done")
        diag_done = sem("diag_done")
        dif_done = sem("dif_done")
        k1_done = sem("k1_done")
        wd_done = sem("wd_done")
        wd_tanh = sem("wd_tanh")
        r1_done = sem("r1_done")
        v1_done = sem("v1_done")
        kk_raw = sem("kk_raw")
        kk_sq = sem("kk_sq")
        kk_root = sem("kk_root")
        kk_inv = sem("kk_inv")
        kk_done = sem("kk_done")
        thw1_done = sem("thw1_done")
        cs_done = sem("cs_done")
        pinc_done = sem("pinc_done")
        pinv_done = sem("pinv_done")
        kgain_done = sem("kgain_done")
        kp_done = sem("kp_done")
        a_done = sem("a_done")
        b_done = sem("b_done")
        bk_done = sem("bk_done")
        kr_done = sem("kr_done")
        rk_prod = sem("rk_prod")
        head_rk_done = sem("head_rk_done")
        bonus_done = sem("bonus_done")
        low_done = sem("low_done")
        inv_step = sem("inv_step")
        inv_done = sem("inv_done")
        tu_zero = sem("tu_zero")
        st_done = sem("st_done")
        csq_done = sem("csq_done")
        groot = sem("groot")
        ginv = sem("ginv")
        gn_step = sem("gn_step")
        yb_lo = sem("yb_lo")
        gth = sem("gth")
        gb_done = sem("gb_done")
        rot_done = sem("rot_done")
        nmax = sem("nmax")
        exp_done = sem("exp_done")
        rsum_done = sem("rsum_done")
        pr_done = sem("pr_done")
        fs_done = sem("fs_done")
        fm_done = sem("fm_done")
        fr_done = sem("fr_done")
        fi_done = sem("fi_done")
        o_done = sem("o_done")

        def free_bank(eng, job):
            b, turn = PLACE[job]
            if turn:
                eng.wait_ge(emptied[b], turn)
            return banks[b]

        def fill(ins, job):
            ins.then_inc(filled[PLACE[job][0]], 1)

        def full_bank(eng, job):
            b, turn = PLACE[job]
            eng.wait_ge(filled[b], turn + 1)
            return banks[b]

        def taken(eng, *job):
            b, turn = PLACE[job]
            eng.wait_ge(emptied[b], turn + 1)

        def empty(ins, job):
            ins.then_inc(emptied[PLACE[job][0]], 1)

        def piece_used(eng, n):
            b, q = PIECES[n]
            if q == LAST_PIECE[b]:
                at, turn = PLACE[(b, 0 if b == "wd" else 1)]
                eng.wait_ge(filled[at], turn + 1)
            else:
                eng.wait_ge(w_used, sum(q2 != LAST_PIECE[b2] for b2, q2 in PIECES[:n + 1]))

        def state_ready(eng, c):
            if c == 0:
                taken(eng, "St", 0)
            else:
                eng.wait_ge(st_done, c)

        block = ctx.enter_context(nc.Block())

        @block.sync
        def _(sp):
            sp.dma_start(xt[:, 0, :], x[0:P, :]).then_inc(s_x[0], 16)
            sp.dma_start(xt[:, 1, :], x[P:SEQ, :]).then_inc(s_x[1], 16)
            sp.dma_start(cst[:, 0:P], const[:, 0:P]).then_inc(s_ident, 16)
            sp.dma_start(prm[:, :], param).then_inc(s_ident, 16)

            def load(n):
                b, q = PIECES[n]
                if n >= RAW_SLOTS:
                    sp.wait_ge(lo_done, n - RAW_SLOTS + 1)
                dst = w_raw[n % RAW_SLOTS]
                if b == "wd":
                    sp.dma_start(dst[:, :, :].rearrange("p k n -> p (k n)"), w_blocks[b]).then_inc(s_raw[n % RAW_SLOTS], 16)
                elif b == "wo":
                    sp.dma_start(dst[:, :, :], w_blocks[b][:, q % 2, q // 2 * 2:q // 2 * 2 + 2, :]).then_inc(s_raw[n % RAW_SLOTS], 16)
                else:
                    sp.dma_start(dst[:, :, :], w_blocks[b][:, 2 * q:2 * q + 2, :]).then_inc(s_raw[n % RAW_SLOTS], 16)

            for n in range(RAW_SLOTS):
                load(n)
            sp.dma_start(cst[:, P:N_CONST], const[:, P:N_CONST]).then_inc(s_const, 16)
            sp.dma_start(up_sb[:, :], up).then_inc(s_up, 16)
            for item in ORDER:
                if item[0] == "w" and piece_number(item) + RAW_SLOTS < len(PIECES):
                    load(piece_number(item) + RAW_SLOTS)
                elif item[0] == "gather":
                    taken(sp, "A", 0)
                    taken(sp, "A", 1)
                    sp.dma_start(a_scratch, a_neg).then_inc(s_a_out, 16)
                    sp.wait_ge(s_a_out, 16)
                    for par in range(2):
                        for b in range(C // BASE):
                            u0, row, col = (par * 4 + b) * UNITS, 64 * par + BASE * b, BASE * b
                            sp.dma_start(blk[u0:u0 + UNITS, 0, :].rearrange("u (i j) -> u i j", i=BASE),
                                         a_scratch[row:row + BASE, :, col:col + BASE].rearrange("i u j -> u i j")
                                         ).then_inc(s_gather, 16)
                elif item[0] == "inv" and item[2] == BASE:
                    sp.wait_ge(inv_done, 1)
                    sp.dma_start(t_scratch, blk[:, 1:3, :]).then_inc(s_t_out, 16)
                    sp.wait_ge(tu_zero, 2)
                    sp.wait_ge(s_t_out, 16)
                    for dst, src in ((t_inv, 0), (u_inv, 1)):
                        for par in range(2):
                            for b in range(C // BASE):
                                u0, row, col = (par * 4 + b) * UNITS, 64 * par + BASE * b, BASE * b
                                sp.dma_start(dst[row:row + BASE, :, col:col + BASE],
                                             t_scratch[u0:u0 + UNITS, src, :].rearrange("u (i j) -> i u j", i=BASE)
                                             ).then_inc(s_scatter, 16)
            b, turn = PLACE[("Yc", CHUNKS - 1)]
            sp.wait_ge(filled[b], turn + 1)
            sp.dma_start(x_res, x.rearrange("(t p) n -> p t n", t=TT)).then_inc(s_res, 16)
            sp.dma_start(fgain, final_gain.partition_broadcast(P)).then_inc(s_fg, 16)
            for t in range(TT):
                sp.wait_ge(o_done, t + 1)
                sp.dma_start(out[t * P:(t + 1) * P, :], x_res[:, t, :]).then_inc(s_out, 16)
            sp.wait_ge(s_out, 16 * TT)

        @block.gpsimd
        def _(pool):
            nc.gpsimd.memset(r1[:, 0, :], 0.0).then_inc(warm_zero, 1)
            nc.gpsimd.memset(pad_w[:, 0:1], 0.0).then_inc(zeroed, 1)
            nc.gpsimd.memset(pad_a[:, :, 0:1], 0.0).then_inc(zeroed, 1)
            nc.gpsimd.memset(pad_b[:, :, 0:1], 0.0).then_inc(zeroed, 1)
            nc.gpsimd.memset(v1[:, :, 0:C], 0.0).then_inc(zeroed, 1)
            nc.gpsimd.memset(pinc[:, :, 0:1], 1.0).then_inc(zeroed, 1)
            nc.gpsimd.memset(sav[0:C, :, :, :], 0.0).then_inc(zeroed, 1)
            def split_lo(n):
                pool.wait_ge(hi_done, n + 1)
                nc.gpsimd.tensor_tensor(w_lo[n % SLOTS][:, :, :], w_raw[n % RAW_SLOTS][:, :, :],
                                        w_hi[n % SLOTS][:, :, :].bitcast(f32), ALU.subtract).then_inc(lo_done, 1)

            for n in range(LEAD):
                split_lo(n)
            for item in ORDER:
                if item[0] == "w" and piece_number(item) + LEAD < len(PIECES):
                    split_lo(piece_number(item) + LEAD)
                elif item[0] == "clear":
                    pool.wait_ge(bk_done, 2)
                    nc.gpsimd.memset(t_inv, 0.0).then_inc(tu_zero, 1)
                    nc.gpsimd.memset(u_inv, 0.0).then_inc(tu_zero, 1)
                elif item[0] == "masks":
                    taken(pool, "A", 0)
                    taken(pool, "A", 1)
                    for m, dst in (("low16", b16), ("low32", b32)):
                        nc.gpsimd.tensor_tensor(dst, a_neg, cn(m).unsqueeze(1).to_broadcast([P, UNITS, C]),
                                                ALU.mult).then_inc(low_done, 1)

        @block.scalar
        def _(act):
            A = nc.scalar.activation

            def split_hi(n):
                act.wait_ge(s_raw[n % RAW_SLOTS], 16 * (n // RAW_SLOTS + 1))
                if n >= SLOTS:
                    piece_used(act, n - SLOTS)
                A(w_hi[n % SLOTS][:, :, :], w_raw[n % RAW_SLOTS][:, :, :], ACT.Copy).then_inc(hi_done, 1)

            def halves(bank):
                return bank[:, :].rearrange("p (a b) -> p a b", a=2)

            def copy_out(job, dst, src, **kw):
                bank = full_bank(act, job)
                empty(A(dst, src(bank), ACT.Copy, **kw), job)

            def pairs_v(bank):
                return bank[:, 0:PAIRS * C].rearrange("p (a v) -> p a v", a=PAIRS)

            act.wait_ge(s_x[0], 16)
            A(k1[:, :, :].rearrange("p a b -> p (a b)"), xt[:, 0, :], ACT.Square, accum_out=stat[:, 0:1]).then_inc(ss_done, 1)
            for t in range(TT):
                act.wait_ge(ms_done, t + 1)
                A(stat[:, 4 + t:5 + t], stat[:, 2 + t:3 + t], ACT.Sqrt).then_inc(sq_done, 1)
            split_hi(0)
            split_hi(1)
            act.wait_ge(s_ident, 32)

            def act_part(item):
                kind, a = item[0], item[1:]
                if kind == "xT":
                    bank = full_bank(act, item)
                    for i in range(2):
                        k = 2 * a[0] + i
                        ins = A(u_hi[:, k, :], bank[:, i * SEQ:(i + 1) * SEQ], ACT.Copy, scale=pm("norm_gain", k))
                    ins.then_inc(u_hi_done, 1)
                    if a[0] in (1, 3):
                        split_hi(2 + a[0] // 2)
                elif kind == "w":
                    if piece_number(item) + LEAD < len(PIECES):
                        split_hi(piece_number(item) + LEAD)
                elif item == ("take", "wd"):
                    act.wait_ge(zeroed, 6)
                    copy_out(("wd", 0), pad_w[:, 1:SEQ + 1], lambda b: b[:, 0:SEQ])
                    act.wait_ge(wd_done, 1)
                    A(wd[0:64, :], wd[0:64, :], ACT.Tanh).then_inc(wd_tanh, 1)
                elif kind == "take" and a[0] in ("k", "r", "v"):
                    pad = pad_b if a[0] == "r" else pad_a
                    if a[0] == "v":
                        act.wait_ge(k1_done, PAIRS)
                    for j in range(2):
                        copy_out((a[0], j), pad[:, 2 * j:2 * j + 2, 1:SEQ + 1], halves)
                elif kind in ("upw", "upa"):
                    act.wait_ge(drv_done, 5)
                    bank = full_bank(act, item)
                    for i in range(2):
                        p = 2 * a[0] + i
                        dst, bias = (thw, HALF_DB) if kind == "upw" else (tha, HALF_IB)
                        ins = A(dst[:, p, :], bank[:, i * SEQ:(i + 1) * SEQ], ACT.Tanh, scale=0.5, bias=drv[:, bias, p:p + 1])
                    empty(ins, item)
                elif kind == "decay":
                    act.wait_ge(cs_done, PAIRS)
                    cs_u = cs[:, :, :].rearrange("p a (b c) -> p (a b) c", c=C)
                    A(pinc[:, :, 1:C + 1], cs_u, ACT.Exp, scale=-DECAY).then_inc(pinc_done, 1)
                    A(cs_u, cs_u, ACT.Exp, scale=DECAY).then_inc(pinv_done, 1)
                elif kind == "sq":
                    for p in range(PAIRS):
                        act.wait_ge(k1_done, p + 1)
                        A(rn[:, p, :], k1[:, p, :], ACT.Square, scale=pm("k_k", p)).then_inc(kk_sq, 1)
                elif kind == "kk":
                    taken(act, "kn", 0)
                    taken(act, "kn", 1)
                    A(rn[:, :, :], rn[:, :, :], ACT.Sqrt).then_inc(kk_root, 1)
                elif kind in ("qT", "kT"):
                    copy_out(item, (qT if kind == "qT" else kT)[:, 2 * a[0]:2 * a[0] + 2, :], halves)
                elif item == ("take", "av"):
                    act.wait_ge(rk_prod, 1)
                    for t in range(TT):
                        copy_out(("av", t), v_att[:, t, :], lambda b: b[:, :])
                elif kind == "vT":
                    if a[0] >= 2:
                        taken(act, "Yc", a[0] - 2)
                        taken(act, "St", a[0] - 2)
                    copy_out(item, sav[C:P, a[0] % 2, :, :], lambda b: b[C:P, :].rearrange("p (h v) -> p h v", h=HEADS))
                elif kind == "bT":
                    copy_out(item, bkt[:, a[0] % 2, :, :], lambda b: b[:, :].rearrange("p (h v) -> p h v", h=HEADS))
                elif kind == "S":
                    h = a[0]
                    act.wait_ge(nmax, h + 1)
                    for t in range(TT):
                        lo, hi = (0, P) if t == 0 else (P, 3 * P)
                        A(pr[:, h % 2, lo:hi], pr[:, h % 2, lo:hi], ACT.Exp, scale=HEAD ** -0.5,
                          bias=amax[:, h, 1, t:t + 1], accum_out=amax[:, h, 2, t:t + 1]).then_inc(exp_done, 1)
                elif kind == "PT":
                    act.wait_ge(v1_done, PAIRS)
                    if a[0] >= 2:
                        taken(act, "PV", (a[0] - 2) // 2)
                    copy_out(item, prT[:, a[0] % 2, :], lambda b: b[:, 0:3 * P])
                elif kind == "PV":
                    taken(act, "PV", a[0])
                    taken(act, "U2", 1)
                    A(y_hi[:, a[0], :], ya[:, a[0] % 2, :], ACT.Copy).then_inc(ya_hi, 1)
                elif kind in ("Y1", "Y2"):
                    if kind == "Y2":
                        taken(act, "U1", a[0])
                    copy_out(item, y_sb[:, 8 * a[0]:8 * a[0] + 8, :], lambda b: b[:, :].rearrange("p (u c) -> p u c", c=C))
                elif item in (("take", "ga"), ("take", "gb")):
                    dst = g_a if a[0] == "ga" else g_b
                    if a[0] == "ga":
                        taken(act, "qT", 1)
                    for j in range(2):
                        bank = full_bank(act, (a[0], j))
                        A(dst[:, 2 * j:2 * j + 2, :], halves(bank), ACT.Tanh, scale=0.5).then_inc(gth, 1)
                elif kind == "R":
                    if a[0]:
                        taken(act, "SA", a[0] - 1, 1)
                    copy_out(item, r_neg[:, :, :], pairs_v, scale=-1.0)
                elif kind == "Yc":
                    copy_out(item, yc[:, :, a[0] * C:(a[0] + 1) * C], pairs_v)
                elif kind == "mean":
                    taken(act, "mean", a[0])
                    A(gn_r[:, a[0], :, :], yc[:, :, a[0] * P:(a[0] + 1) * P], ACT.Square).then_inc(csq_done, 1)
                elif kind == "var":
                    taken(act, "var", a[0])
                    A(gn_r[:, a[0], :, :], gn_r[:, a[0], :, :], ACT.Sqrt).then_inc(groot, 1)
                elif kind == "gn":
                    tok = slice(a[0] * P, (a[0] + 1) * P)
                    act.wait_ge(y_done, a[0] + 1)
                    A(y_hi[:, PAIRS:2 * PAIRS, tok], yc[:, :, tok], ACT.Copy).then_inc(yb_hi, 1)
                elif item == ("take", "out"):
                    for t in range(TT):
                        taken(act, "out", t, 0)
                        taken(act, "out", t, 1)
                        A(lr[:, t, :, :].rearrange("p h n -> p (h n)"), x_res[:, t, :], ACT.Square,
                          accum_out=stat[:, t:t + 1]).then_inc(fs_done, 1)
                        act.wait_ge(fm_done, t + 1)
                        A(stat[:, 4 + t:5 + t], stat[:, 2 + t:3 + t], ACT.Sqrt).then_inc(fr_done, 1)

            for item in ORDER:
                act_part(item)

        @block.vector
        def _(dve):
            V = nc.vector

            def halves(bank):
                return bank[:, :].rearrange("p (a b) -> p a b", a=2)

            def pairs_v(bank):
                return bank[:, 0:PAIRS * C].rearrange("p (a v) -> p a v", a=PAIRS)

            def tiles_v(bank):
                return bank[:, :].rearrange("p (a v) -> p a v", a=PAIRS)

            dve.wait_ge(s_x[1], 16)
            V.tensor_tensor_reduce(out=cs[:, :, :].rearrange("p a b -> p (a b)"), in0=xt[:, 1, :], in1=xt[:, 1, :],
                                   scale=1.0, scalar=0.0, op0=ALU.mult, op1=ALU.add, accum_out=stat[:, 1:2]).then_inc(ss1_done, 1)
            for t in range(TT):
                dve.wait_ge(*((ss_done, 1), (ss1_done, 1))[t])
                V.tensor_scalar(stat[:, 2 + t:3 + t], stat[:, t:t + 1], 1.0 / D_MODEL, 1e-6, ALU.mult, ALU.add).then_inc(ms_done, 1)
            dve.wait_ge(s_ident, 32)
            for t in range(TT):
                dve.wait_ge(sq_done, t + 1)
                V.reciprocal(stat[:, 6 + t:7 + t], stat[:, 4 + t:5 + t]).then_inc(rstd_done, 1)
                dve.wait_ge(rstd_done, t + 1)
                V.tensor_scalar(diag[:, t, :], cn("ident"), stat[:, 6 + t:7 + t], None, ALU.mult).then_inc(diag_done, 1)
            for i, (name, s, o) in enumerate((("decay_bias", 0.5, 0.0), ("iclr_bias", 0.5, 0.0), ("k_a", 0.5, 0.0),
                                              ("k_a", -0.5, 1.0), ("gn_gain", 0.5, 0.0))):
                V.tensor_scalar(drv[:, i, :], pm_all(name), s, o, ALU.mult, ALU.add).then_inc(drv_done, 1)
            def shift(pad, mu, dst, off, kind, n_dif, done, after=None):
                taken(dve, kind, 0)
                taken(dve, kind, 1)
                dve.wait_ge(*after)
                V.tensor_tensor(dif[:, :, :], pad[:, :, 0:SEQ], pad[:, :, 1:SEQ + 1], ALU.subtract).then_inc(dif_done, 1)
                dve.wait_ge(dif_done, n_dif)
                for p in range(PAIRS):
                    V.scalar_tensor_tensor(dst[:, p, off:off + SEQ], dif[:, p, :], pm(mu, p), pad[:, p, 1:SEQ + 1],
                                           ALU.mult, ALU.add).then_inc(done, 1)

            def units(t):
                return t[:, :, :].rearrange("p a (b c) -> p (a b) c", c=C)

            def rotate(kind, t, dst, n):
                bank = full_bank(dve, (kind, t))
                v = bank[:, :].rearrange("p (h d) -> p h d", d=HEAD)
                cos = cn("cos")[:, t * HEAD:(t + 1) * HEAD].unsqueeze(1).to_broadcast([P, HEADS, HEAD])
                sin = cn("sin")[:, t * HEAD:(t + 1) * HEAD].unsqueeze(1).to_broadcast([P, HEADS, HEAD])
                o = dst[:, t, :].rearrange("p (h d) -> p h d", d=HEAD)
                tmp = rtmp[:, (n % 2) * WIDTH:(n % 2 + 1) * WIDTH].rearrange("p (h d) -> p h d", d=HEAD)
                H2 = HEAD // 2
                if n >= 2:
                    dve.wait_ge(rot_done, n - 1)
                V.tensor_tensor(o, v, cos, ALU.mult)
                V.tensor_tensor(tmp[:, :, 0:H2], v[:, :, H2:HEAD], sin[:, :, 0:H2], ALU.mult)
                empty(V.tensor_tensor(tmp[:, :, H2:HEAD], v[:, :, 0:H2], sin[:, :, H2:HEAD], ALU.mult), (kind, t))
                taken(dve, kind, t)
                V.tensor_tensor(o, o, tmp, ALU.add).then_inc(rot_done, 1)

            T_in = blk[:, 1, :].rearrange("p (i j) -> p i j", i=BASE)
            T_tr = blk[:, 1, :].rearrange("p (i j) -> p j i", i=BASE)

            def invert(first, last):
                neg = blk[:, 0, :].rearrange("p (i j) -> p i j", i=BASE)
                prod = blk[:, 3, :].rearrange("p (i j) -> p i j", i=BASE)
                if first == 1:
                    V.tensor_copy(blk[:, 1, :], cn("block_eye")).then_inc(inv_step, 1)
                    dve.wait_ge(s_gather, 16 * 8)
                for i in range(first, last):
                    dve.wait_ge(inv_step, 2 * i - 1)
                    V.tensor_tensor(prod[:, 0:i, 0:i], T_tr[:, 0:i, 0:i], neg[:, i:i + 1, 0:i].to_broadcast([P, i, i]),
                                    ALU.mult).then_inc(inv_step, 1)
                    dve.wait_ge(inv_step, 2 * i)
                    V.tensor_reduce(T_in[:, i, 0:i], prod[:, 0:i, 0:i], AX.X, ALU.add).then_inc(inv_step, 1)
                if last == BASE:
                    dve.wait_ge(inv_step, 2 * BASE - 1)
                    V.tensor_copy(blk[:, 2, :].rearrange("p (i j) -> p i j", i=BASE), T_tr).then_inc(inv_done, 1)

            def dve_part(item):
                kind, a = item[0], item[1:]
                if kind == "xT":
                    dve.wait_ge(u_hi_done, a[0] + 1)
                    bank = banks[PLACE[item][0]]
                    for i in range(2):
                        k = 2 * a[0] + i
                        ins = V.scalar_tensor_tensor(u_lo[:, k, :], bank[:, i * SEQ:(i + 1) * SEQ], pm("norm_gain", k),
                                                     u_hi[:, k, :].bitcast(f32), ALU.mult, ALU.subtract)
                    empty(ins, item)
                elif item == ("take", "wd"):
                    taken(dve, "wd", 0)
                    V.tensor_tensor(dif[:, 0, :], pad_w[:, 0:SEQ], pad_w[:, 1:SEQ + 1], ALU.subtract).then_inc(dif_done, 1)
                    dve.wait_ge(dif_done, 1)
                    V.scalar_tensor_tensor(wd[:, :], dif[:, 0, :], pm("mu_w"), pad_w[:, 1:SEQ + 1], ALU.mult, ALU.add).then_inc(wd_done, 1)
                    dve.wait_ge(s_const, 16)
                    for p in range(PAIRS):
                        V.tensor_scalar(head_rk[:, p, :], cn("head_sum"), pm("r_k", p), None, ALU.mult).then_inc(head_rk_done, 1)
                elif kind == "decay":
                    for p in range(PAIRS):
                        taken(dve, "upw", p // 2)
                        V.tensor_scalar(thw[:, p, :], thw[:, p, :], 1.0, None, ALU.add).then_inc(thw1_done, 1)
                    for p in range(PAIRS):
                        dve.wait_ge(thw1_done, p + 1)
                        V.tensor_tensor_scan(cs[:, p, :], cn("scan"), thw[:, p, :], 0.0, ALU.mult, ALU.add).then_inc(cs_done, 1)
                    for p in range(PAIRS):
                        taken(dve, "upa", p // 2)
                        V.tensor_scalar(kp[:, p, :], tha[:, p, :], drv[:, HALF_KA, p:p + 1], drv[:, ONE_KA, p:p + 1],
                                        ALU.mult, ALU.add).then_inc(kgain_done, 1)
                    dve.wait_ge(kgain_done, PAIRS)
                    V.tensor_scalar(tha[:, :, :], tha[:, :, :], 0.5, 0.5, ALU.mult, ALU.add).then_inc(a_done, 1)
                elif item == ("take", "k"):
                    shift(pad_a, "mu_k", k1, 0, "k", 2, k1_done, (wd_done, 1))
                elif kind == "sq":
                    dve.wait_ge(k1_done, PAIRS)
                    for p in range(PAIRS):
                        V.tensor_scalar(kk[:, p, :], k1[:, p, :], pm("k_k", p), None, ALU.mult).then_inc(kk_raw, 1)
                    dve.wait_ge(kgain_done, PAIRS)
                    V.tensor_tensor(kp[:, :, :], kp[:, :, :], k1[:, :, :], ALU.mult).then_inc(kp_done, 1)
                elif kind == "kn":
                    bank = full_bank(dve, item)
                    empty(V.tensor_scalar(rn[:, 2 * a[0]:2 * a[0] + 2, :], halves(bank), 1e-24, None, ALU.max), item)
                elif kind == "kk":
                    dve.wait_ge(pinv_done, 1)
                    dve.wait_ge(kp_done, 1)
                    V.tensor_tensor(bk[:, :, 1, :], units(kp), units(cs), ALU.mult).then_inc(bk_done, 1)
                    dve.wait_ge(kk_root, 1)
                    V.reciprocal(rn[:, :, :], rn[:, :, :]).then_inc(kk_inv, 1)
                    dve.wait_ge(kk_inv, 1)
                    dve.wait_ge(kk_raw, PAIRS)
                    V.tensor_tensor(kk[:, :, :], kk[:, :, :], rn[:, :, :], ALU.mult).then_inc(kk_done, 1)
                    dve.wait_ge(kk_done, 1)
                    V.tensor_tensor(tha[:, :, :], tha[:, :, :], kk[:, :, :], ALU.mult).then_inc(b_done, 1)
                    dve.wait_ge(pinc_done, 1)
                    V.tensor_tensor(kr[:, :, 0, :], units(kk), pinc[:, :, 0:C], ALU.mult).then_inc(kr_done, 1)
                    dve.wait_ge(b_done, 1)
                    V.tensor_tensor(bk[:, :, 0, :], units(tha), units(cs), ALU.mult).then_inc(bk_done, 1)
                elif item == ("take", "r"):
                    shift(pad_b, "mu_r", r1, 0, "r", 3, r1_done, (k1_done, PAIRS))
                elif kind == "rk":
                    dve.wait_ge(r1_done, PAIRS)
                    V.tensor_tensor(kr[:, :, 1, :], units(r1), pinc[:, :, 1:C + 1], ALU.mult).then_inc(kr_done, 1)
                    V.tensor_tensor(k1[:, :, :], r1[:, :, :], kp[:, :, :], ALU.mult).then_inc(rk_prod, 1)
                elif item == ("take", "v"):
                    shift(pad_a, "mu_v", v1, C, "v", 4, v1_done, (r1_done, PAIRS))
                elif item in (("take", "aq"), ("take", "ak")):
                    dve.wait_ge(v1_done, PAIRS)
                    dve.wait_ge(rk_prod, 1)
                    for t in range(TT):
                        rotate(a[0], t, rot if a[0] == "aq" else rot_k, t + (0 if a[0] == "aq" else TT))
                elif kind == "bonus":
                    bank = full_bank(dve, item)
                    j = a[0]
                    dve.wait_ge(v1_done, PAIRS)
                    empty(V.tensor_tensor(bonus[:, 2 * j:2 * j + 2, :], halves(bank), v1[:, 2 * j:2 * j + 2, C:C + SEQ],
                                          ALU.mult), item)
                    if j == 1:
                        taken(dve, "bonus", 1)
                        for p in range(PAIRS):
                            V.tensor_scalar(bonus[:, p, :], bonus[:, p, :], pm("gn_bias", p), None, ALU.add).then_inc(bonus_done, 1)
                elif kind == "A":
                    bank = full_bank(dve, item)
                    j = a[0]
                    empty(V.tensor_tensor(a_neg[:, 8 * j:8 * j + 8, :], bank[:, :].rearrange("p (u c) -> p u c", c=C),
                                          cn("a_mask").unsqueeze(1).to_broadcast([P, 8, C]), ALU.mult), item)
                elif kind == "inv":
                    invert(*a)
                elif kind == "gram":
                    c, par = a
                    if c >= 2:
                        taken(dve, "Yc", c - 2)
                    bank = full_bank(dve, item)
                    heads = lr[:, c % 2, :, :].rearrange("p (a b) n -> p a b n", b=2)[:, :, par, :]
                    empty(V.tensor_tensor(heads, bank[:, :].rearrange("p (a n) -> p a n", a=PAIRS),
                                          cn("gram_mask").unsqueeze(1).to_broadcast([P, PAIRS, P]), ALU.mult), item)
                elif kind == "S":
                    h = a[0]
                    dve.wait_ge(rot_done, 2 * TT)
                    bank = full_bank(dve, item)
                    if h >= 2:
                        taken(dve, "PT", h - 2)
                    for t in range(TT):
                        lo, hi = (0, P) if t == 0 else (P, 3 * P)
                        ins = V.tensor_tensor_reduce(out=pr[:, h % 2, lo:hi], in0=bank[:, lo:hi], in1=cn("causal")[:, lo:hi],
                                                     scale=1.0, scalar=-3.0e38, op0=ALU.add, op1=ALU.max,
                                                     accum_out=amax[:, h, 0, t:t + 1])
                    empty(ins, item)
                    taken(dve, "S", h)
                    V.tensor_scalar(amax[:, h, 1, :], amax[:, h, 0, :], -HEAD ** -0.5, None, ALU.mult).then_inc(nmax, 1)
                elif kind == "norm":
                    h = a[0]
                    dve.wait_ge(exp_done, TT * (h + 1))
                    V.reciprocal(amax[:, h, 0, :], amax[:, h, 2, :]).then_inc(rsum_done, 1)
                    dve.wait_ge(rsum_done, h + 1)
                    for t in range(TT):
                        lo, hi = (0, P) if t == 0 else (P, 3 * P)
                        V.tensor_scalar(pr[:, h % 2, lo:hi], pr[:, h % 2, lo:hi], amax[:, h, 0, t:t + 1], None,
                                        ALU.mult).then_inc(pr_done, 1)
                elif kind == "PV":
                    p = a[0]
                    bank = full_bank(dve, item)
                    taken(dve, "ga", 1)
                    y = ya[:, p % 2, :]
                    empty(V.scalar_tensor_tensor(y, bank[:, 0:SEQ], 0.5, g_a[:, p, :], ALU.mult, ALU.mult), item)
                    dve.wait_ge(ya_hi, p + 1)
                    V.tensor_tensor(y_lo[:, p, :], y, y_hi[:, p, :].bitcast(f32), ALU.subtract).then_inc(ya_lo, 1)
                elif kind in ("T1", "U1", "U2"):
                    half = a[0]
                    if kind == "T1":
                        b, turn = PLACE[("U1", half)]
                        dve.wait_ge(filled[b], turn + 1)
                    bank = full_bank(dve, item)
                    d = (t_inv if kind == "T1" else u_inv)[:, 8 * half:8 * half + 8, :]
                    empty(V.tensor_tensor(d, bank[:, :].rearrange("p (u c) -> p u c", c=C), d, ALU.add), item)
                elif item in (("take", "ga"), ("take", "gb")):
                    dst, n = (g_a, 1) if a[0] == "ga" else (g_b, 3)
                    for j in range(2):
                        dve.wait_ge(gth, n + j)
                        bank = full_bank(dve, (a[0], j))
                        d = dst[:, 2 * j:2 * j + 2, :]
                        empty(V.scalar_tensor_tensor(d, d, 1.0, halves(bank), ALU.add, ALU.mult), (a[0], j))
                    if a[0] == "gb":
                        taken(dve, "gb", 1)
                        dve.wait_ge(bonus_done, PAIRS)
                        V.scalar_tensor_tensor(bonus[:, :, :], bonus[:, :, :], 0.5, g_b[:, :, :], ALU.mult, ALU.mult).then_inc(bonus_done, 1)
                        dve.wait_ge(bonus_done, 1 + PAIRS)
                        for p in range(PAIRS):
                            V.tensor_scalar(g_b[:, p, :], g_b[:, p, :], drv[:, HALF_GAIN, p:p + 1], None, ALU.mult).then_inc(gb_done, 1)
                elif kind == "SA":
                    c, par = a
                    bank = full_bank(dve, item)
                    heads = sav[0:C, c % 2, :, :].rearrange("p (a b) v -> p a b v", b=2)[:, :, par, :]
                    if c >= 2:
                        taken(dve, "Yc", c - 2)
                        taken(dve, "St", c - 2)
                    empty(V.tensor_copy(heads, bank[0:C, 0:PAIRS * C].rearrange("p (a v) -> p a v", a=PAIRS)), item)
                elif kind == "St":
                    c = a[0]
                    bank = full_bank(dve, item)
                    new, old = state[:, (c + 1) % 2, :, :], state[:, c % 2, :, :]
                    p_end = pinc[:, :, C:C + 1].rearrange("p (a b) o -> p a b o", b=CHUNKS)[:, :, c, :].to_broadcast([P, PAIRS, C])
                    if c >= 1:
                        taken(dve, "Yc", c - 1)
                    if c == 0:
                        empty(V.tensor_tensor(new, pairs_v(bank), p_end, ALU.mult), item)
                    else:
                        state_ready(dve, c - 1)
                        empty(V.tensor_tensor(new, pairs_v(bank), old, ALU.add), item)
                        taken(dve, "St", c)
                        V.tensor_tensor(new, new, p_end, ALU.mult).then_inc(st_done, 1)
                elif kind == "mean":
                    t = a[0]
                    taken(dve, "Yc", 2 * t)
                    taken(dve, "Yc", 2 * t + 1)
                    bank = full_bank(dve, item)
                    y = yc[:, :, t * P:(t + 1) * P]
                    empty(V.tensor_tensor(y, y, tiles_v(bank), ALU.subtract), item)
                elif kind == "var":
                    bank = full_bank(dve, item)
                    empty(V.tensor_scalar(gn_r[:, a[0], :, :], tiles_v(bank), 64e-5, None, ALU.add), item)
                elif kind == "gn":
                    t = a[0]
                    tok = slice(t * P, (t + 1) * P)
                    y, g = yc[:, :, tok], gn_r[:, t, :, :]
                    dve.wait_ge(groot, t + 1)
                    V.reciprocal(g, g).then_inc(ginv, 1)
                    dve.wait_ge(ginv, t + 1)
                    V.tensor_tensor(y, y, g, ALU.mult).then_inc(gn_step, 1)
                    dve.wait_ge(gn_step, 2 * t + 1)
                    dve.wait_ge(gb_done, PAIRS)
                    V.tensor_tensor(y, y, g_b[:, :, tok], ALU.mult).then_inc(gn_step, 1)
                    dve.wait_ge(gn_step, 2 * t + 2)
                    dve.wait_ge(bonus_done, 1 + PAIRS)
                    V.tensor_tensor(y, y, bonus[:, :, tok], ALU.add).then_inc(y_done, 1)
                    dve.wait_ge(yb_hi, t + 1)
                    V.tensor_tensor(y_lo[:, PAIRS:2 * PAIRS, tok], y, y_hi[:, PAIRS:2 * PAIRS, tok].bitcast(f32),
                                    ALU.subtract).then_inc(yb_lo, 1)
                elif item == ("take", "out"):
                    dve.wait_ge(s_res, 16)
                    for t in range(TT):
                        for n in range(2):
                            bank = full_bank(dve, ("out", t, n))
                            h = x_res[:, t, n * 512:(n + 1) * 512]
                            empty(V.tensor_tensor(h, bank[:, :], h, ALU.add), ("out", t, n))
                        dve.wait_ge(fs_done, t + 1)
                        V.tensor_scalar(stat[:, 2 + t:3 + t], stat[:, t:t + 1], 1.0 / D_MODEL, 1e-6, ALU.mult, ALU.add).then_inc(fm_done, 1)
                        dve.wait_ge(fr_done, t + 1)
                        V.reciprocal(stat[:, 6 + t:7 + t], stat[:, 4 + t:5 + t]).then_inc(fi_done, 1)
                        dve.wait_ge(fi_done, t + 1)
                        dve.wait_ge(s_fg, 16)
                        V.scalar_tensor_tensor(x_res[:, t, :], x_res[:, t, :], stat[:, 6 + t:7 + t], fgain, ALU.mult,
                                               ALU.mult).then_inc(o_done, 1)

            for item in ORDER:
                dve_part(item)

        @block.tensor
        def _(pe):
            mm = nc.tensor.matmul

            def rows(par):
                return slice(64 * par, 64 * par + 64)

            def split_mm(out, a_hi, a_lo, b_hi, b_lo, first, last):
                mm(out, a_hi, b_hi, start=first, stop=False, skip_group_check=True)
                mm(out, a_lo, b_hi, start=False, stop=False, skip_group_check=True)
                return mm(out, a_hi, b_lo, start=False, stop=last, skip_group_check=True)

            def project(item):
                _, name, q = item
                n = piece_number(item)
                last_piece = q == LAST_PIECE[name]
                hi, lo = w_hi[n % SLOTS], w_lo[n % SLOTS]
                pe.wait_ge(lo_done, n + 1)
                if name == "wd":
                    bank = free_bank(pe, ("wd", 0))
                    h8, l8 = (t[:, :, :].rearrange("p a (b n) -> p (a b) n", n=P) for t in (hi, lo))
                    for k in range(KC):
                        pe.wait_ge(u_hi_done, k // 2 + 1)
                        mm(bank[:, 0:SEQ], h8[:, k, :], u_hi[:, k, :], start=(k == 0), stop=False)
                        mm(bank[:, 0:SEQ], l8[:, k, :], u_hi[:, k, :], start=False, stop=False)
                    for k in range(KC):
                        taken(pe, "xT", k // 2)
                        ins = mm(bank[:, 0:SEQ], h8[:, k, :], u_lo[:, k, :], start=False, stop=(k == KC - 1))
                    fill(ins, ("wd", 0))
                elif name == "wo":
                    half, kp2 = q % 2, q // 2
                    if kp2 == 0:
                        pe.wait_ge(ya_lo, PAIRS)
                    for t in range(TT):
                        job = ("out", t, half)
                        bank = free_bank(pe, job) if kp2 == 0 else banks[PLACE[job][0]]
                        if kp2 == 2:
                            pe.wait_ge(yb_lo, t + 1)
                        for i in range(2):
                            k = 2 * kp2 + i
                            tok = slice(t * P, (t + 1) * P)
                            ins = split_mm(bank[:, :], y_hi[:, k, tok], y_lo[:, k, tok], hi[:, i, :], lo[:, i, :], k == 0, k == KC - 1)
                        if kp2 == 3:
                            fill(ins, job)
                    if kp2 < 3:
                        ins.then_inc(w_used, 1)
                else:
                    by_channel = name in ("k", "r", "v", "ga", "gb")
                    if q == 0:
                        free_bank(pe, (name, 0))
                        free_bank(pe, (name, 1))
                    for j in range(2):
                        bank = banks[PLACE[(name, j)][0]]
                        for i in range(2):
                            k = 2 * q + i
                            if by_channel:
                                for m in range(2):
                                    ch = (2 * j + m) * P
                                    ins = split_mm(bank[:, m * SEQ:(m + 1) * SEQ], hi[:, i, ch:ch + P], lo[:, i, ch:ch + P],
                                                   u_hi[:, k, :], u_lo[:, k, :], k == 0 and m == 0, k == KC - 1)
                            else:
                                tok = slice(j * P, (j + 1) * P)
                                ins = split_mm(bank[:, :], u_hi[:, k, tok], u_lo[:, k, tok], hi[:, i, :], lo[:, i, :], k == 0, k == KC - 1)
                        if last_piece:
                            fill(ins, (name, j))
                    if not last_piece:
                        ins.then_inc(w_used, 1)

            def x_transposed(j):
                bank = free_bank(pe, ("xT", j))
                for t in range(TT):
                    pe.wait_ge(diag_done, t + 1)
                    for i in range(2):
                        at = i * SEQ + t * P
                        ins = mm(bank[:, at:at + P], xt[:, t, (2 * j + i) * P:(2 * j + i + 1) * P], diag[:, t, :],
                                 start=True, stop=True)
                fill(ins, ("xT", j))

            def up_project(kind, j):
                bank = free_bank(pe, (kind, j))
                pe.wait_ge(s_up, 16)
                pe.wait_ge(wd_done, 1)
                pe.wait_ge(wd_tanh, 1)
                r = rows(0 if kind == "upw" else 1)
                for i in range(2):
                    ch = (2 * j + i) * P
                    ins = mm(bank[:, i * SEQ:(i + 1) * SEQ], up_sb[r, ch:ch + P], wd[r, :], start=True, stop=True)
                fill(ins, (kind, j))

            def head_sums(kind, j):
                bank = free_bank(pe, (kind, j))
                if kind == "kn":
                    pe.wait_ge(kk_sq, 2 * j + 2)
                    ins = mm(bank[:, :], cn("head_sum"), rn[:, 2 * j:2 * j + 2, :].rearrange("p a b -> p (a b)"),
                             start=True, stop=True)
                else:
                    pe.wait_ge(rk_prod, 1)
                    pe.wait_ge(head_rk_done, PAIRS)
                    for i in range(2):
                        ins = mm(bank[:, i * SEQ:(i + 1) * SEQ], head_rk[:, 2 * j + i, :], k1[:, 2 * j + i, :],
                                 start=True, stop=True)
                fill(ins, (kind, j))

            def a_matrix(half):
                bank = free_bank(pe, ("A", half))
                pe.wait_ge(kr_done, 1)
                pe.wait_ge(bk_done, 2)
                for n in range(8):
                    c, p = 2 * half + n // PAIRS, n % PAIRS
                    u = p * CHUNKS + c
                    for par in range(2):
                        ins = mm(bank[rows(par), n * C:(n + 1) * C], kr[rows(par), u, 0, :], bk[rows(par), u, 0, :],
                                 start=True, stop=True)
                fill(ins, ("A", half))

            def transposed(kind, j, src):
                bank = free_bank(pe, (kind, j))
                for i in range(2):
                    for t in range(TT):
                        at = i * SEQ + t * P
                        ins = nc.tensor.transpose(bank[:, at:at + P], src[:, t, (2 * j + i) * P:(2 * j + i + 1) * P], cn("ident"))
                fill(ins, (kind, j))

            def v_tokens(c):
                bank = free_bank(pe, ("vT", c))
                pe.wait_ge(v1_done, PAIRS)
                pe.wait_ge(zeroed, 6)
                for p in range(PAIRS):
                    ins = nc.tensor.transpose(bank[:, p * P:(p + 1) * P], v1[:, p, c * C:c * C + P], cn("ident"))
                fill(ins, ("vT", c))

            def b_tokens(c):
                bank = free_bank(pe, ("bT", c))
                pe.wait_ge(bk_done, 2)
                for p in range(PAIRS):
                    src = bk[:, p * CHUNKS + c, :, :].rearrange("p s c -> p (s c)")
                    ins = nc.tensor.transpose(bank[:, p * P:(p + 1) * P], src, cn("ident"))
                fill(ins, ("bT", c))

            def gram(c, par):
                bank = free_bank(pe, ("gram", c, par))
                pe.wait_ge(kr_done, 2)
                for p in range(PAIRS):
                    u = p * CHUNKS + c
                    ins = mm(bank[:, p * P:(p + 1) * P], bk[rows(par), u, :, :].rearrange("p s c -> p (s c)"),
                             kr[rows(par), u, :, :].rearrange("p s c -> p (s c)"), start=True, stop=True)
                fill(ins, ("gram", c, par))

            def scores(h):
                p, par = h // 2, h % 2
                bank = free_bank(pe, ("S", h))
                taken(pe, "qT", p // 2)
                taken(pe, "kT", p // 2)
                mm(bank[:, 0:P], qT[rows(par), p, 0:P], kT[rows(par), p, 0:P], start=True, stop=True)
                ins = mm(bank[:, P:3 * P], qT[rows(par), p, P:SEQ], kT[rows(par), p, :], start=True, stop=True)
                fill(ins, ("S", h))

            def probs_T(h):
                bank = free_bank(pe, ("PT", h))
                pe.wait_ge(pr_done, TT * (h + 1))
                for i in range(3):
                    ins = nc.tensor.transpose(bank[:, i * P:(i + 1) * P], pr[:, h % 2, i * P:(i + 1) * P], cn("ident"))
                fill(ins, ("PT", h))

            def head_out(p):
                bank = free_bank(pe, ("PV", p))
                taken(pe, "PT", 2 * p)
                taken(pe, "PT", 2 * p + 1)
                taken(pe, "av", 0)
                taken(pe, "av", 1)
                for par in range(2):
                    h = 2 * p + par
                    mm(bank[rows(par), 0:SEQ], v_att[:, 0, h * HEAD:(h + 1) * HEAD], prT[:, par, 0:SEQ], start=True, stop=False)
                    ins = mm(bank[rows(par), P:SEQ], v_att[:, 1, h * HEAD:(h + 1) * HEAD], prT[:, par, SEQ:3 * P],
                             start=False, stop=True)
                fill(ins, ("PV", p))

            def double(kind, half, lhs, rhs):
                bank = free_bank(pe, (kind, half))
                for n in range(8):
                    u = 8 * half + n
                    for par in range(2):
                        ins = mm(bank[rows(par), n * C:(n + 1) * C], lhs[rows(par), u, :], rhs[rows(par), u, :],
                                 start=True, stop=True)
                fill(ins, (kind, half))

            def right_side(c):
                bank = free_bank(pe, ("R", c))
                taken(pe, "gram", c, 0)
                taken(pe, "gram", c, 1)
                taken(pe, "vT", c)
                for h in range(HEADS):
                    p, par = h // 2, h % 2
                    ins = mm(bank[rows(par), p * C:(p + 1) * C], lr[:, c % 2, h, 0:C], sav[:, c % 2, h, :],
                             start=(p == 0), stop=(c == 0), skip_group_check=True)
                if c:
                    state_ready(pe, c - 1)
                    for h in range(HEADS):
                        p, par = h // 2, h % 2
                        ins = mm(bank[rows(par), p * C:(p + 1) * C], kr[rows(par), p * CHUNKS + c, 0, :],
                                 state[rows(par), c % 2, p, :], start=False, stop=True, skip_group_check=True)
                fill(ins, ("R", c))

            def solve(c, par):
                bank = free_bank(pe, ("SA", c, par))
                taken(pe, "R", c)
                taken(pe, "U2", c // 2)
                for p in range(PAIRS):
                    ins = mm(bank[0:C, p * C:(p + 1) * C], u_inv[rows(par), c * PAIRS + p, :], r_neg[rows(par), p, :],
                             start=True, stop=True)
                fill(ins, ("SA", c, par))

            def new_state(c):
                bank = free_bank(pe, ("St", c))
                taken(pe, "SA", c, 0)
                taken(pe, "SA", c, 1)
                taken(pe, "bT", c)
                for h in range(HEADS):
                    p, par = h // 2, h % 2
                    ins = mm(bank[rows(par), p * C:(p + 1) * C], bkt[:, c % 2, h, :], sav[:, c % 2, h, :], start=True, stop=True)
                fill(ins, ("St", c))

            def chunk_out(c):
                bank = free_bank(pe, ("Yc", c))
                taken(pe, "SA", c, 0)
                taken(pe, "SA", c, 1)
                for h in range(HEADS):
                    p, par = h // 2, h % 2
                    ins = mm(bank[rows(par), p * C:(p + 1) * C], sav[:, c % 2, h, :], lr[:, c % 2, h, C:P],
                             start=(p == 0), stop=(c == 0), skip_group_check=True)
                if c:
                    for h in range(HEADS):
                        p, par = h // 2, h % 2
                        ins = mm(bank[rows(par), p * C:(p + 1) * C], state[rows(par), c % 2, p, :],
                                 kr[rows(par), p * CHUNKS + c, 1, :], start=False, stop=True, skip_group_check=True)
                fill(ins, ("Yc", c))

            def mean(t):
                bank = free_bank(pe, ("mean", t))
                taken(pe, "Yc", 2 * t)
                taken(pe, "Yc", 2 * t + 1)
                fill(mm(bank[:, :].rearrange("p (a v) -> p a v", a=PAIRS), cn("head_mean"), yc[:, :, t * P:(t + 1) * P],
                        start=True, stop=True), ("mean", t))

            def var(t):
                bank = free_bank(pe, ("var", t))
                pe.wait_ge(csq_done, t + 1)
                fill(mm(bank[:, :], cn("head_mean"), gn_r[:, t, :, :].rearrange("p a v -> p (a v)"),
                        start=True, stop=True), ("var", t))

            pe.wait_ge(warm_zero, 1)
            for _ in range(WARM_UP):
                mm(banks[PROJ_BANKS[-1]][:, 0:SEQ], r1[:, 0, 0:P], r1[:, 0, :], start=True, stop=True)
            for item in ORDER:
                kind, args = item[0], item[1:]
                if kind == "xT":
                    x_transposed(*args)
                elif kind == "w":
                    project(item)
                elif kind in ("upw", "upa"):
                    up_project(kind, *args)
                elif kind in ("kn", "bonus"):
                    head_sums(kind, *args)
                elif kind == "A":
                    a_matrix(*args)
                elif kind in ("qT", "kT"):
                    pe.wait_ge(rot_done, 2 if kind == "qT" else 4)
                    transposed(kind, *args, rot if kind == "qT" else rot_k)
                elif kind == "vT":
                    v_tokens(*args)
                elif kind == "bT":
                    b_tokens(*args)
                elif kind == "gram":
                    gram(*args)
                elif kind == "S":
                    scores(*args)
                elif kind == "PT":
                    probs_T(*args)
                elif kind == "PV":
                    head_out(*args)
                elif kind == "Y1":
                    pe.wait_ge(s_scatter, 16 * 16)
                    pe.wait_ge(low_done, 1)
                    double(kind, *args, b16, u_inv)
                elif kind == "T1":
                    taken(pe, "Y1", args[0])
                    double(kind, *args, y_sb, t_inv)
                elif kind == "U1":
                    double(kind, *args, t_inv, y_sb)
                elif kind == "Y2":
                    taken(pe, "U1", args[0])
                    pe.wait_ge(low_done, 2)
                    double(kind, *args, b32, u_inv)
                elif kind == "U2":
                    taken(pe, "T1", args[0])
                    taken(pe, "Y2", args[0])
                    double(kind, *args, t_inv, y_sb)
                elif kind == "R":
                    right_side(*args)
                elif kind == "SA":
                    solve(*args)
                elif kind == "St":
                    new_state(*args)
                elif kind == "Yc":
                    chunk_out(*args)
                elif kind == "mean":
                    mean(*args)
                elif kind == "var":
                    var(*args)


def constants():
    a = np.zeros((P, N_CONST), np.float32)
    i = np.arange(P)

    def put(name, v):
        s, e = CONST[name]
        a[:, s:e] = v

    put("ident", np.eye(P))
    same = (i[:, None] // HEAD == i[None, :] // HEAD).astype(np.float32)
    put("head_sum", same)
    put("head_mean", same / HEAD)
    j, t, col = i[:, None] % C, i[None, :] % C, i[None, :] // C
    g = np.where(col == 0, j < t, j <= t).astype(np.float32)
    g[0:C, 0:C] = 0
    put("gram_mask", g)
    r, q = i[:, None] % C, np.arange(C)[None, :]
    put("a_mask", np.where(q < r, -1.0, 0.0))
    put("low16", (r // 32 == q // 32) & (r % 32 >= 16) & (q % 32 < 16))
    put("low32", (r >= 32) & (q < 32))
    put("scan", (np.arange(SEQ) % C != 0)[None, :])
    causal = np.where(i[None, :] <= i[:, None], 0.0, -1e30)
    put("causal", np.concatenate([causal, np.zeros((P, P)), causal], 1))
    inv = 1.0 / (np.float32(10000.0) ** (np.arange(0, HEAD, 2, dtype=np.float32) / np.float32(HEAD)))
    ang = np.arange(SEQ, dtype=np.float32)[:, None] * inv[None, :].astype(np.float32)
    cos, sin = np.cos(ang), np.sin(ang)
    cos2, sin2 = np.concatenate([cos, cos], 1), np.concatenate([-sin, sin], 1)
    put("cos", cos2.reshape(TT, P, HEAD).transpose(1, 0, 2).reshape(P, -1))
    put("sin", sin2.reshape(TT, P, HEAD).transpose(1, 0, 2).reshape(P, -1))
    put("block_eye", np.eye(BASE).reshape(1, -1))
    return a


def kernel(x, norm_gain, w_in, shift_mu, decay_bias, decay_up, iclr_bias, iclr_up,
           k_k, k_a, r_k, gn_gain, gn_bias, w_out, final_gain):
    import concourse.bacc as bacc
    from concourse.bass_utils import run_bass_kernel_spmd as run

    w = np.asarray(w_in)[0].reshape(KC, P, -1).transpose(1, 0, 2)
    wo = np.asarray(w_out)[0].reshape(KC, P, -1).transpose(1, 0, 2)
    W = WIDTH
    start = {"aq": 0, "ak": W, "av": 2 * W, "ga": 3 * W, "r": 4 * W, "k": 5 * W, "v": 6 * W, "gb": 7 * W + P}
    arrays = {"in_" + n: np.ascontiguousarray(w[:, :, s:s + W]) for n, s in start.items()}
    arrays["in_wo"] = np.ascontiguousarray(np.stack([wo[:, :, 0:512], wo[:, :, 512:1024]], 1))
    arrays["in_wd"] = np.ascontiguousarray(w[:, :, 7 * W:7 * W + P]).reshape(P, -1)
    arrays["in_up"] = np.concatenate([np.asarray(decay_up)[0], np.asarray(iclr_up)[0]], 0)
    arrays["in_x"] = np.ascontiguousarray(np.asarray(x)[0])
    arrays["in_const"] = constants()
    by_channel = lambda a: np.asarray(a).reshape(-1, P).T
    mu = np.asarray(shift_mu)[0]
    cols = {"mu_r": mu[0:W], "mu_k": mu[W:2 * W], "mu_v": mu[2 * W:3 * W], "mu_w": mu[3 * W:],
            "decay_bias": decay_bias, "iclr_bias": iclr_bias, "k_k": k_k, "k_a": k_a, "r_k": r_k,
            "gn_gain": gn_gain, "gn_bias": gn_bias, "norm_gain": norm_gain}
    arrays["in_param"] = np.ascontiguousarray(np.concatenate([by_channel(cols[n]) for n in PARAM], 1))
    arrays["in_fg"] = np.ascontiguousarray(np.asarray(final_gain))

    nc = bacc.Bacc("TRN2", target_bir_lowering=False, num_devices=1)
    f32 = mybir.dt.float32
    ap = {n: nc.dram_tensor(n, a.shape, f32, kind="ExternalInput").ap() for n, a in arrays.items()}
    a_scratch = nc.dram_tensor("a_scratch", (P, UNITS, C), f32, kind="Internal").ap()
    t_scratch = nc.dram_tensor("t_scratch", (P, 2, BASE * BASE), f32, kind="Internal").ap()
    out = nc.dram_tensor("out", (SEQ, D_MODEL), f32, kind="ExternalOutput").ap()
    hybrid_layer(nc, ap["in_x"], {n: ap["in_" + n] for n in BLOCKS}, ap["in_up"], ap["in_const"],
                 ap["in_param"], ap["in_fg"], a_scratch, t_scratch, out)
    r = run(nc, [arrays], core_ids=[0])
    return r.results[0]["out"].reshape(1, SEQ, D_MODEL)
```

```python
import concourse.bass as bass
from concourse import mybir
from contextlib import ExitStack
import numpy as np

D_MODEL, SEQ, HEAD, HEADS = 1024, 256, 64, 8
WIDTH = HEAD * HEADS
P = 128
PAIRS = WIDTH // P
KC = D_MODEL // P
TT = SEQ // P
C = 64
CHUNKS = SEQ // C
UNITS = CHUNKS * PAIRS
BASE = 16
DECAY = 0.5 * float(np.exp(-0.5))

CONST = {}
_at = 0
for _name, _n in (("ident", P), ("head_mean", P), ("center", P), ("head_sum", P), ("gram_mask", P), ("a_mask", C),
                  ("low16", C), ("low32", C), ("scan", SEQ), ("causal", 3 * P), ("cos", TT * HEAD),
                  ("sin", TT * HEAD), ("block_eye", BASE * BASE)):
    CONST[_name] = (_at, _at + _n)
    _at += _n
N_CONST = _at
PARAM = {}
_at = 0
for _name, _n in (("mu_r", PAIRS), ("mu_k", PAIRS), ("mu_v", PAIRS), ("mu_w", 1), ("decay_bias", PAIRS),
                  ("iclr_bias", PAIRS), ("k_k", PAIRS), ("k_a", PAIRS), ("r_k", PAIRS),
                  ("gn_gain", PAIRS), ("gn_bias", PAIRS), ("norm_gain", KC)):
    PARAM[_name] = (_at, _at + _n)
    _at += _n
N_PARAM = _at

BLOCKS = ["wd", "k", "r", "v", "aq", "ak", "av", "ga", "gb", "wo"]
PIECES = [("wd", 0)] + [(b, q) for b in BLOCKS[1:-1] for q in range(4)] + \
         [("wo", q) for q in range(8)]
RAW_SLOTS, SLOTS, LEAD = 4, 5, 4
WARM_UP = 8
DVE_PIECES = (0, 4, 8, 12)

PROJ_BANKS, AUX_BANKS = (0, 1, 2, 3), (4, 5, 6, 7)


ORDER = [
    ("xT", 0), ("xT", 1), ("xT", 2), ("xT", 3),
    ("w", "wd", 0), ("take", "wd"),
    ("w", "k", 0),
    ("w", "k", 1), ("upw", 0), ("upa", 0), ("upw", 1), ("upa", 1),
    ("w", "k", 2), ("decay",),
    ("w", "k", 3), ("take", "k"), ("sq",),
    ("w", "r", 0), ("kn", 0), ("kn", 1),
    ("w", "r", 1), ("kk",),
    ("w", "r", 2),
    ("w", "r", 3), ("take", "r"),
    ("w", "v", 0),
    ("w", "v", 1),
    ("w", "v", 2), ("A", 0),
    ("w", "v", 3), ("A", 1), ("rk",), ("take", "v"), ("clear",), ("masks",),
    ("w", "aq", 0), ("bonus", 0), ("a_out",),
    ("w", "aq", 1), ("bonus", 1), ("inv", 1, 8), ("vT", 0), ("inv", 8, 12), ("bT", 0),
    ("w", "aq", 2), ("gram", 0),
    ("w", "aq", 3), ("inv", 12, 16), ("take", "aq"), ("gather",),
    ("w", "ak", 0),
    ("w", "ak", 1), ("t_out",), ("scatter",), ("qT", 0), ("qT", 1),
    ("w", "ak", 2),
    ("w", "ak", 3), ("Y1", 0), ("Y1", 1), ("take", "ak"), ("kT", 0), ("kT", 1),
    ("w", "av", 0), ("S", 0), ("T1", 0), ("norm", 0), ("U1", 0),
    ("w", "av", 1), ("norm", 1), ("T1", 1), ("U1", 1), ("Y2", 0), ("PT", 0),
    ("w", "av", 2), ("U2", 0), ("Y2", 1), ("PT", 1), ("R", 0), ("U2", 1), ("SA", 0),
    ("w", "av", 3), ("take", "av"), ("vT", 1), ("bT", 1), ("St", 0),
    ("w", "ga", 0), ("Yc", 0), ("S", 1), ("norm", 2),
    ("w", "ga", 1), ("norm", 3), ("gram", 1),
    ("w", "ga", 2), ("R", 1),
    ("w", "ga", 3), ("take", "ga"), ("SA", 1), ("PV", 0), ("PT", 2),
    ("w", "gb", 0), ("PT", 3), ("S", 2), ("norm", 4), ("norm", 5), ("St", 1), ("vT", 2), ("bT", 2),
    ("w", "gb", 1), ("PV", 1), ("PT", 4), ("PT", 5), ("S", 3), ("norm", 6), ("norm", 7), ("PV", 2),
        ("gram", 2),
    ("w", "gb", 2), ("Yc", 1), ("R", 2), ("PT", 6), ("PT", 7),
    ("w", "gb", 3), ("take", "gb"), ("vT", 3), ("bT", 3), ("SA", 2), ("gram", 3), ("mid", 0), ("St", 2),
        ("PV", 3), ("R", 3), ("Yc", 2), ("var", 0), ("SA", 3),
    ("w", "wo", 0), ("gn", 0, 0), ("Yc", 3),
    ("w", "wo", 1), ("gn", 0, 1), ("mid", 1),
    ("w", "wo", 2), ("var", 1),
    ("w", "wo", 3), ("gn", 1, 0), ("gn", 1, 1),
    ("w", "wo", 4),
    ("w", "wo", 5),
    ("w", "wo", 6),
    ("w", "wo", 7),
    ("w1", "wo", 4),
    ("w1", "wo", 6),
    ("w1", "wo", 5),
    ("w1", "wo", 7), ("take", "out"),
]
LAST_PIECE = {b: max(q for b2, q in PIECES if b2 == b) for b in BLOCKS}


def piece_number(item):
    return PIECES.index(item[1:])


def place_jobs():
    turn, used, place = {"proj": 0, "aux": 0}, [0] * 8, {}

    def put(name, kind):
        banks = PROJ_BANKS if kind == "proj" else AUX_BANKS
        b = banks[turn[kind] % len(banks)]
        turn[kind] += 1
        place[name] = (b, used[b])
        used[b] += 1

    for item in ORDER:
        if item[0] == "w":
            if item[2] == 0:
                for j in range(1 if item[1] == "wd" else 4 if item[1] == "wo" else 2):
                    put(("out", j // 2, j % 2) if item[1] == "wo" else (item[1], j), "proj")
        elif item[0] not in ("take", "decay", "kk", "rk", "inv", "norm", "gn", "a_out", "gather", "t_out", "scatter", "sq", "clear", "masks", "w1"):
            if item[0] in ("gram", "SA", "S"):
                for par in range(2):
                    put((item[0], 2 * item[1] + par), "aux")
            else:
                put(item, "aux")
    return place


def hybrid_layer(nc, x, w_blocks, up, const, param, final_gain, a_scratch, t_scratch, out):
    f32, f32r = mybir.dt.float32, mybir.dt.float32r
    ALU = mybir.AluOpType
    ACT = mybir.ActivationFunctionType
    AX = mybir.AxisListType
    PLACE = place_jobs()
    ctx = ExitStack()
    with ctx:
        def sb(name, shape, dt=f32, scope=ctx):
            return scope.enter_context(nc.sbuf_tensor(name, shape, dt))

        def sem(name):
            return ctx.enter_context(nc.semaphore(name))

        banks = [ctx.enter_context(nc.psum_tensor(f"bank{b}", [P, 512], f32)) for b in range(8)]

        cst = sb("cst", [P, N_CONST])
        prm = sb("prm", [P, N_PARAM])
        drv = sb("drv", [P, 6, PAIRS])
        w_raw = [sb(f"w_raw{s}", [P, 2, 512]) for s in range(RAW_SLOTS)]
        w_hi = [sb(f"w_hi{s}", [P, 2, 512], f32r) for s in range(SLOTS)]
        w_lo = [sb(f"w_lo{s}", [P, 2, 512], f32r) for s in range(SLOTS)]
        up_sb = sb("up_sb", [P, WIDTH])
        u_hi = sb("u_hi", [P, KC, SEQ], f32r)
        u_lo = sb("u_lo", [P, KC, SEQ], f32r)
        stat = sb("stat", [P, 4 * TT])
        fin = sb("fin", [P, 2, TT])
        gn_eps = sb("gn_eps", [P, 1])
        pad_a = sb("pad_a", [P, PAIRS, SEQ + 1])
        pad_b = sb("pad_b", [P, PAIRS, SEQ + 1])
        pad_w = sb("pad_w", [P, SEQ + 1])
        wd = sb("wd", [P, SEQ])
        dif = sb("dif", [P, PAIRS, SEQ])
        k1 = sb("k1", [P, PAIRS, SEQ])
        r1 = sb("r1", [P, PAIRS, SEQ])
        v1 = sb("v1", [P, PAIRS, C + SEQ])
        with ExitStack() as early:
            kk = sb("kk", [P, PAIRS, SEQ], scope=early)
            rn = sb("rn", [P, PAIRS, SEQ], scope=early)
            thw = sb("thw", [P, PAIRS, SEQ], scope=early)
            cs = sb("cs", [P, PAIRS, SEQ], scope=early)
        y_hi = sb("y_hi", [P, 2 * PAIRS, SEQ], f32r)
        y_lo = sb("y_lo", [P, 2 * PAIRS, SEQ], f32r)
        with ExitStack() as early:
            xt = sb("xt", [P, TT, D_MODEL], scope=early)
        lr = sb("lr", [P, 2, HEADS, P])
        tha = sb("tha", [P, PAIRS, SEQ])
        kp = sb("kp", [P, PAIRS, SEQ])
        pinc = sb("pinc", [P, UNITS, C + 1])
        bk = sb("bk", [P, UNITS, 2, C])
        kr = sb("kr", [P, UNITS, 2, C])
        head_rk = sb("head_rk", [P, PAIRS, P])
        y_sb = sb("y_sb", [P, UNITS, C])
        blk = sb("blk", [P, 4, BASE * BASE])
        bkt = sb("bkt", [P, 2, HEADS, C])
        sav = sb("sav", [P, 2, HEADS, C])
        state = sb("state", [P, 2, PAIRS, C])
        r_neg = sb("r_neg", [P, PAIRS, C])
        yc = sb("yc", [P, PAIRS, SEQ])
        gn_r = sb("gn_r", [P, 2, PAIRS, P])
        yz = sb("yz", [P, PAIRS, P])
        ya = sb("ya", [P, 2, SEQ])
        g_b = sb("g_b", [P, PAIRS, SEQ])
        qT = sb("qT", [P, PAIRS, SEQ])
        kT = sb("kT", [P, PAIRS, SEQ])
        amax = sb("amax", [P, HEADS, 3, TT])
        xn = [y_sb[:, :, :].rearrange("p u c -> p (u c)"), bk[:, 0:8, :, :].rearrange("p u s c -> p (u s c)")]
        a_neg = kk[:, :, :].rearrange("p a (b c) -> p (a b) c", c=C)
        b16 = rn[:, :, :].rearrange("p a (b c) -> p (a b) c", c=C)
        b32 = thw[:, :, :].rearrange("p a (b c) -> p (a b) c", c=C)
        t_inv = cs[:, :, :].rearrange("p a (b c) -> p (a b) c", c=C)
        u_inv = tha[:, :, :].rearrange("p a (b c) -> p (a b) c", c=C)
        rot = r1[:, :, :].rearrange("p a b -> p (a b)").rearrange("p (t n) -> p t n", t=TT)
        v_att = kp[:, :, :].rearrange("p a b -> p (a b)").rearrange("p (t n) -> p t n", t=TT)
        rot_k = pad_b[:, :, :].rearrange("p a b -> p (a b)")[:, 0:TT * WIDTH].rearrange("p (t n) -> p t n", t=TT)
        g_a = r1
        x_res = kr[:, :, :, :].rearrange("p u s c -> p (u s c)").rearrange("p (t n) -> p t n", t=TT)
        fgain = bk[:, 0:8, :, :].rearrange("p u s c -> p (u s c)")
        pad_a_flat = pad_a[:, :, :].rearrange("p a b -> p (a b)")
        rtmp = dif[:, :, :].rearrange("p a b -> p (a b)")
        bonus = k1
        pr = rtmp[:, 0:6 * P].rearrange("p (b n) -> p b n", b=2)
        h_gain = [b[:, :, :].rearrange("p a b -> p (a b)") for b in (qT, kT)]
        prT = pad_a_flat[:, 0:6 * P].rearrange("p (b n) -> p b n", b=2)

        def cn(name):
            a, b = CONST[name]
            return cst[:, a:b]

        def pm(name, i=0):
            a, _ = PARAM[name]
            return prm[:, a + i:a + i + 1]

        def pm_all(name):
            a, b = PARAM[name]
            return prm[:, a:b]

        HALF_DB, HALF_IB, HALF_KA, ONE_KA, HALF_GAIN = range(5)

        s_const = sem("s_const")
        s_x = [sem(f"s_x{t}") for t in range(TT)]
        s_ident = sem("s_ident")
        s_raw = [sem(f"s_raw{s}") for s in range(RAW_SLOTS)]
        s_res = sem("s_res")
        hi_done = sem("hi_done")
        lo_pool = sem("lo_pool")
        lo_dve = sem("lo_dve")
        w_used = sem("w_used")
        ya_hi = sem("ya_hi")
        ya_lo = sem("ya_lo")
        y_done = sem("y_done")
        yb_hi = sem("yb_hi")
        s_up = sem("s_up")
        s_fg = sem("s_fg")
        s_out = sem("s_out")
        s_gather = sem("s_gather")
        s_scatter = sem("s_scatter")
        s_a_out = sem("s_a_out")
        s_t_out = sem("s_t_out")
        filled = [sem(f"filled{b}") for b in range(8)]
        emptied = [sem(f"emptied{b}") for b in range(8)]
        warm_zero = sem("warm_zero")
        eps_done = sem("eps_done")
        table_in = sem("table_in")
        zeroed = sem("zeroed")
        drv_done = sem("drv_done")
        ss_done = sem("ss_done")
        u_hi_done = sem("u_hi_done")
        ms_done = sem("ms_done")
        sq_done = sem("sq_done")
        rstd_done = sem("rstd_done")
        xn_done = sem("xn_done")
        dif_done = sem("dif_done")
        k1_done = sem("k1_done")
        wd_done = sem("wd_done")
        wd_tanh = sem("wd_tanh")
        r1_done = sem("r1_done")
        v1_done = sem("v1_done")
        kk_raw = sem("kk_raw")
        kk_sq = sem("kk_sq")
        kk_root = sem("kk_root")
        kk_inv = sem("kk_inv")
        kk_done = sem("kk_done")
        thw1_done = sem("thw1_done")
        cs_done = sem("cs_done")
        pinc_done = sem("pinc_done")
        pinv_done = sem("pinv_done")
        kgain_done = sem("kgain_done")
        kp_done = sem("kp_done")
        a_done = sem("a_done")
        b_done = sem("b_done")
        bk_done = sem("bk_done")
        kr_done = sem("kr_done")
        rk_prod = sem("rk_prod")
        head_rk_done = sem("head_rk_done")
        bonus_done = sem("bonus_done")
        low_done = sem("low_done")
        inv_step = sem("inv_step")
        inv_done = sem("inv_done")
        tu_zero = sem("tu_zero")
        y_zero = sem("y_zero")
        st_done = sem("st_done")
        csq_done = sem("csq_done")
        ginv = sem("ginv")
        gn_step = sem("gn_step")
        yb_lo = sem("yb_lo")
        gth = sem("gth")
        gb_done = sem("gb_done")
        rot_done = sem("rot_done")
        nmax = sem("nmax")
        exp_done = sem("exp_done")
        rsum_done = sem("rsum_done")
        pr_done = sem("pr_done")
        fs_done = sem("fs_done")
        fm_done = sem("fm_done")
        fr_done = sem("fr_done")
        fi_done = sem("fi_done")
        hg_done = sem("hg_done")
        o_done = sem("o_done")

        def free_bank(eng, job):
            b, turn = PLACE[job]
            if turn:
                eng.wait_ge(emptied[b], turn)
            return banks[b]

        def fill(ins, job):
            ins.then_inc(filled[PLACE[job][0]], 1)

        def full_bank(eng, job):
            b, turn = PLACE[job]
            eng.wait_ge(filled[b], turn + 1)
            return banks[b]

        def taken(eng, *job):
            b, turn = PLACE[job]
            eng.wait_ge(emptied[b], turn + 1)

        def empty(ins, job):
            ins.then_inc(emptied[PLACE[job][0]], 1)

        def on_dve(n):
            return n in DVE_PIECES

        def lo_ready(eng, n):
            eng.wait_ge(lo_dve if on_dve(n) else lo_pool, sum(on_dve(m) == on_dve(n) for m in range(n + 1)))

        def piece_used(eng, n):
            b, q = PIECES[n]
            if q == LAST_PIECE[b]:
                at, turn = PLACE[(b, 0 if b == "wd" else 1)]
                eng.wait_ge(filled[at], turn + 1)
            else:
                eng.wait_ge(w_used, sum(q2 != LAST_PIECE[b2] for b2, q2 in PIECES[:n + 1]))

        def state_ready(eng, c):
            if c == 0:
                taken(eng, "St", 0)
            else:
                eng.wait_ge(st_done, c)

        def lower16(t):
            return t.rearrange("p u (b c) -> p u b c", b=2)[:, :, :, 0:BASE]

        def upper16(t):
            return t.rearrange("p u (b c) -> p u b c", b=2)[:, :, :, BASE:2 * BASE]

        def upper32(t):
            return t[:, :, 2 * BASE:C]

        def filled16(bank):
            return bank[:, 0:8 * C // 2].rearrange("p (u b c) -> p u b c", b=2, c=BASE)

        def filled32(bank):
            return bank[:, 0:8 * C // 2].rearrange("p (u c) -> p u c", c=2 * BASE)

        block = ctx.enter_context(nc.Block())

        @block.sync
        def _(sp):
            sp.dma_start(xt[:, 0, :], x[0:P, :]).then_inc(s_x[0], 16)
            sp.dma_start(xt[:, 1, :], x[P:SEQ, :]).then_inc(s_x[1], 16)
            sp.dma_start(cst[:, 0:P], const[:, 0:P]).then_inc(s_ident, 16)
            sp.dma_start(prm[:, :], param).then_inc(s_ident, 16)

            def load(n):
                b, q = PIECES[n]
                if n >= RAW_SLOTS:
                    lo_ready(sp, n - RAW_SLOTS)
                dst = w_raw[n % RAW_SLOTS]
                if b == "wd":
                    sp.dma_start(dst[:, :, :].rearrange("p k n -> p (k n)"), w_blocks[b]).then_inc(s_raw[n % RAW_SLOTS], 16)
                elif b == "wo":
                    sp.dma_start(dst[:, :, :], w_blocks[b][:, q % 2, q // 2 * 2:q // 2 * 2 + 2, :]).then_inc(s_raw[n % RAW_SLOTS], 16)
                else:
                    sp.dma_start(dst[:, :, :], w_blocks[b][:, 2 * q:2 * q + 2, :]).then_inc(s_raw[n % RAW_SLOTS], 16)

            for n in range(RAW_SLOTS):
                load(n)
            for item in ORDER:
                if item[0] == "w" and piece_number(item) + RAW_SLOTS < len(PIECES):
                    load(piece_number(item) + RAW_SLOTS)
                    if item[1] == "wd":
                        sp.dma_start(up_sb[:, :], up).then_inc(s_up, 16)
                        sp.dma_start(cst[:, P:N_CONST], const[:, P:N_CONST]).then_inc(s_const, 16)
                elif item[0] == "a_out":
                    taken(sp, "A", 0)
                    taken(sp, "A", 1)
                    sp.dma_start(a_scratch, a_neg).then_inc(s_a_out, 16)
                elif item[0] == "gather":
                    sp.wait_ge(s_a_out, 16)
                    for par in range(2):
                        for b in range(C // BASE):
                            u0, row, col = (par * 4 + b) * UNITS, 64 * par + BASE * b, BASE * b
                            sp.dma_start(blk[u0:u0 + UNITS, 0, :].rearrange("u (i j) -> u i j", i=BASE),
                                         a_scratch[row:row + BASE, :, col:col + BASE].rearrange("i u j -> u i j")
                                         ).then_inc(s_gather, 16)
                elif item[0] == "t_out":
                    sp.wait_ge(inv_done, 1)
                    sp.dma_start(t_scratch, blk[:, 1:3, :]).then_inc(s_t_out, 16)
                elif item[0] == "scatter":
                    sp.wait_ge(tu_zero, 2)
                    sp.wait_ge(s_t_out, 16)
                    for dst, src in ((t_inv, 0), (u_inv, 1)):
                        for par in range(2):
                            for b in range(C // BASE):
                                u0, row, col = (par * 4 + b) * UNITS, 64 * par + BASE * b, BASE * b
                                sp.dma_start(dst[row:row + BASE, :, col:col + BASE],
                                             t_scratch[u0:u0 + UNITS, src, :].rearrange("u (i j) -> i u j", i=BASE)
                                             ).then_inc(s_scatter, 16)
            b, turn = PLACE[("Yc", CHUNKS - 1)]
            sp.wait_ge(filled[b], turn + 1)
            sp.dma_start(x_res, x.rearrange("(t p) n -> p t n", t=TT)).then_inc(s_res, 16)
            sp.dma_start(fgain, final_gain.partition_broadcast(P)).then_inc(s_fg, 16)
            for t in range(TT):
                for n in range(2):
                    sp.wait_ge(o_done, 2 * t + n + 1)
                    sp.dma_start(out[t * P:(t + 1) * P, n * 512:(n + 1) * 512],
                                 h_gain[t][:, n * 512:(n + 1) * 512]).then_inc(s_out, 16)
            sp.wait_ge(s_out, 16 * 2 * TT)

        @block.gpsimd
        def _(pool):
            nc.gpsimd.memset(gn_eps[:, :], 64e-5).then_inc(eps_done, 1)
            nc.gpsimd.memset(r1[:, 0, :], 0.0).then_inc(warm_zero, 1)
            nc.gpsimd.memset(pad_w[:, 0:1], 0.0).then_inc(zeroed, 1)
            nc.gpsimd.memset(pad_a[:, :, 0:1], 0.0).then_inc(zeroed, 1)
            nc.gpsimd.memset(pad_b[:, :, 0:1], 0.0).then_inc(zeroed, 1)
            nc.gpsimd.memset(v1[:, :, 0:C], 0.0).then_inc(zeroed, 1)
            nc.gpsimd.memset(pinc[:, :, 0:1], 1.0).then_inc(zeroed, 1)
            nc.gpsimd.memset(sav[0:C, :, :, :], 0.0).then_inc(zeroed, 1)
            def split_lo(n):
                pool.wait_ge(hi_done, n + 1)
                nc.gpsimd.tensor_tensor(w_lo[n % SLOTS][:, :, :], w_raw[n % RAW_SLOTS][:, :, :],
                                        w_hi[n % SLOTS][:, :, :].bitcast(f32), ALU.subtract).then_inc(lo_pool, 1)

            for n in range(LEAD):
                if not on_dve(n):
                    split_lo(n)
            for item in ORDER:
                if item[0] == "w":
                    n = piece_number(item) + LEAD
                    if n < len(PIECES) and not on_dve(n):
                        split_lo(n)
                elif item[0] == "clear":
                    pool.wait_ge(bk_done, 2)
                    taken(pool, "xT", KC // 2 - 1)
                    nc.gpsimd.memset(y_sb[:, :, :], 0.0).then_inc(y_zero, 1)
                    nc.gpsimd.memset(t_inv, 0.0).then_inc(tu_zero, 1)
                    nc.gpsimd.memset(u_inv, 0.0).then_inc(tu_zero, 1)
                elif item[0] == "masks":
                    taken(pool, "A", 0)
                    taken(pool, "A", 1)
                    for m, dst in (("low16", b16), ("low32", b32)):
                        nc.gpsimd.tensor_tensor(dst, a_neg, cn(m).unsqueeze(1).to_broadcast([P, UNITS, C]),
                                                ALU.mult).then_inc(low_done, 1)

        @block.scalar
        def _(act):
            A = nc.scalar.activation

            def split_hi(n):
                act.wait_ge(s_raw[n % RAW_SLOTS], 16 * (n // RAW_SLOTS + 1))
                if n >= SLOTS:
                    piece_used(act, n - SLOTS)
                A(w_hi[n % SLOTS][:, :, :], w_raw[n % RAW_SLOTS][:, :, :], ACT.Copy).then_inc(hi_done, 1)

            def halves(bank):
                return bank[:, :].rearrange("p (a b) -> p a b", a=2)

            def copy_out(job, dst, src, **kw):
                bank = full_bank(act, job)
                empty(A(dst, src(bank), ACT.Copy, **kw), job)

            def pairs_v(bank):
                return bank[:, 0:PAIRS * C].rearrange("p (a v) -> p a v", a=PAIRS)

            def tiles_v(bank):
                return bank[:, :].rearrange("p (a v) -> p a v", a=PAIRS)

            act.wait_ge(eps_done, 1)
            A(fin[:, 0, 0:1], gn_eps[:, 0:1], ACT.Sqrt).then_inc(table_in, 1)
            for t in range(TT):
                act.wait_ge(s_x[t], 16)
                A((k1, cs)[t][:, :, :].rearrange("p a b -> p (a b)"), xt[:, t, :], ACT.Square, accum_out=stat[:, t:t + 1]).then_inc(ss_done, 1)
                act.wait_ge(ms_done, t + 1)
                A(stat[:, 4 + t:5 + t], stat[:, 2 + t:3 + t], ACT.Sqrt).then_inc(sq_done, 1)
            split_hi(0)
            split_hi(1)
            act.wait_ge(s_ident, 32)

            def act_part(item):
                kind, a = item[0], item[1:]
                if kind == "xT":
                    bank = full_bank(act, item)
                    for i in range(2):
                        k = 2 * a[0] + i
                        ins = A(u_hi[:, k, :], bank[:, i * SEQ:(i + 1) * SEQ], ACT.Copy, scale=pm("norm_gain", k))
                    ins.then_inc(u_hi_done, 1)
                    if a[0] == 3:
                        split_hi(2)
                        split_hi(3)
                elif kind == "w":
                    if piece_number(item) + LEAD < len(PIECES):
                        split_hi(piece_number(item) + LEAD)
                elif item == ("take", "wd"):
                    act.wait_ge(zeroed, 6)
                    copy_out(("wd", 0), pad_w[:, 1:SEQ + 1], lambda b: b[:, 0:SEQ])
                    act.wait_ge(wd_done, 1)
                    A(wd[0:64, :], wd[0:64, :], ACT.Tanh).then_inc(wd_tanh, 1)
                elif kind == "take" and a[0] in ("k", "r", "v"):
                    pad = pad_b if a[0] == "r" else pad_a
                    if a[0] == "v":
                        act.wait_ge(k1_done, PAIRS)
                    for j in range(2):
                        copy_out((a[0], j), pad[:, 2 * j:2 * j + 2, 1:SEQ + 1], halves)
                elif kind in ("upw", "upa"):
                    act.wait_ge(drv_done, 5)
                    bank = full_bank(act, item)
                    for i in range(2):
                        p = 2 * a[0] + i
                        dst, bias = (thw, HALF_DB) if kind == "upw" else (tha, HALF_IB)
                        ins = A(dst[:, p, :], bank[:, i * SEQ:(i + 1) * SEQ], ACT.Tanh, scale=0.5, bias=drv[:, bias, p:p + 1])
                    empty(ins, item)
                elif kind == "decay":
                    act.wait_ge(cs_done, PAIRS)
                    cs_u = cs[:, :, :].rearrange("p a (b c) -> p (a b) c", c=C)
                    A(pinc[:, :, 1:C + 1], cs_u, ACT.Exp, scale=-DECAY).then_inc(pinc_done, 1)
                    A(cs_u, cs_u, ACT.Exp, scale=DECAY).then_inc(pinv_done, 1)
                elif kind == "sq":
                    for p in range(PAIRS):
                        act.wait_ge(k1_done, p + 1)
                        A(rn[:, p, :], k1[:, p, :], ACT.Square, scale=pm("k_k", p)).then_inc(kk_sq, 1)
                elif kind == "kk":
                    taken(act, "kn", 0)
                    taken(act, "kn", 1)
                    A(rn[:, :, :], rn[:, :, :], ACT.Sqrt).then_inc(kk_root, 1)
                elif kind in ("qT", "kT"):
                    copy_out(item, (qT if kind == "qT" else kT)[:, 2 * a[0]:2 * a[0] + 2, :], halves)
                elif item == ("take", "av"):
                    act.wait_ge(rk_prod, 1)
                    for t in range(TT):
                        copy_out(("av", t), v_att[:, t, :], lambda b: b[:, :])
                elif kind == "vT":
                    if a[0] >= 2:
                        taken(act, "Yc", a[0] - 2)
                        taken(act, "St", a[0] - 2)
                    copy_out(item, sav[C:P, a[0] % 2, :, :], lambda b: b[C:P, :].rearrange("p (h v) -> p h v", h=HEADS))
                elif kind == "bT":
                    copy_out(item, bkt[:, a[0] % 2, :, :], lambda b: b[:, :].rearrange("p (h v) -> p h v", h=HEADS))
                elif kind == "S":
                    for h in (2 * a[0], 2 * a[0] + 1):
                        act.wait_ge(nmax, h + 1)
                        for t in range(TT):
                            lo, hi = (0, P) if t == 0 else (P, 3 * P)
                            A(pr[:, h % 2, lo:hi], pr[:, h % 2, lo:hi], ACT.Exp, scale=HEAD ** -0.5,
                              bias=amax[:, h, 1, t:t + 1], accum_out=amax[:, h, 2, t:t + 1]).then_inc(exp_done, 1)
                elif kind == "PT":
                    act.wait_ge(v1_done, PAIRS)
                    if a[0] >= 2:
                        taken(act, "PV", (a[0] - 2) // 2)
                    copy_out(item, prT[:, a[0] % 2, :], lambda b: b[:, 0:3 * P])
                elif kind == "PV":
                    taken(act, "PV", a[0])
                    taken(act, "U2", 1)
                    A(y_hi[:, a[0], :], ya[:, a[0] % 2, :], ACT.Copy).then_inc(ya_hi, 1)
                elif kind in ("Y1", "Y2"):
                    if kind == "Y2":
                        taken(act, "U1", a[0])
                        copy_out(item, upper32(y_sb[:, 8 * a[0]:8 * a[0] + 8, :]), filled32)
                    else:
                        act.wait_ge(y_zero, 1)
                        copy_out(item, upper16(y_sb[:, 8 * a[0]:8 * a[0] + 8, :]), filled16)
                elif item in (("take", "ga"), ("take", "gb")):
                    dst = g_a if a[0] == "ga" else g_b
                    if a[0] == "ga":
                        taken(act, "qT", 1)
                    for j in range(2):
                        bank = full_bank(act, (a[0], j))
                        A(dst[:, 2 * j:2 * j + 2, :], halves(bank), ACT.Tanh, scale=0.5).then_inc(gth, 1)
                elif kind == "R":
                    if a[0]:
                        taken(act, "SA", 2 * a[0] - 1)
                    copy_out(item, r_neg[:, :, :], pairs_v, scale=-1.0)
                elif kind == "Yc":
                    copy_out(item, yc[:, :, a[0] * C:(a[0] + 1) * C], pairs_v)
                elif kind == "mid":
                    bank = full_bank(act, item)
                    A(gn_r[:, a[0], :, :], tiles_v(bank), ACT.Square).then_inc(csq_done, 1)
                elif kind == "var":
                    bank = full_bank(act, item)
                    empty(A(gn_r[:, a[0], :, :], tiles_v(bank), ACT.Sqrt, bias=gn_eps[:, 0:1]), item)
                elif kind == "gn":
                    t, j = a
                    tok = slice(t * P, (t + 1) * P)
                    act.wait_ge(y_done, 2 * t + j + 1)
                    A(y_hi[:, PAIRS + 2 * j:PAIRS + 2 * j + 2, tok], yc[:, 2 * j:2 * j + 2, tok], ACT.Copy).then_inc(yb_hi, 1)
                elif item == ("take", "out"):
                    for t in range(TT):
                        for n in range(2):
                            taken(act, "out", t, n)
                            A(lr[:, t, 4 * n:4 * n + 4, :].rearrange("p h n -> p (h n)"), x_res[:, t, n * 512:(n + 1) * 512],
                              ACT.Square, accum_out=fin[:, n, t:t + 1]).then_inc(fs_done, 1)
                        act.wait_ge(fm_done, 2 * t + 2)
                        A(stat[:, 4 + t:5 + t], stat[:, 2 + t:3 + t], ACT.Sqrt).then_inc(fr_done, 1)

            for item in ORDER:
                act_part(item)

        @block.vector
        def _(dve):
            V = nc.vector

            def halves(bank):
                return bank[:, :].rearrange("p (a b) -> p a b", a=2)

            def pairs_v(bank):
                return bank[:, 0:PAIRS * C].rearrange("p (a v) -> p a v", a=PAIRS)

            def tiles_v(bank):
                return bank[:, :].rearrange("p (a v) -> p a v", a=PAIRS)

            def split_lo(n):
                dve.wait_ge(hi_done, n + 1)
                V.tensor_tensor(w_lo[n % SLOTS][:, :, :], w_raw[n % RAW_SLOTS][:, :, :],
                                w_hi[n % SLOTS][:, :, :].bitcast(f32), ALU.subtract).then_inc(lo_dve, 1)

            for t in range(TT):
                dve.wait_ge(ss_done, t + 1)
                V.tensor_scalar(stat[:, 2 + t:3 + t], stat[:, t:t + 1], 1.0 / D_MODEL, 1e-6, ALU.mult, ALU.add).then_inc(ms_done, 1)
                dve.wait_ge(sq_done, t + 1)
                V.reciprocal(stat[:, 6 + t:7 + t], stat[:, 4 + t:5 + t]).then_inc(rstd_done, 1)
                dve.wait_ge(rstd_done, t + 1)
                V.tensor_scalar(xn[t], xt[:, t, :], stat[:, 6 + t:7 + t], None, ALU.mult).then_inc(xn_done, 1)
            split_lo(0)
            dve.wait_ge(s_ident, 32)
            for i, (name, s, o) in enumerate((("decay_bias", 0.5, 0.0), ("iclr_bias", 0.5, 0.0), ("k_a", 0.5, 0.0),
                                              ("k_a", -0.5, 1.0), ("gn_gain", 0.5, 0.0))):
                V.tensor_scalar(drv[:, i, :], pm_all(name), s, o, ALU.mult, ALU.add).then_inc(drv_done, 1)
            def shift(pad, mu, dst, off, kind, n_dif, done, after=None):
                taken(dve, kind, 0)
                taken(dve, kind, 1)
                dve.wait_ge(*after)
                V.tensor_tensor(dif[:, :, :], pad[:, :, 0:SEQ], pad[:, :, 1:SEQ + 1], ALU.subtract).then_inc(dif_done, 1)
                dve.wait_ge(dif_done, n_dif)
                for p in range(PAIRS):
                    V.scalar_tensor_tensor(dst[:, p, off:off + SEQ], dif[:, p, :], pm(mu, p), pad[:, p, 1:SEQ + 1],
                                           ALU.mult, ALU.add).then_inc(done, 1)

            def units(t):
                return t[:, :, :].rearrange("p a (b c) -> p (a b) c", c=C)

            def rotate(kind, t, dst, n):
                bank = full_bank(dve, (kind, t))
                v = bank[:, :].rearrange("p (h d) -> p h d", d=HEAD)
                cos = cn("cos")[:, t * HEAD:(t + 1) * HEAD].unsqueeze(1).to_broadcast([P, HEADS, HEAD])
                sin = cn("sin")[:, t * HEAD:(t + 1) * HEAD].unsqueeze(1).to_broadcast([P, HEADS, HEAD])
                o = dst[:, t, :].rearrange("p (h d) -> p h d", d=HEAD)
                tmp = rtmp[:, (n % 2) * WIDTH:(n % 2 + 1) * WIDTH].rearrange("p (h d) -> p h d", d=HEAD)
                H2 = HEAD // 2
                if n >= 2:
                    dve.wait_ge(rot_done, n - 1)
                V.tensor_tensor(o, v, cos, ALU.mult)
                V.tensor_tensor(tmp[:, :, 0:H2], v[:, :, H2:HEAD], sin[:, :, 0:H2], ALU.mult)
                empty(V.tensor_tensor(tmp[:, :, H2:HEAD], v[:, :, 0:H2], sin[:, :, H2:HEAD], ALU.mult), (kind, t))
                taken(dve, kind, t)
                V.tensor_tensor(o, o, tmp, ALU.add).then_inc(rot_done, 1)

            T_in = blk[:, 1, :].rearrange("p (i j) -> p i j", i=BASE)
            T_tr = blk[:, 1, :].rearrange("p (i j) -> p j i", i=BASE)

            def invert(first, last):
                neg = blk[:, 0, :].rearrange("p (i j) -> p i j", i=BASE)
                prod = blk[:, 3, :].rearrange("p (i j) -> p i j", i=BASE)
                if first == 1:
                    V.tensor_copy(blk[:, 1, :], cn("block_eye")).then_inc(inv_step, 1)
                    dve.wait_ge(s_gather, 16 * 8)
                for i in range(first, last):
                    dve.wait_ge(inv_step, 2 * i - 1)
                    V.tensor_tensor(prod[:, 0:i, 0:i], T_tr[:, 0:i, 0:i], neg[:, i:i + 1, 0:i].to_broadcast([P, i, i]),
                                    ALU.mult).then_inc(inv_step, 1)
                    dve.wait_ge(inv_step, 2 * i)
                    V.tensor_reduce(T_in[:, i, 0:i], prod[:, 0:i, 0:i], AX.X, ALU.add).then_inc(inv_step, 1)
                if last == BASE:
                    dve.wait_ge(inv_step, 2 * BASE - 1)
                    V.tensor_copy(blk[:, 2, :].rearrange("p (i j) -> p i j", i=BASE), T_tr).then_inc(inv_done, 1)

            def dve_part(item):
                kind, a = item[0], item[1:]
                if kind == "xT":
                    dve.wait_ge(u_hi_done, a[0] + 1)
                    bank = banks[PLACE[item][0]]
                    for i in range(2):
                        k = 2 * a[0] + i
                        ins = V.scalar_tensor_tensor(u_lo[:, k, :], bank[:, i * SEQ:(i + 1) * SEQ], pm("norm_gain", k),
                                                     u_hi[:, k, :].bitcast(f32), ALU.mult, ALU.subtract)
                    empty(ins, item)
                elif kind == "w":
                    n = piece_number(item) + LEAD
                    if n < len(PIECES) and on_dve(n):
                        split_lo(n)
                elif item == ("take", "wd"):
                    taken(dve, "wd", 0)
                    V.tensor_tensor(dif[:, 0, :], pad_w[:, 0:SEQ], pad_w[:, 1:SEQ + 1], ALU.subtract).then_inc(dif_done, 1)
                    dve.wait_ge(dif_done, 1)
                    V.scalar_tensor_tensor(wd[:, :], dif[:, 0, :], pm("mu_w"), pad_w[:, 1:SEQ + 1], ALU.mult, ALU.add).then_inc(wd_done, 1)
                    dve.wait_ge(s_const, 16)
                    for p in range(PAIRS):
                        V.tensor_scalar(head_rk[:, p, :], cn("head_sum"), pm("r_k", p), None, ALU.mult).then_inc(head_rk_done, 1)
                elif kind == "decay":
                    for p in range(PAIRS):
                        taken(dve, "upw", p // 2)
                        V.tensor_scalar(thw[:, p, :], thw[:, p, :], 1.0, None, ALU.add).then_inc(thw1_done, 1)
                    for p in range(PAIRS):
                        dve.wait_ge(thw1_done, p + 1)
                        V.tensor_tensor_scan(cs[:, p, :], cn("scan"), thw[:, p, :], 0.0, ALU.mult, ALU.add).then_inc(cs_done, 1)
                    for p in range(PAIRS):
                        taken(dve, "upa", p // 2)
                        V.tensor_scalar(kp[:, p, :], tha[:, p, :], drv[:, HALF_KA, p:p + 1], drv[:, ONE_KA, p:p + 1],
                                        ALU.mult, ALU.add).then_inc(kgain_done, 1)
                    dve.wait_ge(kgain_done, PAIRS)
                    V.tensor_scalar(tha[:, :, :], tha[:, :, :], 0.5, 0.5, ALU.mult, ALU.add).then_inc(a_done, 1)
                elif item == ("take", "k"):
                    shift(pad_a, "mu_k", k1, 0, "k", 2, k1_done, (wd_done, 1))
                elif kind == "sq":
                    dve.wait_ge(k1_done, PAIRS)
                    for p in range(PAIRS):
                        V.tensor_scalar(kk[:, p, :], k1[:, p, :], pm("k_k", p), None, ALU.mult).then_inc(kk_raw, 1)
                    dve.wait_ge(kgain_done, PAIRS)
                    V.tensor_tensor(kp[:, :, :], kp[:, :, :], k1[:, :, :], ALU.mult).then_inc(kp_done, 1)
                elif kind == "kn":
                    bank = full_bank(dve, item)
                    empty(V.tensor_scalar(rn[:, 2 * a[0]:2 * a[0] + 2, :], halves(bank), 1e-24, None, ALU.max), item)
                elif kind == "kk":
                    dve.wait_ge(pinv_done, 1)
                    dve.wait_ge(kp_done, 1)
                    taken(dve, "xT", KC // 2 - 1)
                    V.tensor_tensor(bk[:, :, 1, :], units(kp), units(cs), ALU.mult).then_inc(bk_done, 1)
                    dve.wait_ge(kk_root, 1)
                    V.reciprocal(rn[:, :, :], rn[:, :, :]).then_inc(kk_inv, 1)
                    dve.wait_ge(kk_inv, 1)
                    dve.wait_ge(kk_raw, PAIRS)
                    V.tensor_tensor(kk[:, :, :], kk[:, :, :], rn[:, :, :], ALU.mult).then_inc(kk_done, 1)
                    dve.wait_ge(kk_done, 1)
                    V.tensor_tensor(tha[:, :, :], tha[:, :, :], kk[:, :, :], ALU.mult).then_inc(b_done, 1)
                    dve.wait_ge(pinc_done, 1)
                    V.tensor_tensor(kr[:, :, 0, :], units(kk), pinc[:, :, 0:C], ALU.mult).then_inc(kr_done, 1)
                    dve.wait_ge(b_done, 1)
                    V.tensor_tensor(bk[:, :, 0, :], units(tha), units(cs), ALU.mult).then_inc(bk_done, 1)
                elif item == ("take", "r"):
                    shift(pad_b, "mu_r", r1, 0, "r", 3, r1_done, (k1_done, PAIRS))
                elif kind == "rk":
                    dve.wait_ge(r1_done, PAIRS)
                    V.tensor_tensor(kr[:, :, 1, :], units(r1), pinc[:, :, 1:C + 1], ALU.mult).then_inc(kr_done, 1)
                    V.tensor_tensor(k1[:, :, :], r1[:, :, :], kp[:, :, :], ALU.mult).then_inc(rk_prod, 1)
                elif item == ("take", "v"):
                    shift(pad_a, "mu_v", v1, C, "v", 4, v1_done, (r1_done, PAIRS))
                elif item in (("take", "aq"), ("take", "ak")):
                    dve.wait_ge(v1_done, PAIRS)
                    dve.wait_ge(rk_prod, 1)
                    for t in range(TT):
                        rotate(a[0], t, rot if a[0] == "aq" else rot_k, t + (0 if a[0] == "aq" else TT))
                elif kind == "bonus":
                    bank = full_bank(dve, item)
                    j = a[0]
                    dve.wait_ge(v1_done, PAIRS)
                    empty(V.tensor_tensor(bonus[:, 2 * j:2 * j + 2, :], halves(bank), v1[:, 2 * j:2 * j + 2, C:C + SEQ],
                                          ALU.mult), item)
                    if j == 1:
                        taken(dve, "bonus", 1)
                        for p in range(PAIRS):
                            V.tensor_scalar(bonus[:, p, :], bonus[:, p, :], pm("gn_bias", p), None, ALU.add).then_inc(bonus_done, 1)
                elif kind == "A":
                    bank = full_bank(dve, item)
                    j = a[0]
                    empty(V.tensor_tensor(a_neg[:, 8 * j:8 * j + 8, :], bank[:, :].rearrange("p (u c) -> p u c", c=C),
                                          cn("a_mask").unsqueeze(1).to_broadcast([P, 8, C]), ALU.mult), item)
                elif kind == "inv":
                    invert(*a)
                elif kind == "gram":
                    c = a[0]
                    if c >= 2:
                        taken(dve, "Yc", c - 2)
                    for par in range(2):
                        bank = full_bank(dve, ("gram", 2 * c + par))
                        heads = lr[:, c % 2, :, :].rearrange("p (a b) n -> p a b n", b=2)[:, :, par, :]
                        empty(V.tensor_tensor(heads, bank[:, :].rearrange("p (a n) -> p a n", a=PAIRS),
                                              cn("gram_mask").unsqueeze(1).to_broadcast([P, PAIRS, P]), ALU.mult),
                              ("gram", 2 * c + par))
                elif kind == "S":
                    dve.wait_ge(rot_done, 2 * TT)
                    for h in (2 * a[0], 2 * a[0] + 1):
                        bank = full_bank(dve, ("S", h))
                        if h >= 2:
                            taken(dve, "PT", h - 2)
                        for t in range(TT):
                            lo, hi = (0, P) if t == 0 else (P, 3 * P)
                            ins = V.tensor_tensor_reduce(out=pr[:, h % 2, lo:hi], in0=bank[:, lo:hi], in1=cn("causal")[:, lo:hi],
                                                         scale=1.0, scalar=-3.0e38, op0=ALU.add, op1=ALU.max,
                                                         accum_out=amax[:, h, 0, t:t + 1])
                        empty(ins, ("S", h))
                        taken(dve, "S", h)
                        V.tensor_scalar(amax[:, h, 1, :], amax[:, h, 0, :], -HEAD ** -0.5, None, ALU.mult).then_inc(nmax, 1)
                elif kind == "norm":
                    h = a[0]
                    dve.wait_ge(exp_done, TT * (h + 1))
                    V.reciprocal(amax[:, h, 0, :], amax[:, h, 2, :]).then_inc(rsum_done, 1)
                    dve.wait_ge(rsum_done, h + 1)
                    for t in range(TT):
                        lo, hi = (0, P) if t == 0 else (P, 3 * P)
                        V.tensor_scalar(pr[:, h % 2, lo:hi], pr[:, h % 2, lo:hi], amax[:, h, 0, t:t + 1], None,
                                        ALU.mult).then_inc(pr_done, 1)
                elif kind == "PV":
                    p = a[0]
                    bank = full_bank(dve, item)
                    taken(dve, "ga", 1)
                    y = ya[:, p % 2, :]
                    empty(V.scalar_tensor_tensor(y, bank[:, 0:SEQ], 0.5, g_a[:, p, :], ALU.mult, ALU.mult), item)
                    dve.wait_ge(ya_hi, p + 1)
                    V.tensor_tensor(y_lo[:, p, :], y, y_hi[:, p, :].bitcast(f32), ALU.subtract).then_inc(ya_lo, 1)
                elif kind in ("T1", "U1", "U2"):
                    half = a[0]
                    if kind == "T1":
                        b, turn = PLACE[("U1", half)]
                        dve.wait_ge(filled[b], turn + 1)
                    bank = full_bank(dve, item)
                    d = (t_inv if kind == "T1" else u_inv)[:, 8 * half:8 * half + 8, :]
                    d = {"T1": lower16, "U1": upper16, "U2": upper32}[kind](d)
                    empty(V.tensor_tensor(d, (filled32 if kind == "U2" else filled16)(bank), d, ALU.add), item)
                elif item in (("take", "ga"), ("take", "gb")):
                    dst, n = (g_a, 1) if a[0] == "ga" else (g_b, 3)
                    for j in range(2):
                        dve.wait_ge(gth, n + j)
                        bank = full_bank(dve, (a[0], j))
                        d = dst[:, 2 * j:2 * j + 2, :]
                        empty(V.scalar_tensor_tensor(d, d, 1.0, halves(bank), ALU.add, ALU.mult), (a[0], j))
                    if a[0] == "gb":
                        taken(dve, "gb", 1)
                        dve.wait_ge(bonus_done, PAIRS)
                        V.scalar_tensor_tensor(bonus[:, :, :], bonus[:, :, :], 0.5, g_b[:, :, :], ALU.mult, ALU.mult).then_inc(bonus_done, 1)
                        dve.wait_ge(bonus_done, 1 + PAIRS)
                        for p in range(PAIRS):
                            V.tensor_scalar(g_b[:, p, :], g_b[:, p, :], drv[:, HALF_GAIN, p:p + 1], None, ALU.mult).then_inc(gb_done, 1)
                elif kind == "SA":
                    c = a[0]
                    if c >= 2:
                        taken(dve, "Yc", c - 2)
                        taken(dve, "St", c - 2)
                    for par in range(2):
                        bank = full_bank(dve, ("SA", 2 * c + par))
                        heads = sav[0:C, c % 2, :, :].rearrange("p (a b) v -> p a b v", b=2)[:, :, par, :]
                        empty(V.tensor_copy(heads, bank[0:C, 0:PAIRS * C].rearrange("p (a v) -> p a v", a=PAIRS)),
                              ("SA", 2 * c + par))
                elif kind == "St":
                    c = a[0]
                    bank = full_bank(dve, item)
                    new, old = state[:, (c + 1) % 2, :, :], state[:, c % 2, :, :]
                    p_end = pinc[:, :, C:C + 1].rearrange("p (a b) o -> p a b o", b=CHUNKS)[:, :, c, :].to_broadcast([P, PAIRS, C])
                    if c >= 1:
                        taken(dve, "Yc", c - 1)
                    if c == 0:
                        empty(V.tensor_tensor(new, pairs_v(bank), p_end, ALU.mult), item)
                    else:
                        state_ready(dve, c - 1)
                        empty(V.tensor_tensor(new, pairs_v(bank), old, ALU.add), item)
                        taken(dve, "St", c)
                        V.tensor_tensor(new, new, p_end, ALU.mult).then_inc(st_done, 1)
                elif kind == "mid":
                    t = a[0]
                    bank = full_bank(dve, item)
                    dve.wait_ge(gb_done, PAIRS)
                    dve.wait_ge(csq_done, t + 1)
                    if t:
                        dve.wait_ge(gn_step, 2)
                    empty(V.tensor_tensor(yz[:, :, :], tiles_v(bank), g_b[:, :, t * P:(t + 1) * P], ALU.mult), item)
                elif kind == "gn":
                    t, j = a
                    tok, pairs = slice(t * P, (t + 1) * P), slice(2 * j, 2 * j + 2)
                    y, g = yc[:, pairs, tok], gn_r[:, t, pairs, :]
                    taken(dve, "var", t)
                    V.reciprocal(g, g).then_inc(ginv, 1)
                    dve.wait_ge(ginv, 2 * t + j + 1)
                    taken(dve, "mid", t)
                    V.tensor_tensor(y, yz[:, pairs, :], g, ALU.mult).then_inc(gn_step, 1)
                    dve.wait_ge(gn_step, 2 * t + j + 1)
                    dve.wait_ge(bonus_done, 1 + PAIRS)
                    V.tensor_tensor(y, y, bonus[:, pairs, tok], ALU.add).then_inc(y_done, 1)
                    dve.wait_ge(yb_hi, 2 * t + j + 1)
                    V.tensor_tensor(y_lo[:, PAIRS + 2 * j:PAIRS + 2 * j + 2, tok], y,
                                    y_hi[:, PAIRS + 2 * j:PAIRS + 2 * j + 2, tok].bitcast(f32), ALU.subtract).then_inc(yb_lo, 1)
                elif item == ("take", "out"):
                    dve.wait_ge(s_res, 16)
                    for t in range(TT):
                        for n in range(2):
                            bank = full_bank(dve, ("out", t, n))
                            h = x_res[:, t, n * 512:(n + 1) * 512]
                            empty(V.tensor_tensor(h, bank[:, :], h, ALU.add), ("out", t, n))
                            taken(dve, "out", t, n)
                            dve.wait_ge(s_fg, 16)
                            col = slice(n * 512, (n + 1) * 512)
                            V.tensor_tensor(h_gain[t][:, col], h, fgain[:, col], ALU.mult).then_inc(hg_done, 1)
                        dve.wait_ge(fs_done, 2 * t + 2)
                        V.tensor_tensor(stat[:, t:t + 1], fin[:, 0, t:t + 1], fin[:, 1, t:t + 1], ALU.add).then_inc(fm_done, 1)
                        dve.wait_ge(fm_done, 2 * t + 1)
                        V.tensor_scalar(stat[:, 2 + t:3 + t], stat[:, t:t + 1], 1.0 / D_MODEL, 1e-6, ALU.mult, ALU.add).then_inc(fm_done, 1)
                        dve.wait_ge(fr_done, t + 1)
                        V.reciprocal(stat[:, 6 + t:7 + t], stat[:, 4 + t:5 + t]).then_inc(fi_done, 1)
                        dve.wait_ge(fi_done, t + 1)
                        dve.wait_ge(hg_done, 2 * t + 2)
                        for n in range(2):
                            o = h_gain[t][:, n * 512:(n + 1) * 512]
                            V.tensor_scalar(o, o, stat[:, 6 + t:7 + t], None, ALU.mult).then_inc(o_done, 1)

            for item in ORDER:
                dve_part(item)

        @block.tensor
        def _(pe):
            mm = nc.tensor.matmul

            def rows(par):
                return slice(64 * par, 64 * par + 64)

            def split_mm(out, a_hi, a_lo, b_hi, b_lo, first, last):
                mm(out, a_hi, b_hi, start=first, stop=False, skip_group_check=True)
                mm(out, a_lo, b_hi, start=False, stop=False, skip_group_check=True)
                return mm(out, a_hi, b_lo, start=False, stop=last, skip_group_check=True)

            def out_project(q, tiles):
                half, kp2, n = q % 2, q // 2, PIECES.index(("wo", q))
                hi, lo = w_hi[n % SLOTS], w_lo[n % SLOTS]
                if kp2 == 0:
                    pe.wait_ge(ya_lo, PAIRS)
                for t in tiles:
                    job = ("out", t, half)
                    bank = free_bank(pe, job) if kp2 == 0 else banks[PLACE[job][0]]
                    if kp2 >= 2:
                        pe.wait_ge(yb_lo, 2 * t + kp2 - 1)
                    tok = slice(t * P, (t + 1) * P)
                    for i in range(2):
                        k = 2 * kp2 + i
                        ins = split_mm(bank[:, :], y_hi[:, k, tok], y_lo[:, k, tok], hi[:, i, :], lo[:, i, :], k == 0, k == KC - 1)
                    if kp2 == 3:
                        fill(ins, job)
                if kp2 < 2:
                    ins.then_inc(w_used, 1)

            def project(item):
                _, name, q = item
                n = piece_number(item)
                last_piece = q == LAST_PIECE[name]
                hi, lo = w_hi[n % SLOTS], w_lo[n % SLOTS]
                lo_ready(pe, n)
                if name == "wd":
                    bank = free_bank(pe, ("wd", 0))
                    h8, l8 = (t[:, :, :].rearrange("p a (b n) -> p (a b) n", n=P) for t in (hi, lo))
                    for k in range(KC):
                        pe.wait_ge(u_hi_done, k // 2 + 1)
                        mm(bank[:, 0:SEQ], h8[:, k, :], u_hi[:, k, :], start=(k == 0), stop=False)
                        mm(bank[:, 0:SEQ], l8[:, k, :], u_hi[:, k, :], start=False, stop=False)
                    for k in range(KC):
                        taken(pe, "xT", k // 2)
                        ins = mm(bank[:, 0:SEQ], h8[:, k, :], u_lo[:, k, :], start=False, stop=(k == KC - 1))
                    fill(ins, ("wd", 0))
                elif name == "wo":
                    out_project(q, range(TT) if q < 4 else [0])
                else:
                    by_channel = name in ("k", "r", "v", "ga", "gb")
                    if q == 0:
                        free_bank(pe, (name, 0))
                        free_bank(pe, (name, 1))
                    for j in range(2):
                        bank = banks[PLACE[(name, j)][0]]
                        for i in range(2):
                            k = 2 * q + i
                            if by_channel:
                                for m in range(2):
                                    ch = (2 * j + m) * P
                                    ins = split_mm(bank[:, m * SEQ:(m + 1) * SEQ], hi[:, i, ch:ch + P], lo[:, i, ch:ch + P],
                                                   u_hi[:, k, :], u_lo[:, k, :], k == 0 and m == 0, k == KC - 1)
                            else:
                                tok = slice(j * P, (j + 1) * P)
                                ins = split_mm(bank[:, :], u_hi[:, k, tok], u_lo[:, k, tok], hi[:, i, :], lo[:, i, :], k == 0, k == KC - 1)
                        if last_piece:
                            fill(ins, (name, j))
                    if not last_piece:
                        ins.then_inc(w_used, 1)

            def x_transposed(j):
                for t, js in (((0, range(KC // 2)), (1, (j,))) if j == 0 else ((1, (j,)),)):
                    pe.wait_ge(s_ident, 32)
                    pe.wait_ge(xn_done, t + 1)
                    for jj in js:
                        bank = free_bank(pe, ("xT", jj))
                        for i in range(2):
                            at = i * SEQ + t * P
                            ins = nc.tensor.transpose(bank[:, at:at + P], xn[t][:, (2 * jj + i) * P:(2 * jj + i + 1) * P],
                                                      cn("ident"))
                fill(ins, ("xT", j))

            def up_project(kind, j):
                bank = free_bank(pe, (kind, j))
                pe.wait_ge(s_up, 16)
                pe.wait_ge(wd_done, 1)
                pe.wait_ge(wd_tanh, 1)
                r = rows(0 if kind == "upw" else 1)
                for i in range(2):
                    ch = (2 * j + i) * P
                    ins = mm(bank[:, i * SEQ:(i + 1) * SEQ], up_sb[r, ch:ch + P], wd[r, :], start=True, stop=True)
                fill(ins, (kind, j))

            def head_sums(kind, j):
                bank = free_bank(pe, (kind, j))
                if kind == "kn":
                    pe.wait_ge(kk_sq, 2 * j + 2)
                    ins = mm(bank[:, :], cn("head_sum"), rn[:, 2 * j:2 * j + 2, :].rearrange("p a b -> p (a b)"),
                             start=True, stop=True)
                else:
                    pe.wait_ge(rk_prod, 1)
                    pe.wait_ge(head_rk_done, PAIRS)
                    for i in range(2):
                        ins = mm(bank[:, i * SEQ:(i + 1) * SEQ], head_rk[:, 2 * j + i, :], k1[:, 2 * j + i, :],
                                 start=True, stop=True)
                fill(ins, (kind, j))

            def a_matrix(half):
                bank = free_bank(pe, ("A", half))
                pe.wait_ge(kr_done, 1)
                pe.wait_ge(bk_done, 2)
                for n in range(8):
                    c, p = 2 * half + n // PAIRS, n % PAIRS
                    u = p * CHUNKS + c
                    for par in range(2):
                        ins = mm(bank[rows(par), n * C:(n + 1) * C], kr[rows(par), u, 0, :], bk[rows(par), u, 0, :],
                                 start=True, stop=True)
                fill(ins, ("A", half))

            def transposed(kind, j, src):
                bank = free_bank(pe, (kind, j))
                for i in range(2):
                    for t in range(TT):
                        at = i * SEQ + t * P
                        ins = nc.tensor.transpose(bank[:, at:at + P], src[:, t, (2 * j + i) * P:(2 * j + i + 1) * P], cn("ident"))
                fill(ins, (kind, j))

            def v_tokens(c):
                bank = free_bank(pe, ("vT", c))
                pe.wait_ge(v1_done, PAIRS)
                pe.wait_ge(zeroed, 6)
                for p in range(PAIRS):
                    ins = nc.tensor.transpose(bank[:, p * P:(p + 1) * P], v1[:, p, c * C:c * C + P], cn("ident"))
                fill(ins, ("vT", c))

            def b_tokens(c):
                bank = free_bank(pe, ("bT", c))
                pe.wait_ge(bk_done, 2)
                for p in range(PAIRS):
                    src = bk[:, p * CHUNKS + c, :, :].rearrange("p s c -> p (s c)")
                    ins = nc.tensor.transpose(bank[:, p * P:(p + 1) * P], src, cn("ident"))
                fill(ins, ("bT", c))

            def gram(c):
                both = [free_bank(pe, ("gram", 2 * c + par)) for par in range(2)]
                pe.wait_ge(kr_done, 2)
                for p in range(PAIRS):
                    u = p * CHUNKS + c
                    for par in range(2):
                        ins = mm(both[par][:, p * P:(p + 1) * P], bk[rows(par), u, :, :].rearrange("p s c -> p (s c)"),
                                 kr[rows(par), u, :, :].rearrange("p s c -> p (s c)"), start=True, stop=True)
                        if p == PAIRS - 1:
                            fill(ins, ("gram", 2 * c + par))

            def scores(p):
                both = [free_bank(pe, ("S", 2 * p + par)) for par in range(2)]
                taken(pe, "qT", p // 2)
                taken(pe, "kT", p // 2)
                for par in range(2):
                    mm(both[par][:, 0:P], qT[rows(par), p, 0:P], kT[rows(par), p, 0:P], start=True, stop=True)
                for par in range(2):
                    fill(mm(both[par][:, P:3 * P], qT[rows(par), p, P:SEQ], kT[rows(par), p, :], start=True, stop=True),
                         ("S", 2 * p + par))

            def probs_T(h):
                bank = free_bank(pe, ("PT", h))
                pe.wait_ge(pr_done, TT * (h + 1))
                for i in range(3):
                    ins = nc.tensor.transpose(bank[:, i * P:(i + 1) * P], pr[:, h % 2, i * P:(i + 1) * P], cn("ident"))
                fill(ins, ("PT", h))

            def head_out(p):
                bank = free_bank(pe, ("PV", p))
                taken(pe, "PT", 2 * p)
                taken(pe, "PT", 2 * p + 1)
                taken(pe, "av", 0)
                taken(pe, "av", 1)
                heads = (2 * p, 2 * p + 1)
                for par, h in enumerate(heads):
                    mm(bank[rows(par), 0:SEQ], v_att[:, 0, h * HEAD:(h + 1) * HEAD], prT[:, par, 0:SEQ], start=True, stop=False)
                for par, h in enumerate(heads):
                    ins = mm(bank[rows(par), P:SEQ], v_att[:, 1, h * HEAD:(h + 1) * HEAD], prT[:, par, SEQ:3 * P],
                             start=False, stop=True)
                fill(ins, ("PV", p))

            def double(kind, half, lhs, rhs, cols):
                bank = free_bank(pe, (kind, half))
                for n in range(8):
                    u = 8 * half + n
                    for par in range(2):
                        ins = mm(bank[rows(par), n * C // 2:(n + 1) * C // 2], lhs[rows(par), u, :],
                                 cols(rhs[rows(par), u:u + 1, :]), start=True, stop=True)
                fill(ins, (kind, half))

            def right_side(c):
                bank = free_bank(pe, ("R", c))
                taken(pe, "gram", 2 * c)
                taken(pe, "gram", 2 * c + 1)
                taken(pe, "vT", c)
                for h in range(HEADS):
                    p, par = h // 2, h % 2
                    ins = mm(bank[rows(par), p * C:(p + 1) * C], lr[:, c % 2, h, 0:C], sav[:, c % 2, h, :],
                             start=(p == 0), stop=(c == 0), skip_group_check=True)
                if c:
                    state_ready(pe, c - 1)
                    for h in range(HEADS):
                        p, par = h // 2, h % 2
                        ins = mm(bank[rows(par), p * C:(p + 1) * C], kr[rows(par), p * CHUNKS + c, 0, :],
                                 state[rows(par), c % 2, p, :], start=False, stop=True, skip_group_check=True)
                fill(ins, ("R", c))

            def solve(c):
                both = [free_bank(pe, ("SA", 2 * c + par)) for par in range(2)]
                taken(pe, "R", c)
                taken(pe, "U2", c // 2)
                for p in range(PAIRS):
                    for par in range(2):
                        ins = mm(both[par][0:C, p * C:(p + 1) * C], u_inv[rows(par), c * PAIRS + p, :], r_neg[rows(par), p, :],
                                 start=True, stop=True)
                        if p == PAIRS - 1:
                            fill(ins, ("SA", 2 * c + par))

            def new_state(c):
                bank = free_bank(pe, ("St", c))
                taken(pe, "SA", 2 * c)
                taken(pe, "SA", 2 * c + 1)
                taken(pe, "bT", c)
                for h in range(HEADS):
                    p, par = h // 2, h % 2
                    ins = mm(bank[rows(par), p * C:(p + 1) * C], bkt[:, c % 2, h, :], sav[:, c % 2, h, :], start=True, stop=True)
                fill(ins, ("St", c))

            def chunk_out(c):
                bank = free_bank(pe, ("Yc", c))
                taken(pe, "SA", 2 * c)
                taken(pe, "SA", 2 * c + 1)
                for h in range(HEADS):
                    p, par = h // 2, h % 2
                    ins = mm(bank[rows(par), p * C:(p + 1) * C], sav[:, c % 2, h, :], lr[:, c % 2, h, C:P],
                             start=(p == 0), stop=(c == 0), skip_group_check=True)
                if c:
                    for h in range(HEADS):
                        p, par = h // 2, h % 2
                        ins = mm(bank[rows(par), p * C:(p + 1) * C], state[rows(par), c % 2, p, :],
                                 kr[rows(par), p * CHUNKS + c, 1, :], start=False, stop=True, skip_group_check=True)
                fill(ins, ("Yc", c))

            def center(t):
                bank = free_bank(pe, ("mid", t))
                taken(pe, "Yc", 2 * t)
                taken(pe, "Yc", 2 * t + 1)
                fill(mm(bank[:, :].rearrange("p (a v) -> p a v", a=PAIRS), cn("center"), yc[:, :, t * P:(t + 1) * P],
                        start=True, stop=True), ("mid", t))

            def var(t):
                bank = free_bank(pe, ("var", t))
                pe.wait_ge(csq_done, t + 1)
                fill(mm(bank[:, :], cn("head_mean"), gn_r[:, t, :, :].rearrange("p a v -> p (a v)"),
                        start=True, stop=True), ("var", t))

            pe.wait_ge(warm_zero, 1)
            for _ in range(WARM_UP):
                mm(banks[PROJ_BANKS[-1]][:, 0:SEQ], r1[:, 0, 0:P], r1[:, 0, :], start=True, stop=True)
            for item in ORDER:
                kind, args = item[0], item[1:]
                if kind == "xT":
                    x_transposed(*args)
                elif kind == "w":
                    project(item)
                elif kind == "w1":
                    out_project(args[1], [1])
                elif kind in ("upw", "upa"):
                    up_project(kind, *args)
                elif kind in ("kn", "bonus"):
                    head_sums(kind, *args)
                elif kind == "A":
                    a_matrix(*args)
                elif kind in ("qT", "kT"):
                    pe.wait_ge(rot_done, 2 if kind == "qT" else 4)
                    transposed(kind, *args, rot if kind == "qT" else rot_k)
                elif kind == "vT":
                    v_tokens(*args)
                elif kind == "bT":
                    b_tokens(*args)
                elif kind == "gram":
                    gram(*args)
                elif kind == "S":
                    scores(*args)
                elif kind == "PT":
                    probs_T(*args)
                elif kind == "PV":
                    head_out(*args)
                elif kind == "Y1":
                    pe.wait_ge(s_scatter, 16 * 16)
                    pe.wait_ge(low_done, 1)
                    pe.wait_ge(y_zero, 1)
                    double(kind, *args, b16, u_inv, upper16)
                elif kind == "T1":
                    taken(pe, "Y1", args[0])
                    double(kind, *args, y_sb, t_inv, lower16)
                elif kind == "U1":
                    double(kind, *args, t_inv, y_sb, upper16)
                elif kind == "Y2":
                    taken(pe, "U1", args[0])
                    pe.wait_ge(low_done, 2)
                    double(kind, *args, b32, u_inv, upper32)
                elif kind == "U2":
                    taken(pe, "T1", args[0])
                    taken(pe, "Y2", args[0])
                    double(kind, *args, t_inv, y_sb, upper32)
                elif kind == "R":
                    right_side(*args)
                elif kind == "SA":
                    solve(*args)
                elif kind == "St":
                    new_state(*args)
                elif kind == "Yc":
                    chunk_out(*args)
                elif kind == "mid":
                    center(*args)
                elif kind == "var":
                    var(*args)


def constants():
    a = np.zeros((P, N_CONST), np.float32)
    i = np.arange(P)

    def put(name, v):
        s, e = CONST[name]
        a[:, s:e] = v

    put("ident", np.eye(P))
    same = (i[:, None] // HEAD == i[None, :] // HEAD).astype(np.float32)
    put("head_sum", same)
    put("head_mean", same / HEAD)
    put("center", np.eye(P) - same / HEAD)
    j, t, col = i[:, None] % C, i[None, :] % C, i[None, :] // C
    g = np.where(col == 0, j < t, j <= t).astype(np.float32)
    g[0:C, 0:C] = 0
    put("gram_mask", g)
    r, q = i[:, None] % C, np.arange(C)[None, :]
    put("a_mask", np.where(q < r, -1.0, 0.0))
    put("low16", (r // 32 == q // 32) & (r % 32 >= 16) & (q % 32 < 16))
    put("low32", (r >= 32) & (q < 32))
    put("scan", (np.arange(SEQ) % C != 0)[None, :])
    causal = np.where(i[None, :] <= i[:, None], 0.0, -1e30)
    put("causal", np.concatenate([causal, np.zeros((P, P)), causal], 1))
    inv = 1.0 / (np.float32(10000.0) ** (np.arange(0, HEAD, 2, dtype=np.float32) / np.float32(HEAD)))
    ang = np.arange(SEQ, dtype=np.float32)[:, None] * inv[None, :].astype(np.float32)
    cos, sin = np.cos(ang), np.sin(ang)
    cos2, sin2 = np.concatenate([cos, cos], 1), np.concatenate([-sin, sin], 1)
    put("cos", cos2.reshape(TT, P, HEAD).transpose(1, 0, 2).reshape(P, -1))
    put("sin", sin2.reshape(TT, P, HEAD).transpose(1, 0, 2).reshape(P, -1))
    put("block_eye", np.eye(BASE).reshape(1, -1))
    return a


def kernel(x, norm_gain, w_in, shift_mu, decay_bias, decay_up, iclr_bias, iclr_up,
           k_k, k_a, r_k, gn_gain, gn_bias, w_out, final_gain):
    import concourse.bacc as bacc
    from concourse.bass_utils import run_bass_kernel_spmd as run

    w = np.asarray(w_in)[0].reshape(KC, P, -1).transpose(1, 0, 2)
    wo = np.asarray(w_out)[0].reshape(KC, P, -1).transpose(1, 0, 2)
    W = WIDTH
    start = {"aq": 0, "ak": W, "av": 2 * W, "ga": 3 * W, "r": 4 * W, "k": 5 * W, "v": 6 * W, "gb": 7 * W + P}
    arrays = {"in_" + n: np.ascontiguousarray(w[:, :, s:s + W]) for n, s in start.items()}
    arrays["in_wo"] = np.ascontiguousarray(np.stack([wo[:, :, 0:512], wo[:, :, 512:1024]], 1))
    arrays["in_wd"] = np.ascontiguousarray(w[:, :, 7 * W:7 * W + P]).reshape(P, -1)
    arrays["in_up"] = np.concatenate([np.asarray(decay_up)[0], np.asarray(iclr_up)[0]], 0)
    arrays["in_x"] = np.ascontiguousarray(np.asarray(x)[0])
    arrays["in_const"] = constants()
    by_channel = lambda a: np.asarray(a).reshape(-1, P).T
    mu = np.asarray(shift_mu)[0]
    cols = {"mu_r": mu[0:W], "mu_k": mu[W:2 * W], "mu_v": mu[2 * W:3 * W], "mu_w": mu[3 * W:],
            "decay_bias": decay_bias, "iclr_bias": iclr_bias, "k_k": k_k, "k_a": k_a, "r_k": r_k,
            "gn_gain": gn_gain, "gn_bias": gn_bias, "norm_gain": norm_gain}
    arrays["in_param"] = np.ascontiguousarray(np.concatenate([by_channel(cols[n]) for n in PARAM], 1))
    arrays["in_fg"] = np.ascontiguousarray(np.asarray(final_gain))

    nc = bacc.Bacc("TRN2", target_bir_lowering=False, num_devices=1)
    f32 = mybir.dt.float32
    ap = {n: nc.dram_tensor(n, a.shape, f32, kind="ExternalInput").ap() for n, a in arrays.items()}
    a_scratch = nc.dram_tensor("a_scratch", (P, UNITS, C), f32, kind="Internal").ap()
    t_scratch = nc.dram_tensor("t_scratch", (P, 2, BASE * BASE), f32, kind="Internal").ap()
    out = nc.dram_tensor("out", (SEQ, D_MODEL), f32, kind="ExternalOutput").ap()
    hybrid_layer(nc, ap["in_x"], {n: ap["in_" + n] for n in BLOCKS}, ap["in_up"], ap["in_const"],
                 ap["in_param"], ap["in_fg"], a_scratch, t_scratch, out)
    r = run(nc, [arrays], core_ids=[0])
    return r.results[0]["out"].reshape(1, SEQ, D_MODEL)
```
